# Optimizing a Trainium2 kernel written in Bass

```python
import jax, jax.numpy as jnp
from jax import lax
import numpy as np

D_MODEL = 1024
BATCH = 1
SEQ = 256
DEPTH = 2

CHUNK = 64
Q_BLOCK = 128
D_FF = 2816
EPS = 1e-6

MLA_HEADS = 8
MLA_NOPE = 64
MLA_ROPE = 32
MLA_QK = MLA_NOPE + MLA_ROPE
MLA_V = 64
Q_LORA = 256
KV_LORA = 128
ROPE_BASE = 10000.0

RWKV_HEADS = 8
RWKV_HEAD = 64
RWKV_W = RWKV_HEADS * RWKV_HEAD
DECAY_LORA = 64
A_LORA = 64
GATE_LORA = 160
GN_EPS = 64e-5

MLA_W = MLA_HEADS * MLA_V
MIX_W = MLA_W + RWKV_W
MLA_IN = Q_LORA + KV_LORA + MLA_ROPE
RWKV_SIZES = (RWKV_W, DECAY_LORA, RWKV_W, RWKV_W, A_LORA, GATE_LORA)
RWKV_IN = sum(RWKV_SIZES)
N_IN = MLA_IN + RWKV_IN

kernel_name = 'hybrid_mla_rwkv7_macaron_encoder'

f32 = jnp.float32

def _split(x, sizes):
    idx, acc = [], 0
    for s in sizes[:-1]:
        acc += s
        idx.append(acc)
    return jnp.split(x, idx, axis=-1)

def _rms_norm(x, g):
    xf = x.astype(f32)
    y = xf * lax.rsqrt(jnp.mean(xf * xf, axis=-1, keepdims=True) + EPS)
    return (y * g.astype(f32)).astype(x.dtype)

def _swiglu(h, w_gate, w_up, w_down):
    return (jax.nn.silu(h @ w_gate) * (h @ w_up)) @ w_down

def _rope_tables(seq):
    pos = jnp.arange(seq, dtype=f32)
    inv_freq = ROPE_BASE ** (-jnp.arange(0, MLA_ROPE, 2, dtype=f32) / MLA_ROPE)
    ang = pos[:, None] * inv_freq[None, :]
    return jnp.cos(ang)[None, :, None, :], jnp.sin(ang)[None, :, None, :]

def _rope_tail(x, cos, sin):
    nope, pe = x[..., :MLA_NOPE], x[..., MLA_NOPE:].astype(f32)
    half = MLA_ROPE // 2
    x1, x2 = pe[..., :half], pe[..., half:]
    rot = jnp.concatenate([x1 * cos - x2 * sin, x2 * cos + x1 * sin], axis=-1).astype(x.dtype)
    return jnp.concatenate([nope, rot], axis=-1)

def _chunk_causal_attention(q, k, v):
    B, S, H, Dq = q.shape
    Dv = v.shape[-1]
    nb = S // Q_BLOCK
    scale = MLA_QK ** -0.5
    qt = q.transpose(0, 2, 1, 3).reshape(B, H, nb, Q_BLOCK, Dq).transpose(2, 0, 1, 3, 4)
    kt = k.transpose(0, 2, 1, 3)
    vt = v.transpose(0, 2, 1, 3)
    key_chunk = jnp.arange(S) // CHUNK

    def block(args):
        qb, i = args
        s = jnp.einsum('bhqd,bhkd->bhqk', qb, kt).astype(f32) * scale
        q_chunk = (i * Q_BLOCK + jnp.arange(Q_BLOCK)) // CHUNK
        mask = key_chunk[None, :] <= q_chunk[:, None]
        s = jnp.where(mask[None, None], s, -jnp.inf)
        pr = jax.nn.softmax(s, axis=-1).astype(vt.dtype)
        return jnp.einsum('bhqk,bhkd->bhqd', pr, vt)

    o = lax.map(block, (qt, jnp.arange(nb)))
    return o.transpose(1, 0, 3, 2, 4).reshape(B, S, H * Dv)

def _mla(p, q_lat_norm, w_q_up, kv_lat_norm, w_kv_up, q_norm, k_norm, cos, sin):
    B, S, _ = p.shape
    q_lat, kv_lat, k_pe = _split(p, [Q_LORA, KV_LORA, MLA_ROPE])
    q = (_rms_norm(q_lat, q_lat_norm) @ w_q_up).reshape(B, S, MLA_HEADS, MLA_QK)
    kv = (_rms_norm(kv_lat, kv_lat_norm) @ w_kv_up).reshape(B, S, MLA_HEADS, MLA_NOPE + MLA_V)
    k_nope, v = kv[..., :MLA_NOPE], kv[..., MLA_NOPE:]
    k = jnp.concatenate([k_nope, jnp.broadcast_to(k_pe[:, :, None, :], (B, S, MLA_HEADS, MLA_ROPE))], axis=-1)
    q = _rope_tail(_rms_norm(q, q_norm), cos, sin)
    k = _rope_tail(_rms_norm(k, k_norm), cos, sin)
    return _chunk_causal_attention(q, k, v)

def _rwkv7(p, mu, w0, w2, a0, a2, g2, k_k, k_a, r_k, gn_gain, gn_bias):
    B, S, _ = p.shape
    prev = jnp.pad(p[:, :-1], ((0, 0), (1, 0), (0, 0)))
    p = p + mu * (prev - p)
    r, w_l, k, v, a_l, g_l = _split(p, list(RWKV_SIZES))
    w = -jax.nn.softplus(-(w0 + jnp.tanh(w_l) @ w2).astype(f32)) - 0.5
    decay = jnp.exp(-jnp.exp(w))
    a = jax.nn.sigmoid((a0 + a_l @ a2).astype(f32))
    g = jax.nn.sigmoid(g_l) @ g2

    def heads(t):
        return t.astype(f32).reshape(B, S, RWKV_HEADS, RWKV_HEAD)

    r, k, v, a, decay = heads(r), heads(k), heads(v), heads(a), heads(decay)
    kk = k * k_k.astype(f32).reshape(RWKV_HEADS, RWKV_HEAD)
    kk = kk / jnp.maximum(jnp.sqrt(jnp.sum(kk * kk, axis=-1, keepdims=True)), 1e-12)
    k = k * (1.0 + (a - 1.0) * k_a.astype(f32).reshape(RWKV_HEADS, RWKV_HEAD))
    xs = tuple(jnp.moveaxis(t, 1, 0) for t in (r, decay, k, v, -kk, kk * a))

    def step(state, inp):
        r_t, w_t, k_t, v_t, a_t, b_t = inp
        sa = jnp.einsum('bhvk,bhk->bhv', state, a_t)
        state = state * w_t[:, :, None, :] + sa[..., None] * b_t[:, :, None, :] + v_t[..., None] * k_t[:, :, None, :]
        return state, jnp.einsum('bhvk,bhk->bhv', state, r_t)

    state0 = jnp.zeros((B, RWKV_HEADS, RWKV_HEAD, RWKV_HEAD), f32)
    _, y = lax.scan(step, state0, xs)
    y = jnp.moveaxis(y, 0, 1)
    mean = jnp.mean(y, axis=-1, keepdims=True)
    var = jnp.mean((y - mean) ** 2, axis=-1, keepdims=True)
    y = ((y - mean) * lax.rsqrt(var + GN_EPS)).reshape(B, S, RWKV_W)
    y = y * gn_gain.astype(f32) + gn_bias.astype(f32)
    bonus = jnp.sum(r * k * r_k.astype(f32), axis=-1, keepdims=True) * v
    y = (y + bonus.reshape(B, S, RWKV_W)) * g.astype(f32)
    return y.astype(p.dtype)

def setup_inputs(seed: int = 0) -> dict:
    key = jax.random.key(seed)
    ks = jax.random.split(key, 40)
    cnt = [0]
    L = DEPTH

    def nxt():
        kk = ks[cnt[0]]
        cnt[0] += 1
        return kk

    def nrm(shape, scale):
        return jax.random.normal(nxt(), shape, jnp.float32) * scale

    def gain(shape):
        return 1.0 + nrm(shape, 0.05)

    def unif(shape, lo, hi):
        return jax.random.uniform(nxt(), shape, jnp.float32, lo, hi)

    return {
        'x': nrm((BATCH, SEQ, D_MODEL), 1.0),
        'ffn1_norm': gain((L, D_MODEL)),
        'ffn1_w_gate': nrm((L, D_MODEL, D_FF), D_MODEL ** -0.5),
        'ffn1_w_up': nrm((L, D_MODEL, D_FF), D_MODEL ** -0.5),
        'ffn1_w_down': nrm((L, D_FF, D_MODEL), D_FF ** -0.5),
        'mix_norm': gain((L, D_MODEL)),
        'w_in': nrm((L, D_MODEL, N_IN), D_MODEL ** -0.5),
        'q_lat_norm': gain((L, Q_LORA)),
        'w_q_up': nrm((L, Q_LORA, MLA_HEADS * MLA_QK), Q_LORA ** -0.5),
        'kv_lat_norm': gain((L, KV_LORA)),
        'w_kv_up': nrm((L, KV_LORA, MLA_HEADS * (MLA_NOPE + MLA_V)), KV_LORA ** -0.5),
        'q_norm': gain((L, MLA_QK)),
        'k_norm': gain((L, MLA_QK)),
        'shift_mu': unif((L, RWKV_IN), 0.0, 1.0),
        'w0': unif((L, RWKV_W), -4.0, 0.0),
        'w2': nrm((L, DECAY_LORA, RWKV_W), 0.5 * DECAY_LORA ** -0.5),
        'a0': nrm((L, RWKV_W), 0.1),
        'a2': nrm((L, A_LORA, RWKV_W), A_LORA ** -0.5),
        'g2': nrm((L, GATE_LORA, RWKV_W), GATE_LORA ** -0.5),
        'k_k': 0.85 + nrm((L, RWKV_W), 0.05),
        'k_a': gain((L, RWKV_W)),
        'r_k': nrm((L, RWKV_HEADS, RWKV_HEAD), 0.1),
        'gn_gain': gain((L, RWKV_W)),
        'gn_bias': nrm((L, RWKV_W), 0.02),
        'out_norm_mla': gain((L, MLA_W)),
        'out_norm_rwkv': gain((L, RWKV_W)),
        'w_out': nrm((L, MIX_W, D_MODEL), MIX_W ** -0.5),
        'ffn2_norm': gain((L, D_MODEL)),
        'ffn2_w_gate': nrm((L, D_MODEL, D_FF), D_MODEL ** -0.5),
        'ffn2_w_up': nrm((L, D_MODEL, D_FF), D_MODEL ** -0.5),
        'ffn2_w_down': nrm((L, D_FF, D_MODEL), D_FF ** -0.5),
    }

def reference(x, ffn1_norm, ffn1_w_gate, ffn1_w_up, ffn1_w_down, mix_norm, w_in,
              q_lat_norm, w_q_up, kv_lat_norm, w_kv_up, q_norm, k_norm,
              shift_mu, w0, w2, a0, a2, g2, k_k, k_a, r_k, gn_gain, gn_bias,
              out_norm_mla, out_norm_rwkv, w_out,
              ffn2_norm, ffn2_w_gate, ffn2_w_up, ffn2_w_down):
    S = x.shape[1]
    cos, sin = _rope_tables(S)
    for l in range(DEPTH):
        x = x + 0.5 * _swiglu(_rms_norm(x, ffn1_norm[l]), ffn1_w_gate[l], ffn1_w_up[l], ffn1_w_down[l])
        p = _rms_norm(x, mix_norm[l]) @ w_in[l]
        y_mla = _mla(p[..., :MLA_IN], q_lat_norm[l], w_q_up[l], kv_lat_norm[l], w_kv_up[l],
                     q_norm[l], k_norm[l], cos, sin)
        y_rwkv = _rwkv7(p[..., MLA_IN:], shift_mu[l], w0[l], w2[l], a0[l], a2[l], g2[l],
                        k_k[l], k_a[l], r_k[l], gn_gain[l], gn_bias[l])
        y = jnp.concatenate([_rms_norm(y_mla, out_norm_mla[l]), _rms_norm(y_rwkv, out_norm_rwkv[l])], axis=-1)
        x = x + y @ w_out[l]
        x = x + 0.5 * _swiglu(_rms_norm(x, ffn2_norm[l]), ffn2_w_gate[l], ffn2_w_up[l], ffn2_w_down[l])
    return x


_drawn_inputs = setup_inputs


def setup_inputs(seed=0):
    import zlib

    import numpy as np

    out = dict(_drawn_inputs(seed))
    spreads = {}
    factors = {'k_k': 2.86, 'gn_bias': 3.239, 'ffn2_norm': 2.701}
    for name, (base, spread) in spreads.items():
        noise = np.random.default_rng([zlib.crc32(name.encode()), seed]).standard_normal(out[name].shape)
        drawn = base * np.exp(spread * noise) if base else spread * noise
        out[name] = __import__('jax').numpy.asarray(drawn.astype(out[name].dtype))
    for name, factor in factors.items():
        out[name] = (out[name] * factor).astype(out[name].dtype)
    return out
```

```python
from contextlib import ExitStack

import numpy as np

import concourse.bass as bass
from concourse import mybir

F32 = mybir.dt.float32
F32R = mybir.dt.float32r
BF16 = mybir.dt.bfloat16
I32 = mybir.dt.int32
ALU = mybir.AluOpType
ACT = mybir.ActivationFunctionType
AX_X = mybir.AxisListType.X

P = 128
SEQ, D, DEPTH, F = 256, 1024, 2, 2816
DT, FT = D // P, F // P
H, NOPE, ROPE, DV = 8, 64, 32, 64
QK = NOPE + ROPE
QL, KVL = 256, 128
RW, HEAD, C = 512, 64, 64
NC = SEQ // C
HP = RW // P
G = NC * HP
MLA_IN = QL + KVL + ROPE
O_R = MLA_IN
O_WL = O_R + RW
O_K = O_WL + 64
O_V = O_K + RW
O_AL = O_V + RW
O_GL = O_AL + 64
GLORA = 160
EPS, GN_EPS = 1e-6, 64e-5
DECAY = float(np.exp(-0.5))
SCALE = float(QK) ** -0.5
LEVELS = 5
NEG = -1e30

ROWS = [("ffn1_norm", "ffn1_norm", 0, 8), ("mix_norm", "mix_norm", 0, 8), ("ffn2_norm", "ffn2_norm", 0, 8),
        ("q_lat_norm", "q_lat_norm", 0, 2), ("kv_lat_norm", "kv_lat_norm", 0, 1),
        ("mu_r", "shift_mu", 0, 4), ("mu_k", "shift_mu", O_K - MLA_IN, 4), ("mu_v", "shift_mu", O_V - MLA_IN, 4),
        ("mu_g", "shift_mu", O_GL - MLA_IN, 1), ("mu_g2", "shift_mu", O_GL - MLA_IN + 32, 1),
        ("mu_wa", None, 0, 1),
        ("w0", "w0", 0, 4), ("a0", "a0", 0, 4), ("k_k", "k_k", 0, 4), ("k_a", "k_a", 0, 4), ("r_k", "r_k", 0, 4),
        ("gn_gain", "gn_gain", 0, 4), ("gn_bias", "gn_bias", 0, 4),
        ("out_norm_mla", "out_norm_mla", 0, 4), ("out_norm_rwkv", "out_norm_rwkv", 0, 4)]
ROW = {}
_n = 0
for _name, _, _, _k in ROWS:
    ROW[_name] = _n
    _n += _k
NROWS = _n
MU_N = ROW["mu_wa"] + 1 - ROW["mu_r"]

CONST = {}
_n = 0
for _name, _k in [("ident", 128), ("ones", 128), ("onesbd", 128), ("meanbd", 128), ("eyes", 64), ("upper", 128),
                  ("level", LEVELS * 64), ("level1T", 64), ("reset", 256), ("cos", 32), ("sin", 32)]:
    CONST[_name] = (_n, _n + _k)
    _n += _k
NCONST = _n


def shape_constants():
    c = np.zeros((P, NCONST), np.float32)

    def put(name, a):
        lo, hi = CONST[name]
        c[:, lo:hi] = np.asarray(a, np.float32).reshape(P, hi - lo)

    i = np.arange(P)
    row, col = (i % C)[:, None], np.arange(C)[None, :]
    same = (i[:, None] // C) == (i[None, :] // C)
    put("ident", np.eye(P))
    put("ones", np.ones((P, P)))
    put("onesbd", same)
    put("meanbd", same / HEAD)
    put("eyes", row == col)
    put("upper", np.concatenate([row < col, row <= col], 1))
    lev = []
    for k in range(1, LEVELS + 1):
        s = 1 << k
        lev.append((row // (2 * s) == col // (2 * s)) & (row // s > col // s))
    put("level", np.concatenate(lev, 1))
    put("level1T", (row // 2 == col // 2) & (row < col))
    put("reset", np.broadcast_to((np.arange(SEQ) % C != 0)[None], (P, SEQ)))
    inv = np.float32(10000.0) ** (-np.arange(0, ROPE, 2, dtype=np.float32) / np.float32(ROPE))
    ang = np.arange(SEQ, dtype=np.float32)[:, None] * inv[None, :].astype(np.float32)
    put("cos", np.cos(ang).reshape(2, P, 16).transpose(1, 0, 2))
    put("sin", np.sin(ang).reshape(2, P, 16).transpose(1, 0, 2))
    return c


class Steps:

    def __init__(self, sem, names):
        self.sem, self.names, self.n = sem, names, 0
        assert len(set(names)) == len(names)

    def at(self, rnd, name):
        return rnd * len(self.names) + (self.names.index(name) + 1)

    def done(self, ins, name):
        assert self.names[self.n % len(self.names)] == name, (name, self.names[self.n % len(self.names)])
        self.n += 1
        ins.then_inc(self.sem, 1)


RW_TILES = ["wa"] + [f"r{i}" for i in range(4)] + [f"k{i}" for i in range(4)] + [f"v{i}" for i in range(4)] + ["g0", "g1"]
LAT_TILES = ["q0", "q1", "kv"]
MIX_BLOCKS = RW_TILES + LAT_TILES + ["pe", "kvup", "qup0", "qup1"] + [f"out{i}" for i in range(8)]
FFN_BLOCKS = 3 * FT
LAYER_BLOCKS = 2 * FFN_BLOCKS + len(MIX_BLOCKS)
RING = 3
assert FFN_BLOCKS % RING == 0 and len(MIX_BLOCKS) % RING == 0


class Block:

    def __init__(self, number, fills, slot):
        self.number, self.fills, self.slot = number, fills, slot


def ffn_block(l, which, kind, f):
    first = (FFN_BLOCKS + len(MIX_BLOCKS)) * which
    base, rounds = l * LAYER_BLOCKS + first, l * (LAYER_BLOCKS // RING) + first // RING
    if kind == "gate":
        return Block(base, rounds + 1, 0) if isinstance(f, int) and f == 0 else Block(base + (f * 3 - 1), rounds + f, 2)
    if kind == "up":
        return Block(base + 1, rounds + 1, 1) if isinstance(f, int) and f == 0 else Block(base + f * 3, rounds + (f + 1), 0)
    if isinstance(f, int) and f == FT - 1:
        return Block(base + (FFN_BLOCKS - 1), rounds + FT, 2)
    return Block(base + (f * 3 + 4), rounds + (f + 2), 1)


def mix_block(l, name):
    j = MIX_BLOCKS.index(name)
    return Block(l * LAYER_BLOCKS + (FFN_BLOCKS + j), l * (LAYER_BLOCKS // RING) + (FFN_BLOCKS // RING + j // RING + 1), j % RING)


def block_width(name):
    return DT * ROPE if name == "pe" else 768 if name[:3] == "qup" else 1024


def ffn_order(eng, gate, up, down):
    gate(0, 0), up(0, 0), gate(1, 1), up(1, 1), down(0, 0)
    with eng.Fori(0, FT // 2 - 1) as i:
        f = i * 2
        gate(f + 2, 0), up(f + 2, 0), down(f + 1, 1)
        gate(f + 3, 1), up(f + 3, 1), down(f + 2, 0)
    down(FT - 1, (FT - 1) % 2)


LO, UP = slice(0, 64), slice(64, 128)

def newton(prefix):
    return [f"{prefix}_{s}" for s in ("shift", "seed") + tuple(f"{x}{i}" for i in range(3) for x in ("sq", "err", "y"))]


NORM_V = ["ms"] + newton("norm") + [f"xn{i}" for i in range(4)] + [f"xlo{i}" for i in range(4)]
NORM_A = [f"sq{i}" for i in range(4)] + [f"xhi{i}" for i in range(4)]
LV = range(1, LEVELS + 1)

MIX_V = (["prm", "omm", "half_wa", "half_k", "one_k"] + NORM_V
         + [f"sh_{t}" for t in RW_TILES[:5]] + [f"sh_{t}" for t in RW_TILES[5:9]] + ["kk0", "lw", "lc"]
         + [f"sh_{t}" for t in RW_TILES[9:]] + ["gs", "kkms"] + newton("kk") + ["kkw"] + ["kk"]
         + ["kf", "kmod", "a_c", "r_c", "k_c", "kk2", "b_c", "rk", "bonus"]
         + ["lat_ms"] + newton("lat") + ["lat_n", "lat_lo"]
         + [f"kn{j}" for j in range(4)] + ["kpe"] + [f"qe{j}" for j in range(4)]
         + ["qkss", "qkms"] + newton("qk") + ["qkn", "qkg", "rope_m", "rope"]
         + [f"qkT{i}" for i in range(8)]
         + ["mask0", "max0", "nmax0", "mask1", "max1", "nmax1", "pt0", "pt1"]
         + ["rinv", "o", "yms"] + newton("ym") + ["yn", "yg", "ylo0"]
         + [f"g1_{c}" for c in range(NC)] + [f"g2_{c}" for c in range(NC)] + ["p1a", "p1"]
         + [f"tb{c}" for c in range(NC)] + [f"vc{c}" for c in range(NC)]
         + ["t0_0", "t0_1"]
         + [s for k in LV for s in [f"um{k}_0", f"um{k}_1"]
            + ([f"tc{k}_0", f"pc{k}_0", f"tc{k}_1", f"pc{k}_1"] if k < LEVELS else [])]
         + [s for c in range(NC) for s in ([f"x{c}", f"u{c}"] + ([f"sa{c}"] if 0 < c < NC - 1 else [])
                                           + ([f"s{c}"] if c < NC - 1 else []))]
         + ["y", "yc", "gv"] + newton("gv") + ["gvw"] + ["gy", "gg", "gb", "gm", "rms"] + newton("rms") + ["rg", "ylo1"]
         + [f"res{i}" for i in range(7)])
MIX_A = (NORM_A + [f"mu_{t}" for t in RW_TILES[:5]] + ["tanh_w"] + [f"mu_{t}" for t in RW_TILES[5:9]]
         + ["tz", "ta", "kksq"] + [f"mu_{t}" for t in RW_TILES[9:]] + ["gs0", "E", "einv", "gT"]
         + ["lat_copy", "pe", "lat_sq", "lat_hi"] + [f"v{j}" for j in range(4)] + ["qksq"]
         + ["aP", "bP", "kP", "vP", "ex0", "ex1", "ysq", "yhi0"]
         + [f"tk{c}" for c in range(NC)] + [f"tv{c}" for c in range(NC)] + ["lP", "pP"]
         + [f"{s}{k}_{b}" for k in LV for s in ("us", "ps") for b in range(2)]
         + ["ak"] + [s for c in range(NC) for s in ([f"ub{c}"] + ([f"sb{c}"] if c < NC - 1 else []))]
         + ["gsq", "rsq", "yhi1"])
MIX_P = (["prm", "ss", "rb"] + RW_TILES[:9] + ["z", "a"] + RW_TILES[9:] + ["kkss"] + LAT_TILES + ["pe", "kkb", "gup", "bsum", "latss", "latb"]
         + ["kvup", "qup0", "qup1"] + [f"qkT{i}" for i in range(8)]
         + ["sc0", "sc1", "pt0", "pv0", "pt1", "pv1", "yT"]
         + [f"g1_{c}" for c in range(NC)] + [f"g2_{c}" for c in range(NC)]
         + [f"tb{c}" for c in range(NC)] + [f"tk{c}" for c in range(NC)] + [f"tv{c}" for c in range(NC)] + ["ti0", "ti1"]
         + [s for k in LV for s in [f"u{k}_0", f"u{k}_1"] + [x for b in range(2) for x in
                                                           ([f"t{k}_{b}"] if k < LEVELS else []) + [f"p{k}_{b}"]]]
         + [s for c in range(NC) for s in [f"x{c}", f"u{c}"] + ([f"s{c}"] if c < NC - 1 else []) + [f"y{c}"]]
         + ["mean", "var", "gvb", "rms", "rmsb"] + [f"out{i}" for i in range(8)])


def mu_col(tile):
    return {"wa": ("mu_wa", 0), "g0": ("mu_g", 0), "g1": ("mu_g2", 0)}.get(tile) or (f"mu_{tile[0]}", int(tile[1]))



def build(nc, x, par, w, consts, out):
    with ExitStack() as ctx:
        def sb(name, shape, dt=F32):
            return ctx.enter_context(nc.sbuf_tensor(name, shape, dt))

        def sem(name):
            return ctx.enter_context(nc.semaphore(name))

        bank = [ctx.enter_context(nc.psum_tensor(f"bank{i}", [P, 512], F32)) for i in range(8)]

        cst = sb("cst", [P, NCONST])
        rows = sb("rows", [NROWS, P])
        prm = sb("prm", [P, NROWS])
        omm = sb("omm", [P, MU_N])
        half = sb("half", [P, 16])
        qkgain = sb("qkgain", [P, 2, QK])
        xT = sb("xT", [P, DT, SEQ])
        xhi = sb("xhi", [P, DT, SEQ], F32R)
        xlo = sb("xlo", [P, DT, SEQ], F32R)
        raw = sb("raw", [P, RING, 1024])
        whi = sb("whi", [P, RING, 1024], F32R)
        wlo = sb("wlo", [P, RING, 1024], F32R)
        hhi = sb("hhi", [P, 2, SEQ], F32R)
        hlo = sb("hlo", [P, 2, SEQ], F32R)
        root = sb("root", [P, 3, 32])
        zeros = sb("zeros", [1, 512], BF16)
        E = sb("E", [P, G, C + 1])
        stat = sb("stat", [P, 256])
        shift = sb("shift", [P, 2, SEQ + 1])
        lora = sb("lora", [P, 3, SEQ])
        kpe = sb("kpe", [P, 2, ROPE])
        work = sb("work", [P, 16, 1024])
        pairs = sb("pairs", [P, 7, G, P])

        def unit(i, n=1):
            return work[:, i:i + n, :].rearrange("p u n -> p (u n)")

        def stacks(i):
            return unit(i).rearrange("p (g i) -> p g i", g=G)

        def double(i):
            return unit(i, 2).rearrange("p (g s i) -> p g s i", g=G, s=2)

        rT, kT, vT, zl, ta, lc, kk, sc, einv, kmod, gT, bonus = (unit(i) for i in range(12))
        w2a2 = unit(10)[:, 0:RW]
        g2a, g2b = unit(11)[:, 0:RW], unit(11)[:, RW:2 * RW]
        AR = double(12)
        bC, kC = stacks(14), stacks(15)
        M1, M2 = double(0), double(3)
        vC, tC, pC, uC = stacks(5), stacks(6), stacks(7), stacks(8)
        yT, yN, ysc, scrap = unit(9), unit(6), unit(8), unit(7)
        rec = unit(6).rearrange("p (s h i) -> p s h i", s=4, h=HP)
        aP, bP, kP, vP, lP, pP, uP = (pairs[:, i] for i in range(7))
        lat = unit(6)[:, 0:768].rearrange("p (t n) -> p t n", t=3)
        lat_sq = unit(9)[:, 0:768].rearrange("p (t n) -> p t n", t=3)
        qk = unit(3, 3).rearrange("p (t s h d) -> p t s h d", t=2, s=2, h=H)
        qk_sq = unit(7, 3)
        rope = unit(7, 2).rearrange("p (s t g n) -> p s t g n", s=4, t=2, g=2 * H)
        qkT = unit(6, 4).rearrange("p (s h n) -> p s h n", s=2, h=H)
        V = unit(1).rearrange("p (t h d) -> p t h d", t=2, h=H)
        prob = unit(3, 3)[:, 0:1536].rearrange("p (h k) -> p h k", h=4)
        probT = unit(3, 3)[:, 1536:3072].rearrange("p (m n) -> p m n", m=3)
        ymla = unit(0).rearrange("p (t n) -> p t n", t=2)
        ymT = unit(6).rearrange("p (f n) -> p f n", f=4)
        xn = unit(0, 2).rearrange("p (t n) -> p t n", t=DT)
        xsq = unit(3, 2).rearrange("p (t n) -> p t n", t=DT)
        ft = unit(5).rearrange("p (s n) -> p s n", n=SEQ)
        xtok = unit(0, 2).rearrange("p (b n) -> p b n", b=2)

        def con(name):
            lo, hi = CONST[name]
            return cst[:, lo:hi]

        ident = con("ident")

        def col(name, i=0):
            return prm[:, ROW[name] + i:ROW[name] + i + 1]

        const_in, x_in, rows_in, small_in, half_in = (sem(s) for s in
                                                     ("const_in", "x_in", "rows_in", "small_in", "half_in"))
        raw_in = [sem(f"raw_in{i}") for i in range(RING)]
        hi_ready = sem("hi_ready")
        lo_ready = sem("lo_ready")
        w_used = sem("w_used")
        x_ready = sem("x_ready")
        tanh_done, hhi_done, hlo_done = sem("tanh_done"), sem("hhi_done"), sem("hlo_done")
        h_steps = sem("h_steps")
        once = sem("once")
        x_turned, out_turned, out_copied, out_done = (sem(s) for s in ("x_turned", "out_turned", "out_copied", "out_done"))
        fv, fa, fp = Steps(sem("fv"), NORM_V + ["res0", "res1", "res2"]), Steps(sem("fa"), NORM_A), Steps(sem("fp"), ["ss", "rb"])
        mv, ma, mp = Steps(sem("mv"), MIX_V), Steps(sem("ma"), MIX_A), Steps(sem("mp"), MIX_P)
        ONCE = 5

        def after(eng, steps, rnd, name):
            eng.wait_ge(steps.sem, steps.at(rnd, name))

        def tile_done(l, which, kind, f):
            return ffn_block(l, which, kind, f).number + (RING + 1)

        block = ctx.enter_context(nc.Block())

        @block.gpsimd
        def _(pool):
            pool.memset(zeros[:], 0.0).then_inc(once, 1)
            pool.memset(shift[:], 0.0).then_inc(once, 1)
            pool.memset(E[:, :, 0:1], 1.0).then_inc(once, 1)
            pool.memset(stat[:], 0.0).then_inc(once, 1)
            pool.memset(pairs[:].rearrange("p s g n -> p (s g n)"), 0.0).then_inc(once, 1)

        @block.sync
        def _(sp):
            sp.dma_start(cst[:], consts).then_inc(const_in, 16)
            sp.dma_start(xtok, x.rearrange("o (b p) n -> p (o b) n", p=P)).then_inc(x_in, 16)

            def load(b, dst, src):
                sp.wait_ge(lo_ready, b.number + 1)
                sp.dma_start(dst, src).then_inc(raw_in[b.slot], 16)

            def columns(src, l, first, n=P):
                return src[bass.ds(l, 1), :, bass.ds(first, n)].rearrange("a (t p) n -> p (a t) n", p=P)

            def in_slot(b, n=P):
                return raw[:, b.slot, 0:DT * n].rearrange("p (t n) -> p t n", t=DT)

            def ffn_loads(l, which):
                wg, wu, wd = (w[f"ffn{which + 1}_w_{s}"] for s in ("gate", "up", "down"))

                def gate(f, parity):
                    b = ffn_block(l, which, "gate", f)
                    load(b, in_slot(b), columns(wg, l, f * P))

                def up(f, parity):
                    b = ffn_block(l, which, "up", f)
                    load(b, in_slot(b), columns(wu, l, f * P))

                def down(f, parity):
                    b = ffn_block(l, which, "down", f)
                    load(b, raw[:, b.slot, :], wd[bass.ds(l, 1), bass.ds(f * P, P), :].rearrange("a p n -> p (a n)"))

                ffn_order(sp, gate, up, down)

            def flat(name, l, lo=None, hi=None):
                v = w[name][bass.ds(l, 1)] if lo is None else w[name][bass.ds(l, 1), lo:hi]
                return v.rearrange("a p n -> p (a n)")

            with sp.Fori(0, DEPTH) as l:
                for name, src, first, k in ROWS:
                    r0 = ROW[name]
                    if src is None:
                        for j, o in enumerate((O_WL - MLA_IN, O_AL - MLA_IN)):
                            sp.dma_start(rows[r0:r0 + 1, 64 * j:64 * j + 64],
                                         par["shift_mu"][bass.ds(l, 1), o:o + 64]).then_inc(rows_in, 16)
                    else:
                        v = par[src]
                        if len(v.shape) == 3:
                            v = v.rearrange("a h n -> a (h n)")
                        sp.dma_start(rows[r0:r0 + k, :], v[bass.ds(l, 1), first:first + P * k]
                                     .rearrange("a (k n) -> (a k) n", n=P)).then_inc(rows_in, 16)
                ffn_loads(l, 0)
                first_col = {"g0": O_GL, "g1": O_GL + GLORA - P, "q0": 0, "q1": P, "kv": QL}
                for i in range(4):
                    first_col.update({f"r{i}": O_R + P * i, f"k{i}": O_K + P * i, f"v{i}": O_V + P * i})
                for name in MIX_BLOCKS:
                    b = mix_block(l, name)
                    if name == "wa":
                        load(b, in_slot(b)[:, :, 0:64], columns(w["w_in"], l, O_WL, 64))
                        sp.dma_start(in_slot(b)[:, :, 64:128], columns(w["w_in"], l, O_AL, 64)).then_inc(half_in, 16)
                        sp.dma_start(w2a2[LO, :], flat("w2", l)).then_inc(small_in, 16)
                        sp.dma_start(w2a2[UP, :], flat("a2", l)).then_inc(small_in, 16)
                        sp.dma_start(g2a, flat("g2", l, 0, P)).then_inc(small_in, 16)
                        sp.dma_start(g2b[96:128, :], flat("g2", l, P, GLORA)).then_inc(small_in, 16)
                        for i, nm in enumerate(("q_norm", "k_norm")):
                            sp.dma_start(qkgain[:, i, :], par[nm][bass.ds(l, 1), :].to_broadcast((P, QK))).then_inc(small_in, 16)
                    elif name == "q0":
                        load(b, in_slot(b)[:, 4:, :], columns(w["w_in"], l, 0)[:, 4:, :])
                        sp.dma_start(in_slot(b)[:, 0:4, :], columns(w["w_in"], l, 0)[:, 0:4, :]).then_inc(half_in, 16)
                    elif name in first_col:
                        load(b, in_slot(b), columns(w["w_in"], l, first_col[name]))
                    elif name == "pe":
                        load(b, in_slot(b, ROPE), columns(w["w_in"], l, QL + KVL, ROPE))
                    elif name == "kvup":
                        load(b, raw[:, b.slot, :], flat("w_kv_up", l))
                    elif name[:3] == "qup":
                        c0 = 384 * int(name[3])
                        load(b, raw[:, b.slot, 0:768].rearrange("p (t n) -> p t n", t=2),
                             w["w_q_up"][bass.ds(l, 1), :, c0:c0 + 384].rearrange("a (t p) n -> p (a t) n", p=P))
                    else:
                        load(b, in_slot(b), columns(w["w_out"], l, P * int(name[3])))
                ffn_loads(l, 1)
            for t in range(2):
                sp.wait_ge(out_copied, 2 * (t + 1))
                sp.dma_start(out[0, P * t:P * (t + 1), :], xtok[:, t, :]).then_inc(out_done, 16)
            sp.wait_ge(out_done, 32)

        ROWS_IN, SMALL_IN = 16 * (len(ROWS) + 1), 16 * 6

        @block.scalar
        def _(act):
            def split(b, width=1024, halves=None):
                act.wait_ge(raw_in[b.slot], b.fills * 16)
                if halves is not None:
                    act.wait_ge(half_in, halves * 16)
                act.wait_ge(w_used, b.number + 1)
                nc.scalar.activation(whi[:, b.slot, 0:width], raw[:, b.slot, 0:width], ACT.Copy).then_inc(hi_ready, 1)

            def norm(st, stv, rnd):
                for i in range(4):
                    st.done(nc.scalar.activation(xsq[:, 2 * i:2 * i + 2, :], xT[:, 2 * i:2 * i + 2, :], ACT.Square), f"sq{i}")
                for i in range(4):
                    after(act, stv, rnd, f"xn{i}")
                    st.done(nc.scalar.activation(xhi[:, 2 * i:2 * i + 2, :], xn[:, 2 * i:2 * i + 2, :], ACT.Copy), f"xhi{i}")

            def ffn(l, which):
                rnd = l * 2 + which
                split(ffn_block(l, which, "gate", 0))
                split(ffn_block(l, which, "up", 0))
                act.wait_ge(x_ready, l * 3 + (4 + 2 * which))
                norm(fa, fv, rnd)

                def gate(f, parity):
                    if not (isinstance(f, int) and f == 0):
                        split(ffn_block(l, which, "gate", f))

                def up(f, parity):
                    if not (isinstance(f, int) and f == 0):
                        split(ffn_block(l, which, "up", f))

                def down(f, parity):
                    tile = rnd * FT + f
                    act.wait_ge(w_used, tile_done(l, which, "gate", f))
                    nc.scalar.activation(ft[:, parity, :], bank[4 + parity][:, 0:SEQ], ACT.Tanh, scale=0.5).then_inc(tanh_done, 1)
                    split(ffn_block(l, which, "down", f))
                    act.wait_ge(h_steps, tile * 2 + 6)
                    act.wait_ge(w_used, ffn_block(l, which, "up", 0).number + (f * 3 + 1))
                    nc.scalar.activation(hhi[:, parity, :], ft[:, 2 + parity, :], ACT.Copy).then_inc(hhi_done, 1)

                ffn_order(act, gate, up, down)

            def spread(dst, src, g0=0, n=G):
                nc.scalar.activation(dst[LO, g0:g0 + n, 0:64], src[LO], ACT.Copy)
                return nc.scalar.activation(dst[UP, g0:g0 + n, 64:128], src[UP], ACT.Copy)

            def mixing(l):
                def need(name, st=mp):
                    after(act, st, l, name)

                def ahead(i):
                    if i < len(MIX_BLOCKS):
                        split(mix_block(l, MIX_BLOCKS[i]), block_width(MIX_BLOCKS[i]), {0: l * 2 + 1, Q0: l * 2 + 2}.get(i))

                Q0 = MIX_BLOCKS.index("q0")
                ahead(0), ahead(1)
                act.wait_ge(x_ready, l * 3 + 5)
                norm(ma, mv, l)
                for i, t in enumerate(RW_TILES):
                    ahead(i + 2)
                    need(t)
                    if i >= 2:
                        need(f"sh_{RW_TILES[i - 2]}", mv)
                    ma.done(nc.scalar.activation(shift[:, i % 2, 1:SEQ + 1], bank[i % 4][:, 0:SEQ], ACT.Copy,
                                                 scale=col(*mu_col(t))), f"mu_{t}")
                    if t == "r3":
                        need("sh_wa", mv)
                        ma.done(nc.scalar.activation(lora[LO, 0, :], lora[LO, 0, :], ACT.Tanh), "tanh_w")
                    if t == "k3":
                        need("z")
                        for j in range(4):
                            ins = nc.scalar.activation(zl[:, SEQ * j:SEQ * (j + 1)], bank[4 + j // 2][:, SEQ * (j % 2):SEQ * (j % 2 + 1)],
                                                       ACT.Tanh, bias=half[:, j:j + 1], scale=0.5)
                        ma.done(ins, "tz")
                        need("a")
                        for j in range(4):
                            ins = nc.scalar.activation(ta[:, SEQ * j:SEQ * (j + 1)], bank[6 + j // 2][:, SEQ * (j % 2):SEQ * (j % 2 + 1)],
                                                       ACT.Tanh, bias=half[:, 4 + j:5 + j], scale=0.5)
                        ma.done(ins, "ta")
                        need("kk0", mv)
                        ma.done(nc.scalar.activation(sc, kk, ACT.Square), "kksq")
                need("sh_g1", mv)
                ma.done(nc.scalar.activation(lora[:, 1:3, :], lora[:, 1:3, :], ACT.Tanh, scale=0.5), "gs0")
                ahead(len(RW_TILES) + 2)
                need("lc", mv)
                lc_g = lc.rearrange("p (g i) -> p g i", g=G)
                ma.done(nc.scalar.activation(E[:, :, 1:C + 1], lc_g, ACT.Exp), "E")
                ma.done(nc.scalar.activation(einv, lc, ACT.Exp, scale=-1.0), "einv")
                ahead(len(RW_TILES) + 3)
                need("gup")
                for j in range(2):
                    ins = nc.scalar.activation(gT[:, 512 * j:512 * (j + 1)], bank[4 + j][:], ACT.Copy)
                ma.done(ins, "gT")
                need("b_c", mv)
                for j in range(3):
                    ins = nc.scalar.activation(lat[:, j, :], bank[(len(RW_TILES) + j) % 4][:, 0:SEQ], ACT.Copy)
                ma.done(ins, "lat_copy")
                need("pe")
                ma.done(nc.scalar.activation(kpe[:], bank[2][:, 0:64].rearrange("p (t n) -> p t n", t=2), ACT.Copy), "pe")
                need("rk", mv)
                need("lat_copy", ma)
                ma.done(nc.scalar.activation(lat_sq, lat, ACT.Square), "lat_sq")
                ahead(len(RW_TILES) + 4), ahead(len(RW_TILES) + 5)
                need("lat_n", mv)
                ma.done(nc.scalar.activation(xhi[:, 0:3, :], lat, ACT.Copy), "lat_hi")
                for j in range(4):
                    need(f"kn{j}", mv)
                    t, hf = j // 2, j % 2
                    ma.done(nc.scalar.activation(V[:, t, 4 * hf:4 * hf + 4, :],
                                                 bank[j][:].rearrange("p (h d) -> p h d", h=4)[:, :, NOPE:], ACT.Copy), f"v{j}")
                ahead(len(RW_TILES) + 6)
                need("qe3", mv)
                ma.done(nc.scalar.activation(qk_sq, unit(3, 3), ACT.Square), "qksq")
                ahead(len(RW_TILES) + 7), ahead(len(RW_TILES) + 8)
                ma.done(spread(aP, AR[:, :, 0, :]), "aP")
                ma.done(spread(bP, bC), "bP")
                ma.done(spread(kP, kC), "kP")
                vT_g = vT.rearrange("p (h c i) -> p c h i", h=HP, c=NC)
                for c in range(NC):
                    ins = spread(vP, vT_g[:, c], 4 * c, 4)
                ma.done(ins, "vP")
                for b in range(2):
                    need(f"nmax{b}", mv)
                    if b:
                        need("pt0")
                    for t in range(2):
                        for j in range(4):
                            i = 8 * b + 4 * t + j
                            src = bank[3 * b][:, P * j:P * (j + 1)] if t == 0 else bank[3 * b + 1 + j // 2][:, 256 * (j % 2):256 * (j % 2) + 256]
                            dst = prob[:, j, 0:P] if t == 0 else prob[:, j, P:3 * P]
                            ins = nc.scalar.activation(dst, src, ACT.Exp, bias=stat[:, 96 + i:97 + i], scale=SCALE,
                                                       accum_out=stat[:, 128 + i:129 + i])
                    ma.done(ins, f"ex{b}")
                need("o", mv)
                for t in range(2):
                    ins = nc.scalar.activation(scrap[:, 512 * t:512 * (t + 1)], ymla[:, t, :], ACT.Square, accum_out=stat[:, 160 + t:161 + t])
                ma.done(ins, "ysq")
                need("yg", mv)
                ma.done(nc.scalar.activation(xhi[:, 0:4, :], ymT, ACT.Copy), "yhi0")
                for s, dst in (("tk", kP), ("tv", vP)):
                    for c in range(NC):
                        need(f"{s}{c}")
                        b = bank[4 + c] if s == "tk" else bank[c]
                        ma.done(nc.scalar.activation(dst[:, 4 * c:4 * c + 4, :], b[:].rearrange("p (g n) -> p g n", g=4), ACT.Copy), f"{s}{c}")
                need("g1_3", mv)
                ma.done(spread(lP, M1[:, :, 0, :]), "lP")
                need("p1", mv)
                ma.done(spread(pP, pC), "pP")
                for k in LV:
                    for b in range(2):
                        need(f"um{k}_{b}", mv)
                        ma.done(spread(uP, uC[:, 8 * b:8 * b + 8], 8 * b, 8), f"us{k}_{b}")
                    for b in range(2):
                        if k < LEVELS:
                            need(f"pc{k}_{b}", mv)
                            ma.done(spread(pP, pC[:, 8 * b:8 * b + 8], 8 * b, 8), f"ps{k}_{b}")
                        else:
                            need(f"p{k}_{b}")
                            ma.done(spread(pP, bank[2 + b][:].rearrange("p (g i) -> p g i", g=8), 8 * b, 8), f"ps{k}_{b}")
                ma.done(spread(lP, M2[:, :, 0, :]), "ak")
                for c in range(NC):
                    need(f"u{c}", mv)
                    ma.done(spread(uP, rec[:, 1], 4 * (c % 2), 4), f"ub{c}")
                    if c < NC - 1:
                        need(f"s{c}", mv)
                        ma.done(spread(uP, rec[:, 2 + (c + 1) % 2], 8 + 4 * ((c + 1) % 2), 4), f"sb{c}")
                out0 = MIX_BLOCKS.index("out0")
                assert out0 == len(RW_TILES) + 7
                need("yc", mv)
                ma.done(nc.scalar.activation(ysc, yT, ACT.Square), "gsq")
                need("gm", mv)
                ma.done(nc.scalar.activation(ysc, yN, ACT.Square), "rsq")
                need("rg", mv)
                ma.done(nc.scalar.activation(xhi[:, 4:8, :], yN.rearrange("p (h n) -> p h n", h=HP), ACT.Copy), "yhi1")
                for i in range(out0 + 2, len(MIX_BLOCKS)):
                    ahead(i)

            with act.Fori(0, DEPTH) as l:
                act.wait_ge(once, ONCE)
                ffn(l, 0)
                mixing(l)
                ffn(l, 1)

        @block.vector
        def _(dve):
            V_ = nc.vector
            dve.sem_inc(lo_ready, RING)
            dve.sem_inc(h_steps, 4)

            def split(b, width=1024):
                dve.wait_ge(hi_ready, b.number + 1)
                V_.tensor_tensor(wlo[:, b.slot, 0:width], raw[:, b.slot, 0:width],
                                 whi[:, b.slot, 0:width].bitcast(F32), ALU.subtract).then_inc(lo_ready, 1)

            def rsqrt(st, rnd, prefix, n):
                v, y, t = (root[:, i, 0:n] for i in range(3))

                def did(name, ins):
                    st.done(ins, f"{prefix}_{name}")
                    after(dve, st, rnd, f"{prefix}_{name}")

                did("shift", V_.tensor_scalar(t.bitcast(I32), v.bitcast(I32), 1, None, ALU.logical_shift_right))
                did("seed", V_.tensor_scalar(y.bitcast(I32), t.bitcast(I32), -1.0, float(0x5F3759DF), ALU.mult, ALU.add))
                for i in range(3):
                    did(f"sq{i}", V_.tensor_tensor(t, y, y, ALU.mult))
                    did(f"err{i}", V_.scalar_tensor_tensor(t, t, -0.5, v, ALU.mult, ALU.mult))
                    did(f"y{i}", V_.scalar_tensor_tensor(y, t, 1.5, y, ALU.add, ALU.mult))

            def norm(st, sta, stp, rnd, gain):
                after(dve, stp, rnd, "ss")
                st.done(V_.tensor_scalar(root[:, 0, 0:2], bank[4][:, 0:2], 1.0 / D, EPS, ALU.mult, ALU.add), "ms")
                after(dve, st, rnd, "ms")
                rsqrt(st, rnd, "norm", 2)
                after(dve, stp, rnd, "rb")
                for i in range(4):
                    for t in (2 * i, 2 * i + 1):
                        ins = V_.scalar_tensor_tensor(xn[:, t, :], xT[:, t, :], col(gain, t), bank[5][:, 0:SEQ], ALU.mult, ALU.mult)
                    st.done(ins, f"xn{i}")
                for i in range(4):
                    after(dve, sta, rnd, f"xhi{i}")
                    s = slice(2 * i, 2 * i + 2)
                    st.done(V_.tensor_tensor(xlo[:, s, :], xn[:, s, :], xhi[:, s, :].bitcast(F32), ALU.subtract), f"xlo{i}")

            def ffn(l, which):
                rnd = l * 2 + which
                split(ffn_block(l, which, "gate", 0))
                split(ffn_block(l, which, "up", 0))
                norm(fv, fa, fp, rnd, f"ffn{which + 1}_norm")

                def gate(f, parity):
                    if not (isinstance(f, int) and f == 0):
                        split(ffn_block(l, which, "gate", f))

                def up(f, parity):
                    if not (isinstance(f, int) and f == 0):
                        split(ffn_block(l, which, "up", f))

                def down(f, parity):
                    tile = rnd * FT + f
                    g, u, t, h = bank[4 + parity], bank[6 + parity], ft[:, parity, :], ft[:, 2 + parity, :]
                    dve.wait_ge(tanh_done, tile + 1)
                    dve.wait_ge(w_used, tile_done(l, which, "up", f))
                    V_.scalar_tensor_tensor(h, t, 1.0, u[:, 0:SEQ], ALU.add, ALU.mult).then_inc(h_steps, 1)
                    dve.wait_ge(h_steps, tile * 2 + 5)
                    V_.tensor_tensor(h, h, g[:, 0:SEQ], ALU.mult).then_inc(h_steps, 1)
                    split(ffn_block(l, which, "down", f))
                    dve.wait_ge(hhi_done, tile + 1)
                    V_.tensor_tensor(hlo[:, parity, :], h, hhi[:, parity, :].bitcast(F32), ALU.subtract).then_inc(hlo_done, 1)

                ffn_order(dve, gate, up, down)
                dve.wait_ge(w_used, tile_done(l, which, "down", FT - 1))
                for i in range(4):
                    xs = xT[:, 2 * i:2 * i + 2, :].rearrange("p t n -> p (t n)")
                    ins = V_.scalar_tensor_tensor(xs, bank[i][:], 0.25, xs, ALU.mult, ALU.add)
                    if i < 3:
                        fv.done(ins, f"res{i}")
                    else:
                        ins.then_inc(x_ready, 1)

            def mixing(l):
                def need(name, st=mv):
                    after(dve, st, l, name)

                def step(name, ins):
                    mv.done(ins, name)

                def ahead(i):
                    if i < len(MIX_BLOCKS):
                        split(mix_block(l, MIX_BLOCKS[i]), block_width(MIX_BLOCKS[i]))

                def tiles(v, j):
                    return v[:, SEQ * j:SEQ * (j + 1)]

                def chunked(v):
                    return v.rearrange("p (h c i) -> p c h i", h=HP, c=NC)

                def grouped(v):
                    return v.rearrange("p (c h) i -> p c h i", h=HP)

                ahead(0), ahead(1)
                norm(mv, ma, mp, l, "mix_norm")
                dest = {"wa": lora[:, 0, :], "g0": lora[:, 1, :], "g1": lora[:, 2, :]}
                for j in range(4):
                    dest.update({f"r{j}": tiles(rT, j), f"k{j}": tiles(kT, j), f"v{j}": tiles(vT, j)})
                for i, t in enumerate(RW_TILES):
                    ahead(i + 2)
                    need(f"mu_{t}", ma)
                    m = ROW[mu_col(t)[0]] + mu_col(t)[1] - ROW["mu_r"]
                    step(f"sh_{t}", V_.scalar_tensor_tensor(dest[t], bank[i % 4][:, 0:SEQ], omm[:, m:m + 1],
                                                            shift[:, i % 2, 0:SEQ], ALU.mult, ALU.add))
                    if t == "k3":
                        need("sh_k3")
                        for j in range(4):
                            ins = V_.tensor_scalar(tiles(kk, j), tiles(kT, j), col("k_k", j), None, ALU.mult)
                        step("kk0", ins)
                        need("tz", ma)
                        step("lw", V_.tensor_scalar(zl, zl, -DECAY / 2, -DECAY / 2, ALU.mult, ALU.add))
                        need("lw")
                        for j in range(4):
                            ins = V_.tensor_tensor_scan(tiles(lc, j), con("reset"), tiles(zl, j), 0.0, ALU.mult, ALU.add)
                        step("lc", ins)
                ahead(len(RW_TILES) + 2)
                need("gs0", ma)
                step("gs", V_.tensor_scalar(lora[:, 1:3, :], lora[:, 1:3, :], 0.5, 0.5, ALU.mult, ALU.add))
                ahead(len(RW_TILES) + 3)
                need("kkss", mp)
                step("kkms", V_.tensor_scalar(root[:, 0, 0:16], bank[4][:, 0:16], 1e-24, None, ALU.max))
                need("kkms")
                rsqrt(mv, l, "kk", 16)
                step("kkw", V_.tensor_copy(sc.rearrange("p (g i) -> p g i", g=16), root[:, 1, 0:16].unsqueeze(2).to_broadcast((P, 16, 64))))
                need("kkb", mp)
                for b in range(2):
                    s = slice(512 * b, 512 * (b + 1))
                    ins = V_.tensor_tensor(kk[:, s], kk[:, s], bank[6 + b][:], ALU.mult)
                step("kk", ins)
                need("ta", ma)
                need("kk")
                for j in range(4):
                    ins = V_.tensor_scalar(tiles(sc, j), tiles(ta, j), half[:, 8 + j:9 + j], half[:, 12 + j:13 + j], ALU.mult, ALU.add)
                step("kf", ins)
                need("kf")
                step("kmod", V_.tensor_tensor(kmod, kT, sc, ALU.mult))
                need("einv", ma)
                E_c = E[:].rearrange("p (h c) i -> p c h i", h=HP)

                def per_chunk(fn):
                    for c in range(NC):
                        ins = fn(c)
                    return ins

                step("a_c", per_chunk(lambda c: V_.scalar_tensor_tensor(
                    grouped(AR[:, :, 0, :])[:, c], chunked(kk)[:, c], -1.0, E_c[:, c, :, 0:C], ALU.mult, ALU.mult)))
                step("r_c", per_chunk(lambda c: V_.tensor_tensor(
                    grouped(AR[:, :, 1, :])[:, c], chunked(rT)[:, c], E_c[:, c, :, 1:C + 1], ALU.mult)))
                need("kmod")
                step("k_c", per_chunk(lambda c: V_.tensor_tensor(grouped(kC)[:, c], chunked(kmod)[:, c], chunked(einv)[:, c], ALU.mult)))
                step("kk2", V_.scalar_tensor_tensor(sc, ta, 1.0, kk, ALU.add, ALU.mult))
                need("kk2")
                step("b_c", per_chunk(lambda c: V_.scalar_tensor_tensor(
                    grouped(bC)[:, c], chunked(sc)[:, c], 0.5, chunked(einv)[:, c], ALU.mult, ALU.mult)))
                need("b_c")
                for j in range(4):
                    ins = V_.scalar_tensor_tensor(tiles(sc, j), tiles(rT, j), col("r_k", j), tiles(kmod, j), ALU.mult, ALU.mult)
                step("rk", ins)
                need("bsum", mp)
                for b in range(2):
                    s = slice(512 * b, 512 * (b + 1))
                    ins = V_.tensor_tensor(bonus[:, s], bank[6 + b][:], vT[:, s], ALU.mult)
                step("bonus", ins)
                need("latss", mp)
                V_.tensor_scalar(root[:, 0, 0:2], bank[6][:, 0:2], 1.0 / QL, EPS, ALU.mult, ALU.add)
                step("lat_ms", V_.tensor_scalar(root[:, 0, 2:4], bank[6][:, 2:4], 1.0 / KVL, EPS, ALU.mult, ALU.add))
                need("lat_ms")
                rsqrt(mv, l, "lat", 4)
                need("latb", mp)
                for j in range(3):
                    g = col("q_lat_norm", j) if j < 2 else col("kv_lat_norm")
                    r = bank[7][:, 0:SEQ] if j < 2 else bank[7][:, SEQ:512]
                    ins = V_.scalar_tensor_tensor(lat[:, j, :], lat[:, j, :], g, r, ALU.mult, ALU.mult)
                step("lat_n", ins)
                ahead(len(RW_TILES) + 4), ahead(len(RW_TILES) + 5)
                need("lat_hi", ma)
                step("lat_lo", V_.tensor_tensor(xlo[:, 0:3, :], lat, xhi[:, 0:3, :].bitcast(F32), ALU.subtract))
                need("kvup", mp)
                for j in range(4):
                    t, hf = j // 2, j % 2
                    step(f"kn{j}", V_.tensor_copy(qk[:, t, 1, 4 * hf:4 * hf + 4, 0:NOPE],
                                                  bank[j][:].rearrange("p (h d) -> p h d", h=4)[:, :, 0:NOPE]))
                ahead(len(RW_TILES) + 6)
                need("pe", ma)
                for t in range(2):
                    ins = V_.tensor_copy(qk[:, t, 1, :, NOPE:QK], kpe[:, t:t + 1, :].to_broadcast((P, H, ROPE)))
                step("kpe", ins)
                for hf in range(2):
                    need(f"qup{hf}", mp)
                    for t in range(2):
                        step(f"qe{2 * hf + t}", V_.tensor_copy(qk[:, t, 0, 4 * hf:4 * hf + 4, :],
                                                               bank[4 + 2 * t + hf][:, 0:384].rearrange("p (h d) -> p h d", h=4)))
                need("qksq", ma)
                step("qkss", V_.tensor_reduce(stat[:, 0:32], qk_sq.rearrange("p (g d) -> p g d", d=QK), AX_X, ALU.add))
                ahead(len(RW_TILES) + 7), ahead(len(RW_TILES) + 8)
                need("qkss")
                step("qkms", V_.tensor_scalar(root[:, 0, :], stat[:, 0:32], 1.0 / QK, EPS, ALU.mult, ALU.add))
                need("qkms")
                rsqrt(mv, l, "qk", 32)
                q3 = unit(3, 3).rearrange("p (g d) -> p g d", d=QK)
                step("qkn", V_.tensor_tensor(q3, q3, root[:, 1, :].unsqueeze(2).to_broadcast((P, 32, QK)), ALU.mult))
                need("qkn")
                for t in range(2):
                    for s in range(2):
                        ins = V_.tensor_tensor(qk[:, t, s], qk[:, t, s], qkgain[:, s:s + 1, :].to_broadcast((P, H, QK)), ALU.mult)
                step("qkg", ins)
                need("qkg")
                for t in range(2):
                    qt = qk[:, t].rearrange("p s h d -> p (s h) d")
                    x1, x2 = qt[:, :, NOPE:NOPE + 16], qt[:, :, NOPE + 16:QK]
                    cos, sin = (con(n)[:, 16 * t:16 * t + 16].unsqueeze(1).to_broadcast((P, 2 * H, 16)) for n in ("cos", "sin"))
                    for s, (a, b) in enumerate(((x1, cos), (x2, sin), (x2, cos), (x1, sin))):
                        ins = V_.tensor_tensor(rope[:, s, t], a, b, ALU.mult)
                step("rope_m", ins)
                need("rope_m")
                for t in range(2):
                    qt = qk[:, t].rearrange("p s h d -> p (s h) d")
                    V_.tensor_tensor(qt[:, :, NOPE:NOPE + 16], rope[:, 0, t], rope[:, 1, t], ALU.subtract)
                    ins = V_.tensor_tensor(qt[:, :, NOPE + 16:QK], rope[:, 2, t], rope[:, 3, t], ALU.add)
                step("rope", ins)
                for i in range(8):
                    s, t, hq = i // 4, (i // 2) % 2, i % 2
                    need(f"qkT{i}", mp)
                    step(f"qkT{i}", V_.tensor_copy(qkT[0:QK, s, 4 * hq:4 * hq + 4, P * t:P * (t + 1)],
                                                   bank[i][0:QK, :].rearrange("p (h n) -> p h n", h=4)))
                for b in range(2):
                    need(f"sc{b}", mp)
                    V_.memset(bank[3 * b][LO, :].rearrange("p (h k) -> p h k", h=4)[:, :, 64:128], NEG)
                    for j in range(2):
                        ins = V_.memset(bank[3 * b + 1 + j][LO, :].rearrange("p (h k) -> p h k", h=2)[:, :, 192:256], NEG)
                    step(f"mask{b}", ins)
                    need(f"mask{b}")
                    m0 = 64 + 8 * b
                    V_.tensor_reduce(stat[:, m0:m0 + 4], bank[3 * b][:].rearrange("p (h k) -> p h k", h=4), AX_X, ALU.max)
                    for j in range(2):
                        ins = V_.tensor_reduce(stat[:, m0 + 4 + 2 * j:m0 + 6 + 2 * j],
                                               bank[3 * b + 1 + j][:].rearrange("p (h k) -> p h k", h=2), AX_X, ALU.max)
                    step(f"max{b}", ins)
                    need(f"max{b}")
                    step(f"nmax{b}", V_.tensor_scalar(stat[:, 96 + 8 * b:104 + 8 * b], stat[:, m0:m0 + 8], -SCALE, None, ALU.mult))
                for b in range(2):
                    need(f"pt{b}", mp)
                    if b:
                        need("pv0", mp)
                    for m, bk in enumerate((6, 7, 0)):
                        ins = V_.tensor_copy(probT[:, m, :], bank[bk][:])
                    step(f"pt{b}", ins)
                need("ex1", ma)
                step("rinv", V_.reciprocal(stat[:, 144:160], stat[:, 128:144]))
                need("rinv")
                need("pv1", mp)
                rinv = stat[:, 144:160].rearrange("p (b t j) -> p b t j", b=2, t=2)
                for t in range(2):
                    for b in range(2):
                        y = ymla[:, t, 256 * b:256 * b + 256].rearrange("p (j d) -> p j d", j=4)
                        o = bank[1 + t][:, 256 * b:256 * b + 256].rearrange("p (j d) -> p j d", j=4)
                        ins = V_.tensor_tensor(y, o, rinv[:, b, t, :].unsqueeze(2).to_broadcast((P, 4, DV)), ALU.mult)
                step("o", ins)
                need("ysq", ma)
                step("yms", V_.tensor_scalar(root[:, 0, 0:2], stat[:, 160:162], 1.0 / (H * DV), EPS, ALU.mult, ALU.add))
                need("yms")
                rsqrt(mv, l, "ym", 2)
                for t in range(2):
                    ins = V_.tensor_scalar(ymla[:, t, :], ymla[:, t, :], root[:, 1, t:t + 1], None, ALU.mult)
                step("yn", ins)
                need("yT", mp)
                for f in range(4):
                    ins = V_.tensor_scalar(ymT[:, f, :], bank[3 + f // 2][:, 256 * (f % 2):256 * (f % 2) + 256],
                                           col("out_norm_mla", f), None, ALU.mult)
                step("yg", ins)
                need("yhi0", ma)
                step("ylo0", V_.tensor_tensor(xlo[:, 0:4, :], ymT, xhi[:, 0:4, :].bitcast(F32), ALU.subtract))
                upper = con("upper").unsqueeze(1).to_broadcast((P, 4, P))
                for s, M, b0 in (("g1", M1, 0), ("g2", M2, 4)):
                    for c in range(NC):
                        need(f"{s}_{c}", mp)
                        step(f"{s}_{c}", V_.tensor_tensor(M[:, 4 * c:4 * c + 4].rearrange("p g s i -> p g (s i)"),
                                                          bank[b0 + c][:].rearrange("p (g n) -> p g n", g=4), upper, ALU.mult))
                need("g1_3")
                step("p1a", V_.tensor_tensor(pC, M1[:, :, 0, :], con("level1T").unsqueeze(1).to_broadcast((P, G, C)), ALU.mult))
                need("p1a")
                step("p1", V_.tensor_tensor(pC, pC, con("eyes").unsqueeze(1).to_broadcast((P, G, C)), ALU.add))
                for c in range(NC):
                    need(f"tb{c}", mp)
                    step(f"tb{c}", V_.tensor_copy(bP[:, 4 * c:4 * c + 4, :], bank[c][:].rearrange("p (g n) -> p g n", g=4)))
                for c in range(NC):
                    need(f"tv{c}", ma)
                    b = bank[c][:].rearrange("p (g n) -> p g n", g=4)
                    V_.tensor_copy(vC[LO, 4 * c:4 * c + 4, :], b[LO, :, 0:64])
                    step(f"vc{c}", V_.tensor_copy(vC[UP, 4 * c:4 * c + 4, :], b[UP, :, 64:128]))
                def eight(v, b):
                    return v[:, 8 * b:8 * b + 8, :]

                def bank8(i):
                    return bank[i][:].rearrange("p (g i) -> p g i", g=8)

                for b in range(2):
                    need(f"ti{b}", mp)
                    step(f"t0_{b}", V_.tensor_copy(eight(tC, b), bank8(b)))
                for k in LV:
                    lev = con("level")[:, 64 * (k - 1):64 * k].unsqueeze(1).to_broadcast((P, 8, C))
                    for b in range(2):
                        need(f"u{k}_{b}", mp)
                        step(f"um{k}_{b}", V_.tensor_tensor(eight(uC, b), bank8(4 + b), lev, ALU.mult))
                    if k < LEVELS:
                        for b in range(2):
                            need(f"t{k}_{b}", mp)
                            step(f"tc{k}_{b}", V_.tensor_copy(eight(tC, b), bank8(b)))
                            need(f"p{k}_{b}", mp)
                            step(f"pc{k}_{b}", V_.tensor_copy(eight(pC, b), bank8(2 + b)))
                for c in range(NC):
                    need(f"x{c}", mp)
                    step(f"x{c}", V_.tensor_copy(rec[:, 0], bank[4 + c % 2][:, 0:256].rearrange("p (h i) -> p h i", h=HP)))
                    need(f"u{c}", mp)
                    step(f"u{c}", V_.tensor_copy(rec[:, 1], bank[6 + c % 2][:, 0:256].rearrange("p (h i) -> p h i", h=HP)))
                    if c < NC - 1:
                        need(f"s{c}", mp)
                        grown = bank[2 + c % 2][:, 0:256].rearrange("p (h i) -> p h i", h=HP)
                        new = rec[:, 2 + (c + 1) % 2]
                        if c:
                            step(f"sa{c}", V_.tensor_tensor(new, grown, rec[:, 2 + c % 2], ALU.add))
                            need(f"sa{c}")
                            grown = new
                        step(f"s{c}", V_.tensor_tensor(new, grown, E_c[:, c, :, C:C + 1].to_broadcast((P, HP, HEAD)), ALU.mult))
                for b in range(2):
                    need(f"y{2 * b + 1}", mp)
                    ins = V_.tensor_copy(yT[:, 512 * b:512 * (b + 1)], bank[b][:])
                step("y", ins)
                need("y")
                need("mean", mp)
                for b in range(2):
                    s = slice(512 * b, 512 * (b + 1))
                    ins = V_.tensor_tensor(yT[:, s], yT[:, s], bank[4 + b][:], ALU.subtract)
                step("yc", ins)
                need("var", mp)
                step("gv", V_.tensor_scalar(root[:, 0, 0:16], bank[6][:, 0:16], GN_EPS, None, ALU.add))
                need("gv")
                rsqrt(mv, l, "gv", 16)
                step("gvw", V_.tensor_copy(sc.rearrange("p (g i) -> p g i", g=16), root[:, 1, 0:16].unsqueeze(2).to_broadcast((P, 16, 64))))
                need("gvb", mp)
                for b in range(2):
                    s = slice(512 * b, 512 * (b + 1))
                    ins = V_.tensor_tensor(yT[:, s], yT[:, s], bank[4 + b][:], ALU.mult)
                step("gy", ins)
                need("gy")
                y_h = yT.rearrange("p (c h i) -> p h c i", c=NC, h=HP)
                for j in range(HP):
                    ins = V_.tensor_scalar(tiles(yN, j).rearrange("p (c i) -> p c i", c=NC), y_h[:, j],
                                           col("gn_gain", j), col("gn_bias", j), ALU.mult, ALU.add)
                step("gg", ins)
                need("gg")
                step("gb", V_.tensor_tensor(yN, yN, bonus, ALU.add))
                need("gb")
                step("gm", V_.tensor_tensor(yN, yN, gT, ALU.mult))
                need("rms", mp)
                step("rms", V_.tensor_scalar(root[:, 0, 0:2], bank[2][:, 0:2], 1.0 / RW, EPS, ALU.mult, ALU.add))
                need("rms")
                rsqrt(mv, l, "rms", 2)
                need("rmsb", mp)
                for j in range(4):
                    ins = V_.scalar_tensor_tensor(tiles(yN, j), tiles(yN, j), col("out_norm_rwkv", j), bank[3][:, 0:SEQ], ALU.mult, ALU.mult)
                step("rg", ins)
                need("yhi1", ma)
                step("ylo1", V_.tensor_tensor(xlo[:, 4:8, :], yN.rearrange("p (h n) -> p h n", h=HP), xhi[:, 4:8, :].bitcast(F32), ALU.subtract))
                out0 = MIX_BLOCKS.index("out0")
                for i in range(8):
                    ahead(out0 + i + 2)
                    need(f"out{i}", mp)
                    ins = V_.tensor_tensor(xT[:, i, :], xT[:, i, :], bank[i][:, 0:SEQ], ALU.add)
                    if i < 7:
                        step(f"res{i}", ins)
                    else:
                        ins.then_inc(x_ready, 1)

            dve.wait_ge(const_in, 16)
            dve.wait_ge(once, ONCE)
            for i in range(4):
                dve.wait_ge(x_turned, i + 1)
                V_.tensor_copy(xT[:, 2 * i:2 * i + 2, :].rearrange("p t n -> p (t n)"), bank[i][:]).then_inc(x_ready, 1)

            with dve.Fori(0, DEPTH) as l:
                after(dve, mp, l, "prm")
                mv.done(V_.tensor_copy(prm[:], bank[5][:, 0:NROWS]), "prm")
                after(dve, mv, l, "prm")
                m = ROW["mu_r"]
                mv.done(V_.tensor_scalar(omm[:], prm[:, m:m + MU_N], -1.0, 1.0, ALU.mult, ALU.add), "omm")
                mv.done(V_.tensor_scalar(half[:, 0:8], prm[:, ROW["w0"]:ROW["w0"] + 8], 0.5, None, ALU.mult), "half_wa")
                mv.done(V_.tensor_scalar(half[:, 8:12], prm[:, ROW["k_a"]:ROW["k_a"] + 4], 0.5, None, ALU.mult), "half_k")
                mv.done(V_.tensor_scalar(half[:, 12:16], prm[:, ROW["k_a"]:ROW["k_a"] + 4], -0.5, 1.0, ALU.mult, ALU.add), "one_k")
                ffn(l, 0)
                mixing(l)
                ffn(l, 1)
            for i in range(4):
                dve.wait_ge(out_turned, i + 1)
                V_.tensor_copy(unit(0, 2)[:, 512 * i:512 * (i + 1)], bank[i][:]).then_inc(out_copied, 1)

        @block.tensor
        def _(pe):
            mm = nc.tensor.matmul

            def three(out, hi, lo, mhi, mlo, start, stop, **kw):
                mm(out, hi, mhi, start=start, stop=False, **kw)
                mm(out, hi, mlo, start=False, stop=False, **kw)
                return mm(out, lo, mhi, start=False, stop=stop, **kw)

            def turn(out, in_):
                n = in_.shape[0]
                return nc.tensor.transpose(out, in_, ident[0:n, 0:n])

            def squares(sta, rnd):
                for i in range(4):
                    after(pe, sta, rnd, f"sq{i}")
                for n in range(2):
                    for t in range(DT):
                        ins = mm(bank[4][:, n:n + 1], xsq[:, t, P * n:P * (n + 1)], con("ones")[:, 0:1], start=t == 0, stop=t == DT - 1)
                return ins

            def spread_rows(out, i):
                return mm(out, root[:, 1, i:i + 1].to_broadcast((P, P)), ident, start=True, stop=True)

            def spread_heads(b0):
                for j in range(8):
                    ins = mm(bank[b0 + j // 4][:, P * (j % 4):P * (j % 4 + 1)], sc[:, P * j:P * (j + 1)], ident, start=True, stop=True)
                return ins

            def norm_rows(st, stv, rnd):
                after(pe, stv, rnd, "norm_y2")
                for n in range(2):
                    ins = spread_rows(bank[5][:, P * n:P * (n + 1)], n)
                st.done(ins, "rb")

            def split_ready(b):
                pe.wait_ge(lo_ready, b.number + (RING + 1))

            def column_tile(b, out, wait=None):
                for t in range(DT):
                    if wait is not None and t % 2 == 0:
                        wait(t // 2)
                    s = slice(P * t, P * (t + 1))
                    ins = three(out, whi[:, b.slot, s], wlo[:, b.slot, s], xhi[:, t, :], xlo[:, t, :], t == 0, t == DT - 1)
                return ins

            def ffn(l, which):
                rnd = l * 2 + which
                pe.wait_ge(x_ready, l * 3 + (4 + 2 * which))
                fp.done(squares(fa, rnd), "ss")
                norm_rows(fp, fv, rnd)
                for i in range(4):
                    mm(bank[i][:], zeros[0:1, 0:P], zeros[0:1, :], start=True, stop=False, skip_group_check=True)

                def gate(f, parity):
                    first = isinstance(f, int) and f == 0
                    b = ffn_block(l, which, "gate", f)
                    split_ready(b)
                    pe.wait_ge(h_steps, (rnd * FT + f) * 2 + 2)
                    column_tile(b, bank[4 + parity][:, 0:SEQ],
                                (lambda i: after(pe, fv, rnd, f"xlo{i}")) if first else None).then_inc(w_used, 1)

                def up(f, parity):
                    b = ffn_block(l, which, "up", f)
                    split_ready(b)
                    column_tile(b, bank[6 + parity][:, 0:SEQ]).then_inc(w_used, 1)

                def down(f, parity):
                    last = isinstance(f, int) and f == FT - 1
                    b = ffn_block(l, which, "down", f)
                    split_ready(b)
                    pe.wait_ge(hlo_done, (rnd * FT + f) + 1)
                    for t in range(DT):
                        s = slice(P * t, P * (t + 1))
                        ins = three(bank[t // 2][:, SEQ * (t % 2):SEQ * (t % 2 + 1)], whi[:, b.slot, s], wlo[:, b.slot, s],
                                    hhi[:, parity, :], hlo[:, parity, :], False, last, skip_group_check=True)
                    ins.then_inc(w_used, 1)

                ffn_order(pe, gate, up, down)

            def mixing(l):
                def need(name, st=mv):
                    after(pe, st, l, name)

                def blk(name):
                    b = mix_block(l, name)
                    split_ready(b)
                    return b

                pe.wait_ge(x_ready, l * 3 + 5)
                mp.done(squares(ma, l), "ss")
                norm_rows(mp, mv, l)
                tiles = RW_TILES + LAT_TILES
                for i, t in enumerate(tiles):
                    b = blk(t)
                    if i >= 4 and i - 4 < len(RW_TILES):
                        need(f"sh_{tiles[i - 4]}")
                    out = bank[i % 4][:, 0:SEQ]
                    for kt in range(DT):
                        if i == 0 and kt % 2 == 0:
                            need(f"xlo{kt // 2}")
                        s = slice(P * kt, P * (kt + 1))
                        ins = three(out, whi[:, b.slot, s], wlo[:, b.slot, s], xhi[:, kt, :], xlo[:, kt, :], kt == 0, kt == DT - 1)
                    mp.done(ins, t)
                    pe.wait_ge(mp.sem, mp.at(l, t))
                    pe.sem_inc(w_used, 1)
                    if t == "k3":
                        pe.wait_ge(small_in, l * SMALL_IN + SMALL_IN)
                        need("tanh_w", ma)
                        for nm, part, b0 in (("z", LO, 4), ("a", UP, 6)):
                            for j in range(4):
                                ins = mm(bank[b0 + j // 2][:, SEQ * (j % 2):SEQ * (j % 2 + 1)], w2a2[part, P * j:P * (j + 1)],
                                         lora[part, 0, :], start=True, stop=True)
                            mp.done(ins, nm)
                    if t == "g1":
                        need("kksq", ma)
                        heads = con("onesbd")[:, 0:P:64]
                        for j in range(8):
                            ins = mm(bank[4][:, 2 * j:2 * j + 2], sc[:, P * j:P * (j + 1)], heads, start=True, stop=True)
                        mp.done(ins, "kkss")

                def freed(name):
                    pe.wait_ge(mp.sem, mp.at(l, name))
                    pe.sem_inc(w_used, 1)

                b = blk("pe")
                need("sh_g1")
                for t in range(2):
                    for kt in range(DT):
                        s, n = slice(ROPE * kt, ROPE * (kt + 1)), slice(P * t, P * (t + 1))
                        o = bank[2][:, ROPE * t:ROPE * (t + 1)]
                        mm(o, xhi[:, kt, n], whi[:, b.slot, s], start=kt == 0, stop=False)
                        mm(o, xlo[:, kt, n], whi[:, b.slot, s], start=False, stop=False)
                        ins = mm(o, xhi[:, kt, n], wlo[:, b.slot, s], start=False, stop=kt == DT - 1)
                mp.done(ins, "pe")
                freed("pe")
                need("kkw")
                mp.done(spread_heads(6), "kkb")
                need("gs")
                for j in range(4):
                    o = bank[4 + j // 2][:, SEQ * (j % 2):SEQ * (j % 2 + 1)]
                    mm(o, g2a[:, P * j:P * (j + 1)], lora[:, 1, :], start=True, stop=False)
                    ins = mm(o, g2b[96:128, P * j:P * (j + 1)], lora[96:128, 2, :], start=False, stop=True)
                mp.done(ins, "gup")
                need("rk")
                for j in range(2):
                    ins = mm(bank[6 + j][:], con("onesbd"), sc[:, 512 * j:512 * (j + 1)], start=True, stop=True)
                mp.done(ins, "bsum")
                need("lat_sq", ma)
                need("bonus")
                one = con("ones")[:, 0:1]
                for t in range(2):
                    n = slice(P * t, P * (t + 1))
                    mm(bank[6][:, t:t + 1], lat_sq[:, 0, n], one, start=True, stop=False)
                    mm(bank[6][:, t:t + 1], lat_sq[:, 1, n], one, start=False, stop=True)
                    ins = mm(bank[6][:, 2 + t:3 + t], lat_sq[:, 2, n], one, start=True, stop=True)
                mp.done(ins, "latss")
                need("lat_y2")
                for j in range(4):
                    ins = spread_rows(bank[7][:, P * j:P * (j + 1)], j)
                mp.done(ins, "latb")
                b = blk("kvup")
                need("lat_lo")
                need("pe", ma)
                for t in range(2):
                    n = slice(P * t, P * (t + 1))
                    for hf in range(2):
                        o, s = bank[2 * t + hf][:], slice(512 * hf, 512 * (hf + 1))
                        mm(o, xhi[:, 2, n], whi[:, b.slot, s], start=True, stop=False)
                        mm(o, xlo[:, 2, n], whi[:, b.slot, s], start=False, stop=False)
                        ins = mm(o, xhi[:, 2, n], wlo[:, b.slot, s], start=False, stop=True)
                mp.done(ins, "kvup")
                freed("kvup")
                need("gT", ma)
                for hf in range(2):
                    b = blk(f"qup{hf}")
                    for t in range(2):
                        o, n = bank[4 + 2 * t + hf][:, 0:384], slice(P * t, P * (t + 1))
                        for kt in range(2):
                            s = slice(384 * kt, 384 * (kt + 1))
                            mm(o, xhi[:, kt, n], whi[:, b.slot, s], start=kt == 0, stop=False)
                            mm(o, xlo[:, kt, n], whi[:, b.slot, s], start=False, stop=False)
                            ins = mm(o, xhi[:, kt, n], wlo[:, b.slot, s], start=False, stop=kt == 1)
                    mp.done(ins, f"qup{hf}")
                    freed(f"qup{hf}")
                need("rope")
                need("v3", ma)
                for i in range(8):
                    s, t, hq = i // 4, (i // 2) % 2, i % 2
                    for j in range(4):
                        ins = turn(bank[i][0:QK, P * j:P * (j + 1)], qk[:, t, s, 4 * hq + j, :])
                    mp.done(ins, f"qkT{i}")
                need("qkT7")
                for b in range(2):
                    for j in range(4):
                        h = 4 * b + j
                        mm(bank[3 * b][:, P * j:P * (j + 1)], qkT[0:QK, 0, h, 0:P], qkT[0:QK, 1, h, 0:P], start=True, stop=True)
                        ins = mm(bank[3 * b + 1 + j // 2][:, 256 * (j % 2):256 * (j % 2) + 256], qkT[0:QK, 0, h, P:SEQ], qkT[0:QK, 1, h, :],
                                 start=True, stop=True)
                    mp.done(ins, f"sc{b}")
                for b in range(2):
                    need(f"ex{b}", ma)
                    if b:
                        need("pt0")
                    for m, bk in enumerate((6, 7, 0)):
                        for j in range(4):
                            ins = turn(bank[bk][:, P * j:P * (j + 1)], prob[:, j, P * m:P * (m + 1)])
                    mp.done(ins, f"pt{b}")
                    need(f"pt{b}")
                    for j in range(4):
                        h = 4 * b + j
                        s = slice(DV * h, DV * (h + 1))
                        mm(bank[1][:, s], probT[:, 0, P * j:P * (j + 1)], V[:, 0, h, :], start=True, stop=True)
                        mm(bank[2][:, s], probT[:, 1, P * j:P * (j + 1)], V[:, 0, h, :], start=True, stop=False)
                        ins = mm(bank[2][:, s], probT[:, 2, P * j:P * (j + 1)], V[:, 1, h, :], start=False, stop=True)
                    mp.done(ins, f"pv{b}")
                need("yn")
                for f in range(4):
                    for t in range(2):
                        ins = turn(bank[3 + f // 2][:, 256 * (f % 2) + P * t:256 * (f % 2) + P * (t + 1)], ymla[:, t, P * f:P * (f + 1)])
                mp.done(ins, "yT")
                need("vP", ma)
                need("yg")
                for s, lhs, b0 in (("g1", bP, 0), ("g2", kP, 4)):
                    for c in range(NC):
                        for h in range(HP):
                            g = 4 * c + h
                            ins = mm(bank[b0 + c][:, P * h:P * (h + 1)], lhs[:, g, :], AR[:, g].rearrange("p s i -> p (s i)"), start=True, stop=True)
                        mp.done(ins, f"{s}_{c}")
                for s, src, b0, wait in (("tb", bP, 0, "g1_"), ("tk", kP, 4, "g2_"), ("tv", vP, 0, "tb")):
                    for c in range(NC):
                        need(f"{wait}{c}")
                        for h in range(HP):
                            ins = turn(bank[b0 + c][:, P * h:P * (h + 1)], src[:, 4 * c + h, :])
                        mp.done(ins, f"{s}{c}")
                need("pP", ma)
                need("lP", ma)
                need(f"vc{NC - 1}")
                for b in range(2):
                    for j in range(8):
                        mm(bank[b][:, 64 * j:64 * (j + 1)], pP[:, 8 * b + j, :], con("eyes"), start=j == 0, stop=False, skip_group_check=True)
                    ins = mm(bank[2 + b][:], ident, pC[:, 8 * b:8 * b + 8, :].rearrange("p g i -> p (g i)"), start=True, stop=False, skip_group_check=True)
                    mp.done(ins, f"ti{b}")
                for k in LV:
                    for b in range(2):
                        need(f"t0_{b}" if k == 1 else f"tc{k - 1}_{b}")
                        for j in range(8):
                            g = 8 * b + j
                            ins = mm(bank[4 + b][:, 64 * j:64 * (j + 1)], lP[:, g, :], tC[:, g, :], start=True, stop=True)
                        mp.done(ins, f"u{k}_{b}")
                    for b in range(2):
                        last = k == LEVELS
                        if not last:
                            need(f"um{k}_{b}")
                            if k > 1:
                                need(f"ps{k - 1}_{b}", ma)
                            for j in range(8):
                                g = 8 * b + j
                                ins = mm(bank[b][:, 64 * j:64 * (j + 1)], pP[:, g, :], uC[:, g, :], start=False, stop=k == LEVELS - 1, skip_group_check=True)
                            mp.done(ins, f"t{k}_{b}")
                        need(f"us{k}_{b}", ma)
                        if k > 1:
                            need(f"pc{k - 1}_{b}")
                        for j in range(8):
                            g = 8 * b + j
                            ins = mm(bank[2 + b][:, 64 * j:64 * (j + 1)], uP[:, g, :], pC[:, g, :], start=False, stop=last, skip_group_check=True)
                        mp.done(ins, f"p{k}_{b}")
                need("ak", ma)
                for c in range(NC):
                    x_b, u_b, s_b, y_b = bank[4 + c % 2], bank[6 + c % 2], bank[2 + c % 2], bank[c // 2]
                    for h in range(HP):
                        s = slice(64 * h, 64 * (h + 1))
                        ins = mm(x_b[:, s], lP[:, 4 * c + h, :], vC[:, 4 * c + h, :], start=h == 0, stop=c == 0, skip_group_check=True)
                    if c:
                        need(f"s{c - 1}")
                        for h in range(HP):
                            ins = mm(x_b[:, 64 * h:64 * (h + 1)], aP[:, 4 * c + h, :], rec[:, 2 + c % 2, h, :], start=False, stop=True, skip_group_check=True)
                    mp.done(ins, f"x{c}")
                    need(f"x{c}")
                    for h in range(HP):
                        ins = mm(u_b[:, 64 * h:64 * (h + 1)], pP[:, 4 * c + h, :], rec[:, 0, h, :], start=True, stop=True)
                    mp.done(ins, f"u{c}")
                    need(f"u{c}")
                    if c < NC - 1:
                        for h in range(HP):
                            g, o = 4 * c + h, s_b[:, 64 * h:64 * (h + 1)]
                            mm(o, kP[:, g, :], vC[:, g, :], start=True, stop=False)
                            ins = mm(o, bP[:, g, :], rec[:, 1, h, :], start=False, stop=True)
                        mp.done(ins, f"s{c}")
                    need(f"ub{c}", ma)
                    if c:
                        need(f"sb{c - 1}", ma)
                    for h in range(HP):
                        g, o = 4 * c + h, y_b[:, 256 * (c % 2) + 64 * h:256 * (c % 2) + 64 * (h + 1)]
                        mm(o, vP[:, g, :], M2[:, g, 1, :], start=True, stop=False)
                        ins = mm(o, uP[:, 4 * (c % 2) + h, :], M1[:, g, 1, :], start=False, stop=c == 0)
                        if c:
                            ins = mm(o, uP[:, 8 + 4 * (c % 2) + h, :], AR[:, g, 1, :], start=False, stop=True)
                    mp.done(ins, f"y{c}")
                need("y")
                for b in range(2):
                    ins = mm(bank[4 + b][:], con("meanbd"), yT[:, 512 * b:512 * (b + 1)], start=True, stop=True)
                mp.done(ins, "mean")
                need("gsq", ma)
                for j in range(8):
                    ins = mm(bank[6][:, 2 * j:2 * j + 2], ysc[:, P * j:P * (j + 1)], con("meanbd")[:, 0:P:64], start=True, stop=True)
                mp.done(ins, "var")
                need("gvw")
                mp.done(spread_heads(4), "gvb")
                need("rsq", ma)
                for t in range(2):
                    for j in range(4):
                        ins = mm(bank[2][:, t:t + 1], ysc[:, SEQ * j + P * t:SEQ * j + P * (t + 1)], one, start=j == 0, stop=j == 3)
                mp.done(ins, "rms")
                need("rms_y2")
                for t in range(2):
                    ins = spread_rows(bank[3][:, P * t:P * (t + 1)], t)
                mp.done(ins, "rmsb")
                need("ylo1")
                for j in range(8):
                    name = f"out{j}"
                    b = blk(name)
                    mp.done(column_tile(b, bank[j][:, 0:SEQ]), name)
                    freed(name)

            pe.sem_inc(w_used, RING)
            pe.wait_ge(const_in, 16)
            pe.wait_ge(once, ONCE)
            pe.wait_ge(x_in, 16)
            for i in range(4):
                for d in range(2):
                    for t in range(2):
                        ins = turn(bank[i][:, SEQ * d + P * t:SEQ * d + P * (t + 1)], xtok[:, t, P * (2 * i + d):P * (2 * i + d + 1)])
                ins.then_inc(x_turned, 1)

            with pe.Fori(0, DEPTH) as l:
                pe.wait_ge(rows_in, l * ROWS_IN + ROWS_IN)
                pe.wait_ge(x_ready, l * 3 + 4)
                mp.done(turn(bank[5][:, 0:NROWS], rows[:]), "prm")
                ffn(l, 0)
                mixing(l)
                ffn(l, 1)
            pe.wait_ge(x_ready, DEPTH * 3 + 4)
            for t in range(2):
                for q in range(2):
                    for d in range(4):
                        ins = turn(bank[2 * t + q][:, P * d:P * (d + 1)], xT[:, 4 * q + d, P * t:P * (t + 1)])
                    ins.then_inc(out_turned, 1)


_VECTORS = ['ffn1_norm', 'mix_norm', 'q_lat_norm', 'kv_lat_norm', 'q_norm', 'k_norm', 'shift_mu', 'w0', 'a0', 'k_k', 'k_a',
            'r_k', 'gn_gain', 'gn_bias', 'out_norm_mla', 'out_norm_rwkv', 'ffn2_norm']
_WEIGHTS = ['ffn1_w_gate', 'ffn1_w_up', 'ffn1_w_down', 'w_in', 'w_q_up', 'w_kv_up', 'w2', 'a2', 'g2', 'w_out',
            'ffn2_w_gate', 'ffn2_w_up', 'ffn2_w_down']


def kernel(**inputs):
    import concourse.bacc as _bacc
    from concourse.bass_utils import run_bass_kernel_spmd as _run

    nc = _bacc.Bacc("TRN2", target_bir_lowering=False, num_devices=1)
    arrays, aps = {}, {}
    for name in ['x'] + _VECTORS + _WEIGHTS:
        a = np.ascontiguousarray(inputs[name])
        arrays[f"in_{name}_dram"] = a
        aps[name] = nc.dram_tensor(f"in_{name}_dram", a.shape, mybir.dt.from_np(a.dtype), kind="ExternalInput").ap()
    arrays["in_consts_dram"] = shape_constants()
    consts = nc.dram_tensor("in_consts_dram", (P, NCONST), F32, kind="ExternalInput").ap()
    out = nc.dram_tensor("out_0_dram", (1, SEQ, D), F32, kind="ExternalOutput").ap()
    build(nc, aps['x'], {k: aps[k] for k in _VECTORS}, {k: aps[k] for k in _WEIGHTS}, consts, out)
    r = _run(nc, [arrays], core_ids=[0])
    return r.results[0]["out_0_dram"]
```

```python
from contextlib import ExitStack

import numpy as np

import concourse.bass as bass
from concourse import mybir

F32 = mybir.dt.float32
F32R = mybir.dt.float32r
BF16 = mybir.dt.bfloat16
I32 = mybir.dt.int32
ALU = mybir.AluOpType
ACT = mybir.ActivationFunctionType
AX_X = mybir.AxisListType.X

P = 128
SEQ, D, DEPTH, F = 256, 1024, 2, 2816
DT, FT = D // P, F // P
H, NOPE, ROPE, DV = 8, 64, 32, 64
QK = NOPE + ROPE
QL, KVL = 256, 128
RW, HEAD, C = 512, 64, 64
NC = SEQ // C
HP = RW // P
G = NC * HP
MLA_IN = QL + KVL + ROPE
O_R = MLA_IN
O_WL = O_R + RW
O_K = O_WL + 64
O_V = O_K + RW
O_AL = O_V + RW
O_GL = O_AL + 64
GLORA = 160
EPS, GN_EPS = 1e-6, 64e-5
DECAY = float(np.exp(-0.5))
SCALE = float(QK) ** -0.5
LEVELS = 5
NEG = -1e30

ROWS = [("ffn1_norm", "ffn1_norm", 0, 8), ("mix_norm", "mix_norm", 0, 8), ("ffn2_norm", "ffn2_norm", 0, 8),
        ("q_lat_norm", "q_lat_norm", 0, 2), ("kv_lat_norm", "kv_lat_norm", 0, 1),
        ("mu_r", "shift_mu", 0, 4), ("mu_k", "shift_mu", O_K - MLA_IN, 4), ("mu_v", "shift_mu", O_V - MLA_IN, 4),
        ("mu_g", "shift_mu", O_GL - MLA_IN, 1), ("mu_g2", "shift_mu", O_GL - MLA_IN + 32, 1),
        ("mu_wa", None, 0, 1),
        ("w0", "w0", 0, 4), ("a0", "a0", 0, 4), ("k_k", "k_k", 0, 4), ("k_a", "k_a", 0, 4), ("r_k", "r_k", 0, 4),
        ("gn_gain", "gn_gain", 0, 4), ("gn_bias", "gn_bias", 0, 4),
        ("out_norm_mla", "out_norm_mla", 0, 4), ("out_norm_rwkv", "out_norm_rwkv", 0, 4)]
ROW = {}
_n = 0
for _name, _, _, _k in ROWS:
    ROW[_name] = _n
    _n += _k
NROWS = _n
MU_N = ROW["mu_wa"] + 1 - ROW["mu_r"]

CONST = {}
_n = 0
for _name, _k in [("ident", 128), ("ones", 128), ("onesbd", 128), ("meanbd", 128), ("eyes", 64), ("upper", 128),
                  ("level", LEVELS * 64), ("level1T", 64), ("reset", 256), ("cos", 32), ("sin", 32)]:
    CONST[_name] = (_n, _n + _k)
    _n += _k
NCONST = _n


def shape_constants():
    c = np.zeros((P, NCONST), np.float32)

    def put(name, a):
        lo, hi = CONST[name]
        c[:, lo:hi] = np.asarray(a, np.float32).reshape(P, hi - lo)

    i = np.arange(P)
    row, col = (i % C)[:, None], np.arange(C)[None, :]
    same = (i[:, None] // C) == (i[None, :] // C)
    put("ident", np.eye(P))
    put("ones", np.ones((P, P)))
    put("onesbd", same)
    put("meanbd", same / HEAD)
    put("eyes", row == col)
    put("upper", np.concatenate([row < col, row <= col], 1))
    lev = []
    for k in range(1, LEVELS + 1):
        s = 1 << k
        lev.append((row // (2 * s) == col // (2 * s)) & (row // s > col // s))
    put("level", np.concatenate(lev, 1))
    put("level1T", (row // 2 == col // 2) & (row < col))
    put("reset", np.broadcast_to((np.arange(SEQ) % C != 0)[None], (P, SEQ)))
    inv = np.float32(10000.0) ** (-np.arange(0, ROPE, 2, dtype=np.float32) / np.float32(ROPE))
    ang = np.arange(SEQ, dtype=np.float32)[:, None] * inv[None, :].astype(np.float32)
    put("cos", np.cos(ang).reshape(2, P, 16).transpose(1, 0, 2))
    put("sin", np.sin(ang).reshape(2, P, 16).transpose(1, 0, 2))
    return c


class Steps:

    def __init__(self, sem, names):
        self.sem, self.names, self.n = sem, names, 0
        assert len(set(names)) == len(names)

    def at(self, rnd, name):
        return rnd * len(self.names) + (self.names.index(name) + 1)

    def step(self, name):
        assert self.names[self.n % len(self.names)] == name, (name, self.names[self.n % len(self.names)])
        self.n += 1
        return 1


RW_TILES = ["wa"] + [f"r{i}" for i in range(4)] + [f"k{i}" for i in range(4)] + [f"v{i}" for i in range(4)] + ["g0", "g1"]
LAT_TILES = ["q0", "q1", "kv"]
MIX_BLOCKS = RW_TILES + LAT_TILES + ["pe", "kvup", "qup0", "qup1"] + [f"out{i}" for i in range(8)]
FFN_BLOCKS = 3 * FT
LAYER_BLOCKS = 2 * FFN_BLOCKS + len(MIX_BLOCKS)
RING = 3
assert FFN_BLOCKS % RING == 0 and len(MIX_BLOCKS) % RING == 0


class Block:

    def __init__(self, number, fills, slot):
        self.number, self.fills, self.slot = number, fills, slot


def ffn_block(l, which, kind, f):
    first = (FFN_BLOCKS + len(MIX_BLOCKS)) * which
    base, rounds = l * LAYER_BLOCKS + first, l * (LAYER_BLOCKS // RING) + first // RING
    if kind == "gate":
        return Block(base, rounds + 1, 0) if isinstance(f, int) and f == 0 else Block(base + (f * 3 - 1), rounds + f, 2)
    if kind == "up":
        return Block(base + 1, rounds + 1, 1) if isinstance(f, int) and f == 0 else Block(base + f * 3, rounds + (f + 1), 0)
    if isinstance(f, int) and f == FT - 1:
        return Block(base + (FFN_BLOCKS - 1), rounds + FT, 2)
    return Block(base + (f * 3 + 4), rounds + (f + 2), 1)


def mix_block(l, name):
    j = MIX_BLOCKS.index(name)
    return Block(l * LAYER_BLOCKS + (FFN_BLOCKS + j), l * (LAYER_BLOCKS // RING) + (FFN_BLOCKS // RING + j // RING + 1), j % RING)


def block_width(name):
    return DT * ROPE if name == "pe" else 768 if name[:3] == "qup" else 1024


def ffn_order(eng, gate, up, down):
    gate(0, 0), up(0, 0), gate(1, 1), up(1, 1), down(0, 0)
    with eng.Fori(0, FT // 2 - 1) as i:
        f = i * 2
        gate(f + 2, 0), up(f + 2, 0), down(f + 1, 1)
        gate(f + 3, 1), up(f + 3, 1), down(f + 2, 0)
    down(FT - 1, (FT - 1) % 2)


LO, UP = slice(0, 64), slice(64, 128)

def newton(prefix):
    return [f"{prefix}_{s}" for s in ("shift", "seed") + tuple(f"{x}{i}" for i in range(3) for x in ("sq", "err", "y"))]


NORM_V = [f"lo{i}" for i in range(4)] + ["ms"] + newton("norm") + ["rcol", "row"]
NORM_A = [f"hi{i}" for i in range(4)] + [f"sq{i}" for i in range(4)]
LV = range(1, LEVELS + 1)


def shift_steps():
    steps = []
    for i, t in enumerate(RW_TILES):
        steps += ([f"pr_{t}"] if i == 0 else []) + ([f"pr_{RW_TILES[i + 1]}"] if i + 1 < len(RW_TILES) else []) + [f"sh_{t}"]
        steps += {"k3": ["kk0"], "v0": ["lw"], "v2": ["lc"]}.get(t, [])
    return steps


QK_STEPS = [["qkms"] + newton("qk"), ["qkn"], ["qkg"], ["rope_m0", "rope0"], ["rope_m1", "rope1"]]

MIX_V = (["prm", "omm", "half_wa", "half_k", "one_k"] + NORM_V + shift_steps() + ["gs", "kkms"] + newton("kk") + ["kkw", "lat_copy", "kk"]
         + ["kf", "kmod", "a_c", "r_c", "lat_ms"] + newton("lat") + ["k_c", "lat_n", "kk2", "b_c", "lat_lo", "rk"]
         + [f"kn{j}" for j in range(4)] + ["kpe"] + [f"qe{j}" for j in range(4)] + ["bonus", "qkss"]
         + [f"g1_{c}" for c in range(NC)] + [f"g2_{c}" for c in range(NC)] + ["p1a", "p1"]
         + [f"tb{c}" for c in range(NC)] + [f"vc{c}" for c in range(NC)]
         + ["t0_0", "t0_1"]
         + [s for k in LV for s in [f"um{k}_0", f"um{k}_1"] + QK_STEPS[k - 1]
            + ([f"tc{k}_0", f"pc{k}_0", f"tc{k}_1", f"pc{k}_1"] if k < LEVELS else [])]
         + [f"qkT{i}" for i in range(8)]
         + ["mask0", "max0", "nmax0", "mask1", "max1", "nmax1", "pt0", "pt1"]
         + ["rinv", "o", "yms"] + newton("ym") + ["yn", "yg", "ylo0"]
         + [s for c in range(NC) for s in ([f"x{c}", f"u{c}"] + ([f"sa{c}"] if 0 < c < NC - 1 else [])
                                           + ([f"s{c}"] if c < NC - 1 else []))]
         + ["y", "yc", "gv"] + newton("gv") + ["gvw"] + ["gy", "gg", "gb", "gm"] + [f"ylo{4 + j}" for j in range(HP)]
         + [f"resm{i}" for i in range(4)] + ["rms"] + newton("rms") + ["rmsrow"] + [f"resr{i}" for i in range(4)])
MIX_A = (NORM_A + [f"mu_{t}" for t in RW_TILES[:5]] + ["tanh_w"] + [f"mu_{t}" for t in RW_TILES[5:9]]
         + ["tz", "ta", "kksq"] + [f"mu_{t}" for t in RW_TILES[9:]] + ["gs0", "E", "einv", "lat_sq", "gT"]
         + ["pe", "aP", "lat_hi", "kP", "bP", "vP"] + [f"v{j}" for j in range(4)] + ["qksq"]
         + [f"tk{c}" for c in range(NC)] + [f"tv{c}" for c in range(NC)] + ["lP", "pP"]
         + [f"{s}{k}_{b}" for k in LV for s in ("us", "ps") for b in range(2)]
         + ["ak", "ex0", "ex1", "ysq", "yhi0"] + [s for c in range(NC) for s in ([f"ub{c}"] + ([f"sb{c}"] if c < NC - 1 else []))]
         + ["gsq"] + [f"yhi{4 + j}" for j in range(HP)] + ["rsq"])
MIX_P = (["prm", "ss", "rb", "z", "a", "kkss", "kkb", "latss", "gup", "latb", "bsum"]
         + [f"g1_{c}" for c in range(NC)] + [f"g2_{c}" for c in range(NC)]
         + [f"tb{c}" for c in range(NC)] + [f"tk{c}" for c in range(NC)] + [f"tv{c}" for c in range(NC)] + ["ti0", "ti1"]
         + [s for k in LV for s in [f"u{k}_0", f"u{k}_1"] + [x for b in range(2) for x in
                                                           ([f"t{k}_{b}"] if k < LEVELS else []) + [f"p{k}_{b}"]]]
         + [f"qkT{i}" for i in range(8)] + ["sc0", "sc1", "pt0", "pv0", "pt1", "pv1", "yT"]
         + [s for c in range(NC) for s in [f"x{c}", f"u{c}"] + ([f"s{c}"] if c < NC - 1 else []) + [f"y{c}"]]
         + ["mean", "var", "gvb", "rms", "rmsb"])


def mu_col(tile):
    return {"wa": ("mu_wa", 0), "g0": ("mu_g", 0), "g1": ("mu_g2", 0)}.get(tile) or (f"mu_{tile[0]}", int(tile[1]))



def build(nc, x, par, w, consts, out):
    with ExitStack() as ctx:
        def sb(name, shape, dt=F32):
            return ctx.enter_context(nc.sbuf_tensor(name, shape, dt))

        def sem(name):
            return ctx.enter_context(nc.semaphore(name))

        bank = [ctx.enter_context(nc.psum_tensor(f"bank{i}", [P, 512], F32)) for i in range(8)]

        cst = sb("cst", [P, NCONST])
        rows = sb("rows", [NROWS, P])
        prm = sb("prm", [P, NROWS])
        omm = sb("omm", [P, MU_N])
        half = sb("half", [P, 16])
        qkgain = sb("qkgain", [P, 2, QK])
        xT = sb("xT", [P, DT, SEQ])
        xhi = sb("xhi", [P, DT, SEQ], F32R)
        xlo = sb("xlo", [P, DT, SEQ], F32R)
        raw = sb("raw", [P, RING, 1024])
        whi = sb("whi", [P, RING, 1024], F32R)
        wlo = sb("wlo", [P, RING, 1024], F32R)
        hhi = sb("hhi", [P, 2, SEQ], F32R)
        hlo = sb("hlo", [P, 2, SEQ], F32R)
        root = sb("root", [P, 3, 32])
        R = sb("R", [P, SEQ])
        scaled = sb("scaled", [P, 2, SEQ])
        rcol = sb("rcol", [P, 2])
        zeros = sb("zeros", [P, 512], BF16)
        E = sb("E", [P, G, C + 1])
        stat = sb("stat", [P, 256])
        shift = sb("shift", [P, 2, SEQ + 1])
        lora = sb("lora", [P, 3, SEQ])
        kpe = sb("kpe", [P, 2, ROPE])
        work = sb("work", [P, 16, 1024])
        pairs = sb("pairs", [P, 7, G, P])

        def unit(i, n=1):
            return work[:, i:i + n, :].rearrange("p u n -> p (u n)")

        def stacks(i):
            return unit(i).rearrange("p (g i) -> p g i", g=G)

        def double(i):
            return unit(i, 2).rearrange("p (g s i) -> p g s i", g=G, s=2)

        rT, kT, vT, zl, ta, lc, kk, sc, einv, kmod, gT, bonus = (unit(i) for i in range(12))
        w2a2 = unit(10)[:, 0:RW]
        g2a, g2b = unit(11)[:, 0:RW], unit(11)[:, RW:2 * RW]
        AR = double(12)
        bC, kC = stacks(14), stacks(15)
        def two(i, j):
            return work[:, i:j + 1:j - i, :].rearrange("p s (g i) -> p g s i", g=G)

        M1, M2 = two(0, 7), two(8, 9)
        vC, tC, pC, uC = stacks(2), stacks(14), stacks(15), stacks(1)
        rec = unit(3).rearrange("p (s h i) -> p s h i", s=4, h=HP)
        yT, yN, ysc, scrap = unit(4), unit(5), unit(8), unit(14)
        aP, bP, kP, vP, lP, pP, uP = (pairs[:, i] for i in range(7))
        lat = unit(3)[:, 0:768].rearrange("p (t n) -> p t n", t=3)
        lat_sq = unit(5)[:, 0:768].rearrange("p (t n) -> p t n", t=3)
        qk = unit(3, 3).rearrange("p (t s h d) -> p t s h d", t=2, s=2, h=H)
        qk_sq = unit(7, 3)
        rope = [lora[:, 0, :], lora[:, 1, :], lora[:, 2, :], scaled[:, 0, :]]
        qkT = [unit(u, 2).rearrange("p (h n) -> p h n", h=H) for u in (14, 0)]
        V = unit(6).rearrange("p (t h d) -> p t h d", t=2, h=H)
        prob = unit(3, 3)[:, 0:1536].rearrange("p (h k) -> p h k", h=4)
        probT = unit(3, 3)[:, 1536:3072].rearrange("p (m n) -> p m n", m=3)
        ymla = unit(8).rearrange("p (t n) -> p t n", t=2)
        ymT = unit(6).rearrange("p (f n) -> p f n", f=4)
        xsq = unit(3, 2).rearrange("p (t n) -> p t n", t=DT)
        ft = unit(5).rearrange("p (s n) -> p s n", n=SEQ)
        gs = unit(6)[:, 0:512].rearrange("p (s n) -> p s n", n=SEQ)
        xtok = unit(0, 2).rearrange("p (b n) -> p b n", b=2)

        def con(name):
            lo, hi = CONST[name]
            return cst[:, lo:hi]

        ident = con("ident")

        def col(name, i=0):
            return prm[:, ROW[name] + i:ROW[name] + i + 1]

        const_in, x_in, rows_in, small_in, half_in = (sem(s) for s in
                                                     ("const_in", "x_in", "rows_in", "small_in", "half_in"))
        raw_in = [sem(f"raw_in{i}") for i in range(RING)]
        hi_ready = sem("hi_ready")
        lo_ready = sem("lo_ready")
        w_used = sem("w_used")
        x_ready = sem("x_ready")
        tanh_done, hhi_done, hlo_done = sem("tanh_done"), sem("hhi_done"), sem("hlo_done")
        h_steps = sem("h_steps")
        once = sem("once")
        x_turned, out_turned, out_copied, out_done = (sem(s) for s in ("x_turned", "out_turned", "out_copied", "out_done"))
        fv, fa, fp = Steps(sem("fv"), NORM_V), Steps(sem("fa"), NORM_A), Steps(sem("fp"), ["ss", "rb"])
        mv, ma, mp = Steps(sem("mv"), MIX_V), Steps(sem("ma"), MIX_A), Steps(sem("mp"), MIX_P)
        ONCE = 5

        def quarter(phase, i):
            return phase * 4 + (i + 1)

        def mixed(l, name):
            return mix_block(l, name).number + (RING + 1)

        def tile_done(l, which, kind, f):
            return ffn_block(l, which, kind, f).number + (RING + 1)

        block = ctx.enter_context(nc.Block())

        @block.gpsimd
        def _(pool):
            pool.memset(zeros[:], 0.0).then_inc(once, 1)
            pool.memset(shift[:], 0.0).then_inc(once, 1)
            pool.memset(E[:, :, 0:1], 1.0).then_inc(once, 1)
            pool.memset(stat[:], 0.0).then_inc(once, 1)
            pool.memset(pairs[:].rearrange("p s g n -> p (s g n)"), 0.0).then_inc(once, 1)

        @block.sync
        def _(sp):
            sp.dma_start(cst[:], consts).then_inc(const_in, 16)
            sp.dma_start(xtok, x.rearrange("o (b p) n -> p (o b) n", p=P)).then_inc(x_in, 16)

            def load(b, dst, src):
                sp.wait_ge(lo_ready, b.number + 1)
                sp.dma_start(dst, src).then_inc(raw_in[b.slot], 16)

            def columns(src, l, first, n=P):
                return src[bass.ds(l, 1), :, bass.ds(first, n)].rearrange("a (t p) n -> p (a t) n", p=P)

            def in_slot(b, n=P):
                return raw[:, b.slot, 0:DT * n].rearrange("p (t n) -> p t n", t=DT)

            def ffn_loads(l, which):
                wg, wu, wd = (w[f"ffn{which + 1}_w_{s}"] for s in ("gate", "up", "down"))

                def gate(f, parity):
                    b = ffn_block(l, which, "gate", f)
                    load(b, in_slot(b), columns(wg, l, f * P))

                def up(f, parity):
                    b = ffn_block(l, which, "up", f)
                    load(b, in_slot(b), columns(wu, l, f * P))

                def down(f, parity):
                    b = ffn_block(l, which, "down", f)
                    load(b, raw[:, b.slot, :], wd[bass.ds(l, 1), bass.ds(f * P, P), :].rearrange("a p n -> p (a n)"))

                ffn_order(sp, gate, up, down)

            def flat(name, l, lo=None, hi=None):
                v = w[name][bass.ds(l, 1)] if lo is None else w[name][bass.ds(l, 1), lo:hi]
                return v.rearrange("a p n -> p (a n)")

            with sp.Fori(0, DEPTH) as l:
                for name, src, first, k in ROWS:
                    r0 = ROW[name]
                    if src is None:
                        for j, o in enumerate((O_WL - MLA_IN, O_AL - MLA_IN)):
                            sp.dma_start(rows[r0:r0 + 1, 64 * j:64 * j + 64],
                                         par["shift_mu"][bass.ds(l, 1), o:o + 64]).then_inc(rows_in, 16)
                    else:
                        v = par[src]
                        if len(v.shape) == 3:
                            v = v.rearrange("a h n -> a (h n)")
                        sp.dma_start(rows[r0:r0 + k, :], v[bass.ds(l, 1), first:first + P * k]
                                     .rearrange("a (k n) -> (a k) n", n=P)).then_inc(rows_in, 16)
                ffn_loads(l, 0)
                first_col = {"g0": O_GL, "g1": O_GL + GLORA - P, "q0": 0, "q1": P, "kv": QL}
                for i in range(4):
                    first_col.update({f"r{i}": O_R + P * i, f"k{i}": O_K + P * i, f"v{i}": O_V + P * i})
                for name in MIX_BLOCKS:
                    b = mix_block(l, name)
                    if name == "wa":
                        load(b, in_slot(b)[:, :, 0:64], columns(w["w_in"], l, O_WL, 64))
                        sp.dma_start(in_slot(b)[:, :, 64:128], columns(w["w_in"], l, O_AL, 64)).then_inc(half_in, 16)
                        sp.dma_start(w2a2[LO, :], flat("w2", l)).then_inc(small_in, 16)
                        sp.dma_start(w2a2[UP, :], flat("a2", l)).then_inc(small_in, 16)
                        sp.dma_start(g2a, flat("g2", l, 0, P)).then_inc(small_in, 16)
                        sp.dma_start(g2b[96:128, :], flat("g2", l, P, GLORA)).then_inc(small_in, 16)
                        for i, nm in enumerate(("q_norm", "k_norm")):
                            sp.dma_start(qkgain[:, i, :], par[nm][bass.ds(l, 1), :].to_broadcast((P, QK))).then_inc(small_in, 16)
                    elif name == "q0":
                        load(b, in_slot(b)[:, 4:, :], columns(w["w_in"], l, 0)[:, 4:, :])
                        sp.dma_start(in_slot(b)[:, 0:4, :], columns(w["w_in"], l, 0)[:, 0:4, :]).then_inc(half_in, 16)
                    elif name in first_col:
                        load(b, in_slot(b), columns(w["w_in"], l, first_col[name]))
                    elif name == "pe":
                        load(b, in_slot(b, ROPE), columns(w["w_in"], l, QL + KVL, ROPE))
                    elif name == "kvup":
                        load(b, raw[:, b.slot, :], flat("w_kv_up", l))
                    elif name[:3] == "qup":
                        c0 = 384 * int(name[3])
                        load(b, raw[:, b.slot, 0:768].rearrange("p (t n) -> p t n", t=2),
                             w["w_q_up"][bass.ds(l, 1), :, c0:c0 + 384].rearrange("a (t p) n -> p (a t) n", p=P))
                    else:
                        load(b, raw[:, b.slot, :], flat("w_out", l, P * int(name[3]), P * (int(name[3]) + 1)))
                ffn_loads(l, 1)
            for t in range(2):
                sp.wait_ge(out_copied, 2 * (t + 1))
                sp.dma_start(out[0, P * t:P * (t + 1), :], xtok[:, t, :]).then_inc(out_done, 16)
            sp.wait_ge(out_done, 32)

        ROWS_IN, SMALL_IN = 16 * (len(ROWS) + 1), 16 * 6

        @block.scalar
        def _(act):
            def split(b, width=1024, halves=None):
                act.wait_ge(raw_in[b.slot], b.fills * 16)
                if halves is not None:
                    act.wait_ge(half_in, halves * 16)
                act.wait_ge(w_used, b.number + 1)
                nc.scalar.activation(whi[:, b.slot, 0:width], raw[:, b.slot, 0:width], ACT.Copy).then_inc(hi_ready, 1)

            def norm(st, phase, gain):
                for i in range(4):
                    act.wait_ge(x_ready, quarter(phase, i))
                    for t in (2 * i, 2 * i + 1):
                        ins = nc.scalar.activation(xhi[:, t, :], xT[:, t, :], ACT.Copy, scale=col(gain, t))
                    ins.then_inc(st.sem, st.step(f"hi{i}"))
                for i in range(4):
                    nc.scalar.activation(xsq[:, 2 * i:2 * i + 2, :], xT[:, 2 * i:2 * i + 2, :], ACT.Square).then_inc(st.sem, st.step(f"sq{i}"))

            def ffn(l, which):
                rnd = l * 2 + which
                split(ffn_block(l, which, "gate", 0))
                split(ffn_block(l, which, "up", 0))
                norm(fa, l * 3 + 2 * which, f"ffn{which + 1}_norm")

                def gate(f, parity):
                    if not (isinstance(f, int) and f == 0):
                        split(ffn_block(l, which, "gate", f))

                def up(f, parity):
                    if not (isinstance(f, int) and f == 0):
                        split(ffn_block(l, which, "up", f))

                def down(f, parity):
                    tile = rnd * FT + f
                    act.wait_ge(h_steps, tile * 4 + 9)
                    nc.scalar.activation(ft[:, parity, :], gs[:, parity, :], ACT.Tanh, scale=0.5).then_inc(tanh_done, 1)
                    split(ffn_block(l, which, "down", f))
                    act.wait_ge(h_steps, tile * 4 + 12)
                    act.wait_ge(w_used, ffn_block(l, which, "up", 0).number + (f * 3 + 1))
                    nc.scalar.activation(hhi[:, parity, :], ft[:, 2 + parity, :], ACT.Copy).then_inc(hhi_done, 1)

                ffn_order(act, gate, up, down)

            def spread(dst, src, g0=0, n=G):
                nc.scalar.activation(dst[LO, g0:g0 + n, 0:64], src[LO], ACT.Copy)
                return nc.scalar.activation(dst[UP, g0:g0 + n, 64:128], src[UP], ACT.Copy)

            def mixing(l):
                def ahead(i):
                    if i < len(MIX_BLOCKS):
                        split(mix_block(l, MIX_BLOCKS[i]), block_width(MIX_BLOCKS[i]), {0: l * 2 + 1, Q0: l * 2 + 2}.get(i))

                Q0 = MIX_BLOCKS.index("q0")
                ahead(0), ahead(1)
                act.wait_ge(once, ONCE)
                norm(ma, l * 3 + 1, "mix_norm")
                ahead(2), ahead(3)
                for i, t in enumerate(RW_TILES):
                    if i and i + 3 < len(RW_TILES) + 3:
                        ahead(i + 3)
                    act.wait_ge(mv.sem, mv.at(l, f"pr_{t}"))
                    nc.scalar.activation(shift[:, i % 2, 1:SEQ + 1], scaled[:, i % 2, :], ACT.Copy,
                                                 scale=col(*mu_col(t))).then_inc(ma.sem, ma.step(f"mu_{t}"))
                    if t == "r3":
                        act.wait_ge(mv.sem, mv.at(l, "sh_wa"))
                        nc.scalar.activation(lora[LO, 0, :], lora[LO, 0, :], ACT.Tanh).then_inc(ma.sem, ma.step("tanh_w"))
                    if t == "k3":
                        act.wait_ge(mp.sem, mp.at(l, "z"))
                        for j in range(4):
                            ins = nc.scalar.activation(zl[:, SEQ * j:SEQ * (j + 1)], bank[4 + j // 2][:, SEQ * (j % 2):SEQ * (j % 2 + 1)],
                                                       ACT.Tanh, bias=half[:, j:j + 1], scale=0.5)
                        ins.then_inc(ma.sem, ma.step("tz"))
                        act.wait_ge(mp.sem, mp.at(l, "a"))
                        for j in range(4):
                            ins = nc.scalar.activation(ta[:, SEQ * j:SEQ * (j + 1)], bank[6 + j // 2][:, SEQ * (j % 2):SEQ * (j % 2 + 1)],
                                                       ACT.Tanh, bias=half[:, 4 + j:5 + j], scale=0.5)
                        ins.then_inc(ma.sem, ma.step("ta"))
                        act.wait_ge(mv.sem, mv.at(l, "kk0"))
                        nc.scalar.activation(sc, kk, ACT.Square).then_inc(ma.sem, ma.step("kksq"))
                act.wait_ge(mv.sem, mv.at(l, "sh_g1"))
                nc.scalar.activation(lora[:, 1:3, :], lora[:, 1:3, :], ACT.Tanh, scale=0.5).then_inc(ma.sem, ma.step("gs0"))
                act.wait_ge(mv.sem, mv.at(l, "lc"))
                lc_g = lc.rearrange("p (g i) -> p g i", g=G)
                nc.scalar.activation(E[:, :, 1:C + 1], lc_g, ACT.Exp).then_inc(ma.sem, ma.step("E"))
                nc.scalar.activation(einv, lc, ACT.Exp, scale=-1.0).then_inc(ma.sem, ma.step("einv"))
                ahead(len(RW_TILES) + 3)
                act.wait_ge(mv.sem, mv.at(l, "lat_copy"))
                act.wait_ge(ma.sem, ma.at(l, "einv"))
                nc.scalar.activation(lat_sq, lat, ACT.Square).then_inc(ma.sem, ma.step("lat_sq"))
                ahead(len(RW_TILES) + 4)
                act.wait_ge(mp.sem, mp.at(l, "gup"))
                for j in range(2):
                    ins = nc.scalar.activation(gT[:, 512 * j:512 * (j + 1)], bank[4 + j][:], ACT.Copy)
                ins.then_inc(ma.sem, ma.step("gT"))
                act.wait_ge(w_used, mixed(l, "pe"))
                for t in range(2):
                    ins = nc.scalar.activation(kpe[:, t, :], bank[2][:, ROPE * t:ROPE * (t + 1)], ACT.Copy, scale=rcol[:, t:t + 1])
                ins.then_inc(ma.sem, ma.step("pe"))
                ahead(len(RW_TILES) + 5)
                act.wait_ge(mv.sem, mv.at(l, "a_c"))
                spread(aP, AR[:, :, 0, :]).then_inc(ma.sem, ma.step("aP"))
                act.wait_ge(mv.sem, mv.at(l, "lat_n"))
                nc.scalar.activation(xhi[:, 0:3, :], lat, ACT.Copy).then_inc(ma.sem, ma.step("lat_hi"))
                act.wait_ge(mv.sem, mv.at(l, "k_c"))
                spread(kP, kC).then_inc(ma.sem, ma.step("kP"))
                act.wait_ge(mv.sem, mv.at(l, "b_c"))
                spread(bP, bC).then_inc(ma.sem, ma.step("bP"))
                vT_g = vT.rearrange("p (h c i) -> p c h i", h=HP, c=NC)
                for c in range(NC):
                    ins = spread(vP, vT_g[:, c], 4 * c, 4)
                ins.then_inc(ma.sem, ma.step("vP"))
                for j in range(4):
                    act.wait_ge(mv.sem, mv.at(l, f"kn{j}"))
                    t, hf = j // 2, j % 2
                    nc.scalar.activation(V[:, t, 4 * hf:4 * hf + 4, :], bank[j][:].rearrange("p (h d) -> p h d", h=4)[:, :, NOPE:],
                                         ACT.Copy).then_inc(ma.sem, ma.step(f"v{j}"))
                ahead(len(RW_TILES) + 6)
                act.wait_ge(mv.sem, mv.at(l, "qe3"))
                act.wait_ge(mp.sem, mp.at(l, "bsum"))
                nc.scalar.activation(qk_sq, unit(3, 3), ACT.Square).then_inc(ma.sem, ma.step("qksq"))
                ahead(len(RW_TILES) + 7), ahead(len(RW_TILES) + 8), ahead(len(RW_TILES) + 9)
                for s, dst in (("tk", kP), ("tv", vP)):
                    for c in range(NC):
                        act.wait_ge(mp.sem, mp.at(l, f"{s}{c}"))
                        b = bank[4 + c] if s == "tk" else bank[c]
                        nc.scalar.activation(dst[:, 4 * c:4 * c + 4, :], b[:].rearrange("p (g n) -> p g n", g=4), ACT.Copy).then_inc(ma.sem, ma.step(f"{s}{c}"))
                act.wait_ge(mv.sem, mv.at(l, "g1_3"))
                spread(lP, M1[:, :, 0, :]).then_inc(ma.sem, ma.step("lP"))
                act.wait_ge(mv.sem, mv.at(l, "p1"))
                spread(pP, pC).then_inc(ma.sem, ma.step("pP"))
                for k in LV:
                    for b in range(2):
                        act.wait_ge(mv.sem, mv.at(l, f"um{k}_{b}"))
                        spread(uP, uC[:, 8 * b:8 * b + 8], 8 * b, 8).then_inc(ma.sem, ma.step(f"us{k}_{b}"))
                    for b in range(2):
                        if k < LEVELS:
                            act.wait_ge(mv.sem, mv.at(l, f"pc{k}_{b}"))
                            spread(pP, pC[:, 8 * b:8 * b + 8], 8 * b, 8).then_inc(ma.sem, ma.step(f"ps{k}_{b}"))
                        else:
                            act.wait_ge(mp.sem, mp.at(l, f"p{k}_{b}"))
                            spread(pP, bank[2 + b][:].rearrange("p (g i) -> p g i", g=8), 8 * b, 8).then_inc(ma.sem, ma.step(f"ps{k}_{b}"))
                spread(lP, M2[:, :, 0, :]).then_inc(ma.sem, ma.step("ak"))
                for b in range(2):
                    act.wait_ge(mv.sem, mv.at(l, f"nmax{b}"))
                    if b:
                        act.wait_ge(mp.sem, mp.at(l, "pt0"))
                    for t in range(2):
                        for j in range(4):
                            i = 8 * b + 4 * t + j
                            src = bank[3 * b][:, P * j:P * (j + 1)] if t == 0 else bank[3 * b + 1 + j // 2][:, 256 * (j % 2):256 * (j % 2) + 256]
                            dst = prob[:, j, 0:P] if t == 0 else prob[:, j, P:3 * P]
                            ins = nc.scalar.activation(dst, src, ACT.Exp, bias=stat[:, 96 + i:97 + i], scale=SCALE,
                                                       accum_out=stat[:, 128 + i:129 + i])
                    ins.then_inc(ma.sem, ma.step(f"ex{b}"))
                act.wait_ge(mv.sem, mv.at(l, "o"))
                for t in range(2):
                    ins = nc.scalar.activation(scrap[:, 512 * t:512 * (t + 1)], ymla[:, t, :], ACT.Square, accum_out=stat[:, 160 + t:161 + t])
                ins.then_inc(ma.sem, ma.step("ysq"))
                act.wait_ge(mv.sem, mv.at(l, "yg"))
                nc.scalar.activation(xhi[:, 0:4, :], ymT, ACT.Copy).then_inc(ma.sem, ma.step("yhi0"))
                for c in range(NC):
                    act.wait_ge(mv.sem, mv.at(l, f"u{c}"))
                    spread(uP, rec[:, 1], 4 * (c % 2), 4).then_inc(ma.sem, ma.step(f"ub{c}"))
                    if c < NC - 1:
                        act.wait_ge(mv.sem, mv.at(l, f"s{c}"))
                        spread(uP, rec[:, 2 + (c + 1) % 2], 8 + 4 * ((c + 1) % 2), 4).then_inc(ma.sem, ma.step(f"sb{c}"))
                out0 = MIX_BLOCKS.index("out0")
                assert out0 == len(RW_TILES) + 7
                act.wait_ge(mv.sem, mv.at(l, "yc"))
                nc.scalar.activation(ysc, yT, ACT.Square).then_inc(ma.sem, ma.step("gsq"))
                ahead(out0 + 3), ahead(out0 + 4)
                act.wait_ge(mv.sem, mv.at(l, "gm"))
                for j in range(HP):
                    nc.scalar.activation(xhi[:, 4 + j, :], yN[:, SEQ * j:SEQ * (j + 1)], ACT.Copy,
                                                 scale=col("out_norm_rwkv", j)).then_inc(ma.sem, ma.step(f"yhi{4 + j}"))
                nc.scalar.activation(ysc, yN, ACT.Square).then_inc(ma.sem, ma.step("rsq"))
                for i in range(out0 + 5, len(MIX_BLOCKS)):
                    ahead(i)

            with act.Fori(0, DEPTH) as l:
                act.wait_ge(mv.sem, mv.at(l, "prm"))
                ffn(l, 0)
                mixing(l)
                ffn(l, 1)

        @block.vector
        def _(dve):
            V_ = nc.vector
            dve.sem_inc(lo_ready, RING)
            dve.sem_inc(h_steps, 8)

            def split(b, width=1024):
                dve.wait_ge(hi_ready, b.number + 1)
                V_.tensor_tensor(wlo[:, b.slot, 0:width], raw[:, b.slot, 0:width],
                                 whi[:, b.slot, 0:width].bitcast(F32), ALU.subtract).then_inc(lo_ready, 1)

            def rsqrt(st, rnd, prefix, n):
                v, y, t = (root[:, i, 0:n] for i in range(3))

                def did(name, ins):
                    ins.then_inc(st.sem, st.step(f"{prefix}_{name}"))
                    dve.wait_ge(st.sem, st.at(rnd, f"{prefix}_{name}"))

                did("shift", V_.tensor_scalar(t.bitcast(I32), v.bitcast(I32), 1, None, ALU.logical_shift_right))
                did("seed", V_.tensor_scalar(y.bitcast(I32), t.bitcast(I32), -1.0, float(0x5F3759DF), ALU.mult, ALU.add))
                for i in range(3):
                    did(f"sq{i}", V_.tensor_tensor(t, y, y, ALU.mult))
                    did(f"err{i}", V_.scalar_tensor_tensor(t, t, -0.5, v, ALU.mult, ALU.mult))
                    did(f"y{i}", V_.scalar_tensor_tensor(y, t, 1.5, y, ALU.add, ALU.mult))

            def norm(st, sta, stp, rnd, phase, gain, between, before_row, residual=None):
                if residual is not None:
                    residual(0)
                for i in range(4):
                    if residual is not None and i < 3:
                        residual(i + 1)
                    dve.wait_ge(x_ready, quarter(phase, i))
                    dve.wait_ge(sta.sem, sta.at(rnd, f"hi{i}"))
                    for t in (2 * i, 2 * i + 1):
                        ins = V_.scalar_tensor_tensor(xlo[:, t, :], xT[:, t, :], col(gain, t), xhi[:, t, :].bitcast(F32),
                                                      ALU.mult, ALU.subtract)
                    ins.then_inc(st.sem, st.step(f"lo{i}"))
                between()
                dve.wait_ge(stp.sem, stp.at(rnd, "ss"))
                V_.tensor_scalar(root[:, 0, 0:2], bank[7][:, 0:2], 1.0 / D, EPS, ALU.mult, ALU.add).then_inc(st.sem, st.step("ms"))
                dve.wait_ge(st.sem, st.at(rnd, "ms"))
                rsqrt(st, rnd, "norm", 2)
                before_row()
                V_.tensor_copy(rcol[:], root[:, 1, 0:2]).then_inc(st.sem, st.step("rcol"))
                dve.wait_ge(stp.sem, stp.at(rnd, "rb"))
                V_.tensor_copy(R[:], bank[7][:, 0:SEQ]).then_inc(st.sem, st.step("row"))
                dve.wait_ge(st.sem, st.at(rnd, "row"))

            def x_quarter(i):
                return xT[:, 2 * i:2 * i + 2, :].rearrange("p t n -> p (t n)")

            def ffn_residual(l, which):
                def quarter_of(i):
                    if i == 0:
                        dve.wait_ge(w_used, tile_done(l, which, "down", FT - 1))
                    V_.scalar_tensor_tensor(x_quarter(i), bank[i][:], 0.25, x_quarter(i), ALU.mult, ALU.add).then_inc(x_ready, 1)
                return quarter_of

            def mix_residual(l):
                def quarter_of(i):
                    if i == 0:
                        dve.wait_ge(w_used, mixed(l, "out7"))
                    if i >= 2:
                        dve.wait_ge(x_ready, quarter(l * 3 + 2, i - 2))
                    part = scrap[:, 0:512] if i % 2 == 0 else scrap[:, 512:1024]
                    V_.tensor_tensor(part.rearrange("p (t n) -> p t n", t=2), bank[4 + i][:].rearrange("p (t n) -> p t n", t=2),
                                     R[:].unsqueeze(1).to_broadcast((P, 2, SEQ)), ALU.mult).then_inc(mv.sem, mv.step(f"resr{i}"))
                    dve.wait_ge(mv.sem, mv.at(l, f"resr{i}"))
                    V_.tensor_tensor(x_quarter(i), x_quarter(i), part, ALU.add).then_inc(x_ready, 1)
                return quarter_of

            def ffn(l, which):
                rnd = l * 2 + which
                if which == 0:
                    split(ffn_block(l, which, "gate", 0))
                    split(ffn_block(l, which, "up", 0))
                norm(fv, fa, fp, rnd, l * 3 + 2 * which, f"ffn{which + 1}_norm", lambda: split(ffn_block(l, which, "gate", 1)),
                     lambda: None, mix_residual(l) if which else None)

                def gate(f, parity):
                    if not (isinstance(f, int) and f < 2):
                        split(ffn_block(l, which, "gate", f))

                def up(f, parity):
                    if not (isinstance(f, int) and f == 0):
                        split(ffn_block(l, which, "up", f))

                def down(f, parity):
                    tile = rnd * FT + f
                    g, u, t, h = bank[4 + parity], bank[6 + parity], ft[:, parity, :], ft[:, 2 + parity, :]
                    dve.wait_ge(w_used, tile_done(l, which, "gate", f))
                    V_.tensor_tensor(gs[:, parity, :], g[:, 0:SEQ], R[:], ALU.mult).then_inc(h_steps, 1)
                    dve.wait_ge(w_used, tile_done(l, which, "up", f))
                    V_.tensor_tensor(h, u[:, 0:SEQ], R[:], ALU.mult).then_inc(h_steps, 1)
                    dve.wait_ge(h_steps, tile * 4 + 10)
                    V_.tensor_tensor(h, h, gs[:, parity, :], ALU.mult).then_inc(h_steps, 1)
                    dve.wait_ge(tanh_done, tile + 1)
                    dve.wait_ge(h_steps, tile * 4 + 11)
                    V_.scalar_tensor_tensor(h, t, 1.0, h, ALU.add, ALU.mult).then_inc(h_steps, 1)
                    split(ffn_block(l, which, "down", f))
                    dve.wait_ge(hhi_done, tile + 1)
                    V_.tensor_tensor(hlo[:, parity, :], h, hhi[:, parity, :].bitcast(F32), ALU.subtract).then_inc(hlo_done, 1)

                ffn_order(dve, gate, up, down)
                if which == 0:
                    split(mix_block(l, MIX_BLOCKS[0]))
                    split(mix_block(l, MIX_BLOCKS[1]))
                else:
                    for i in range(4):
                        ffn_residual(l, which)(i)

            def mixing(l):
                def ahead(i):
                    if i < len(MIX_BLOCKS):
                        split(mix_block(l, MIX_BLOCKS[i]), block_width(MIX_BLOCKS[i]))

                def tiles(v, j):
                    return v[:, SEQ * j:SEQ * (j + 1)]

                def chunked(v):
                    return v.rearrange("p (h c i) -> p c h i", h=HP, c=NC)

                def grouped(v):
                    return v.rearrange("p (c h) i -> p c h i", h=HP)

                dve.wait_ge(once, ONCE)
                norm(mv, ma, mp, l, l * 3 + 1, "mix_norm", lambda: ahead(2), lambda: ahead(3), ffn_residual(l, 0))
                dest = {"wa": lora[:, 0, :], "g0": lora[:, 1, :], "g1": lora[:, 2, :]}
                for j in range(4):
                    dest.update({f"r{j}": tiles(rT, j), f"k{j}": tiles(kT, j), f"v{j}": tiles(vT, j)})

                def scale(i):
                    if i >= 2:
                        dve.wait_ge(mv.sem, mv.at(l, f"sh_{RW_TILES[i - 2]}"))
                    dve.wait_ge(w_used, mixed(l, RW_TILES[i]))
                    V_.tensor_tensor(scaled[:, i % 2, :], bank[i % 4][:, 0:SEQ], R[:], ALU.mult).then_inc(mv.sem, mv.step(f"pr_{RW_TILES[i]}"))

                scale(0)
                for i, t in enumerate(RW_TILES):
                    if i + 1 < len(RW_TILES):
                        scale(i + 1)
                    if i:
                        ahead(i + 3)
                    dve.wait_ge(mv.sem, mv.at(l, f"pr_{t}"))
                    dve.wait_ge(ma.sem, ma.at(l, f"mu_{t}"))
                    m = ROW[mu_col(t)[0]] + mu_col(t)[1] - ROW["mu_r"]
                    V_.scalar_tensor_tensor(dest[t], scaled[:, i % 2, :], omm[:, m:m + 1],
                                                            shift[:, i % 2, 0:SEQ], ALU.mult, ALU.add).then_inc(mv.sem, mv.step(f"sh_{t}"))
                    if t == "k3":
                        dve.wait_ge(mv.sem, mv.at(l, "sh_k3"))
                        for j in range(4):
                            ins = V_.tensor_scalar(tiles(kk, j), tiles(kT, j), col("k_k", j), None, ALU.mult)
                        ins.then_inc(mv.sem, mv.step("kk0"))
                    if t == "v0":
                        dve.wait_ge(ma.sem, ma.at(l, "tz"))
                        V_.tensor_scalar(zl, zl, -DECAY / 2, -DECAY / 2, ALU.mult, ALU.add).then_inc(mv.sem, mv.step("lw"))
                    if t == "v2":
                        dve.wait_ge(mv.sem, mv.at(l, "lw"))
                        for j in range(4):
                            ins = V_.tensor_tensor_scan(tiles(lc, j), con("reset"), tiles(zl, j), 0.0, ALU.mult, ALU.add)
                        ins.then_inc(mv.sem, mv.step("lc"))
                dve.wait_ge(ma.sem, ma.at(l, "gs0"))
                V_.tensor_scalar(lora[:, 1:3, :], lora[:, 1:3, :], 0.5, 0.5, ALU.mult, ALU.add).then_inc(mv.sem, mv.step("gs"))
                ahead(len(RW_TILES) + 3)
                dve.wait_ge(mp.sem, mp.at(l, "kkss"))
                V_.tensor_scalar(root[:, 0, 0:16], bank[4][:, 0:16], 1e-24, None, ALU.max).then_inc(mv.sem, mv.step("kkms"))
                dve.wait_ge(mv.sem, mv.at(l, "kkms"))
                rsqrt(mv, l, "kk", 16)
                V_.tensor_copy(sc.rearrange("p (g i) -> p g i", g=16), root[:, 1, 0:16].unsqueeze(2).to_broadcast((P, 16, 64))).then_inc(mv.sem, mv.step("kkw"))
                dve.wait_ge(mv.sem, mv.at(l, "lc"))
                dve.wait_ge(w_used, mixed(l, "kv"))
                for j in range(3):
                    ins = V_.tensor_tensor(lat[:, j, :], bank[(len(RW_TILES) + j) % 4][:, 0:SEQ], R[:], ALU.mult)
                ins.then_inc(mv.sem, mv.step("lat_copy"))
                dve.wait_ge(mp.sem, mp.at(l, "kkb"))
                for b in range(2):
                    s = slice(512 * b, 512 * (b + 1))
                    ins = V_.tensor_tensor(kk[:, s], kk[:, s], bank[6 + b][:], ALU.mult)
                ins.then_inc(mv.sem, mv.step("kk"))
                dve.wait_ge(ma.sem, ma.at(l, "ta"))
                dve.wait_ge(mv.sem, mv.at(l, "kk"))
                for j in range(4):
                    ins = V_.tensor_scalar(tiles(sc, j), tiles(ta, j), half[:, 8 + j:9 + j], half[:, 12 + j:13 + j], ALU.mult, ALU.add)
                ins.then_inc(mv.sem, mv.step("kf"))
                dve.wait_ge(mv.sem, mv.at(l, "kf"))
                V_.tensor_tensor(kmod, kT, sc, ALU.mult).then_inc(mv.sem, mv.step("kmod"))
                dve.wait_ge(ma.sem, ma.at(l, "einv"))
                E_c = E[:].rearrange("p (h c) i -> p c h i", h=HP)

                def per_chunk(fn):
                    for c in range(NC):
                        ins = fn(c)
                    return ins

                per_chunk(lambda c: V_.scalar_tensor_tensor(
                    grouped(AR[:, :, 0, :])[:, c], chunked(kk)[:, c], -1.0, E_c[:, c, :, 0:C], ALU.mult, ALU.mult)).then_inc(mv.sem, mv.step("a_c"))
                per_chunk(lambda c: V_.tensor_tensor(
                    grouped(AR[:, :, 1, :])[:, c], chunked(rT)[:, c], E_c[:, c, :, 1:C + 1], ALU.mult)).then_inc(mv.sem, mv.step("r_c"))
                dve.wait_ge(mv.sem, mv.at(l, "kkw"))
                dve.wait_ge(mp.sem, mp.at(l, "latss"))
                V_.tensor_scalar(root[:, 0, 0:2], bank[3][:, 0:2], 1.0 / QL, EPS, ALU.mult, ALU.add)
                V_.tensor_scalar(root[:, 0, 2:4], bank[3][:, 2:4], 1.0 / KVL, EPS, ALU.mult, ALU.add).then_inc(mv.sem, mv.step("lat_ms"))
                dve.wait_ge(mv.sem, mv.at(l, "lat_ms"))
                rsqrt(mv, l, "lat", 4)
                ahead(len(RW_TILES) + 4)
                dve.wait_ge(mv.sem, mv.at(l, "kmod"))
                per_chunk(lambda c: V_.tensor_tensor(grouped(kC)[:, c], chunked(kmod)[:, c], chunked(einv)[:, c], ALU.mult)).then_inc(mv.sem, mv.step("k_c"))
                dve.wait_ge(mp.sem, mp.at(l, "latb"))
                for j in range(3):
                    g = col("q_lat_norm", j) if j < 2 else col("kv_lat_norm")
                    r = bank[3][:, 0:SEQ] if j < 2 else bank[3][:, SEQ:512]
                    ins = V_.scalar_tensor_tensor(lat[:, j, :], lat[:, j, :], g, r, ALU.mult, ALU.mult)
                ins.then_inc(mv.sem, mv.step("lat_n"))
                ahead(len(RW_TILES) + 5)
                V_.scalar_tensor_tensor(sc, ta, 1.0, kk, ALU.add, ALU.mult).then_inc(mv.sem, mv.step("kk2"))
                dve.wait_ge(mv.sem, mv.at(l, "kk2"))
                per_chunk(lambda c: V_.scalar_tensor_tensor(
                    grouped(bC)[:, c], chunked(sc)[:, c], 0.5, chunked(einv)[:, c], ALU.mult, ALU.mult)).then_inc(mv.sem, mv.step("b_c"))
                dve.wait_ge(ma.sem, ma.at(l, "lat_hi"))
                V_.tensor_tensor(xlo[:, 0:3, :], lat, xhi[:, 0:3, :].bitcast(F32), ALU.subtract).then_inc(mv.sem, mv.step("lat_lo"))
                dve.wait_ge(mv.sem, mv.at(l, "b_c"))
                for j in range(4):
                    ins = V_.scalar_tensor_tensor(tiles(sc, j), tiles(rT, j), col("r_k", j), tiles(kmod, j), ALU.mult, ALU.mult)
                ins.then_inc(mv.sem, mv.step("rk"))
                dve.wait_ge(w_used, mixed(l, "kvup"))
                for j in range(4):
                    t, hf = j // 2, j % 2
                    V_.tensor_copy(qk[:, t, 1, 4 * hf:4 * hf + 4, 0:NOPE],
                                                  bank[j][:].rearrange("p (h d) -> p h d", h=4)[:, :, 0:NOPE]).then_inc(mv.sem, mv.step(f"kn{j}"))
                ahead(len(RW_TILES) + 6)
                dve.wait_ge(ma.sem, ma.at(l, "pe"))
                for t in range(2):
                    ins = V_.tensor_copy(qk[:, t, 1, :, NOPE:QK], kpe[:, t:t + 1, :].to_broadcast((P, H, ROPE)))
                ins.then_inc(mv.sem, mv.step("kpe"))
                for hf in range(2):
                    dve.wait_ge(w_used, mixed(l, f"qup{hf}"))
                    for t in range(2):
                        V_.tensor_copy(qk[:, t, 0, 4 * hf:4 * hf + 4, :],
                                                               bank[4 + 2 * t + hf][:, 0:384].rearrange("p (h d) -> p h d", h=4)).then_inc(mv.sem, mv.step(f"qe{2 * hf + t}"))
                dve.wait_ge(mp.sem, mp.at(l, "bsum"))
                for b in range(2):
                    s = slice(512 * b, 512 * (b + 1))
                    ins = V_.tensor_tensor(bonus[:, s], bank[b][:], vT[:, s], ALU.mult)
                ins.then_inc(mv.sem, mv.step("bonus"))
                dve.wait_ge(ma.sem, ma.at(l, "qksq"))
                V_.tensor_reduce(stat[:, 0:32], qk_sq.rearrange("p (g d) -> p g d", d=QK), AX_X, ALU.add).then_inc(mv.sem, mv.step("qkss"))
                dve.wait_ge(mv.sem, mv.at(l, "qkss"))
                upper = con("upper").rearrange("p (s i) -> p s i", s=2).unsqueeze(1).to_broadcast((P, 4, 2, C))
                for s, M, b0 in (("g1", M1, 0), ("g2", M2, 4)):
                    for c in range(NC):
                        dve.wait_ge(mp.sem, mp.at(l, f"{s}_{c}"))
                        V_.tensor_tensor(M[:, 4 * c:4 * c + 4],
                                                          bank[b0 + c][:].rearrange("p (g s i) -> p g s i", g=4, s=2), upper, ALU.mult).then_inc(mv.sem, mv.step(f"{s}_{c}"))
                dve.wait_ge(mv.sem, mv.at(l, "g1_3"))
                V_.tensor_tensor(pC, M1[:, :, 0, :], con("level1T").unsqueeze(1).to_broadcast((P, G, C)), ALU.mult).then_inc(mv.sem, mv.step("p1a"))
                dve.wait_ge(mv.sem, mv.at(l, "p1a"))
                V_.tensor_tensor(pC, pC, con("eyes").unsqueeze(1).to_broadcast((P, G, C)), ALU.add).then_inc(mv.sem, mv.step("p1"))
                for c in range(NC):
                    dve.wait_ge(mp.sem, mp.at(l, f"tb{c}"))
                    V_.tensor_copy(bP[:, 4 * c:4 * c + 4, :], bank[c][:].rearrange("p (g n) -> p g n", g=4)).then_inc(mv.sem, mv.step(f"tb{c}"))
                for c in range(NC):
                    dve.wait_ge(ma.sem, ma.at(l, f"tv{c}"))
                    b = bank[c][:].rearrange("p (g n) -> p g n", g=4)
                    V_.tensor_copy(vC[LO, 4 * c:4 * c + 4, :], b[LO, :, 0:64])
                    V_.tensor_copy(vC[UP, 4 * c:4 * c + 4, :], b[UP, :, 64:128]).then_inc(mv.sem, mv.step(f"vc{c}"))
                def eight(v, b):
                    return v[:, 8 * b:8 * b + 8, :]

                def bank8(i):
                    return bank[i][:].rearrange("p (g i) -> p g i", g=8)

                for b in range(2):
                    dve.wait_ge(mp.sem, mp.at(l, f"ti{b}"))
                    V_.tensor_copy(eight(tC, b), bank8(b)).then_inc(mv.sem, mv.step(f"t0_{b}"))
                q3 = unit(3, 3).rearrange("p (g d) -> p g d", d=QK)

                def qk_piece(k):
                    if k == 1:
                        V_.tensor_scalar(root[:, 0, :], stat[:, 0:32], 1.0 / QK, EPS, ALU.mult, ALU.add).then_inc(mv.sem, mv.step("qkms"))
                        dve.wait_ge(mv.sem, mv.at(l, "qkms"))
                        rsqrt(mv, l, "qk", 32)
                    elif k == 2:
                        V_.tensor_tensor(q3, q3, root[:, 1, :].unsqueeze(2).to_broadcast((P, 32, QK)), ALU.mult).then_inc(mv.sem, mv.step("qkn"))
                    elif k == 3:
                        dve.wait_ge(mv.sem, mv.at(l, "qkn"))
                        for t in range(2):
                            for s in range(2):
                                ins = V_.tensor_tensor(qk[:, t, s], qk[:, t, s], qkgain[:, s:s + 1, :].to_broadcast((P, H, QK)), ALU.mult)
                        ins.then_inc(mv.sem, mv.step("qkg"))
                    else:
                        t = k - 4
                        dve.wait_ge(mv.sem, mv.at(l, f"rope{t - 1}" if t else "qkg"))
                        qt = qk[:, t].rearrange("p s h d -> p (s h) d")
                        x1, x2 = qt[:, :, NOPE:NOPE + 16], qt[:, :, NOPE + 16:QK]
                        cos, sin = (con(n)[:, 16 * t:16 * t + 16].unsqueeze(1).to_broadcast((P, 2 * H, 16)) for n in ("cos", "sin"))
                        r = [v.rearrange("p (g n) -> p g n", g=2 * H) for v in rope]
                        for v, (a, b) in zip(r, ((x1, cos), (x2, sin), (x2, cos), (x1, sin))):
                            ins = V_.tensor_tensor(v, a, b, ALU.mult)
                        ins.then_inc(mv.sem, mv.step(f"rope_m{t}"))
                        dve.wait_ge(mv.sem, mv.at(l, f"rope_m{t}"))
                        V_.tensor_tensor(x1, r[0], r[1], ALU.subtract)
                        V_.tensor_tensor(x2, r[2], r[3], ALU.add).then_inc(mv.sem, mv.step(f"rope{t}"))

                for k in LV:
                    lev = con("level")[:, 64 * (k - 1):64 * k].unsqueeze(1).to_broadcast((P, 8, C))
                    for b in range(2):
                        dve.wait_ge(mp.sem, mp.at(l, f"u{k}_{b}"))
                        V_.tensor_tensor(eight(uC, b), bank8(4 + b), lev, ALU.mult).then_inc(mv.sem, mv.step(f"um{k}_{b}"))
                    qk_piece(k)
                    if k < LEVELS:
                        for b in range(2):
                            dve.wait_ge(mp.sem, mp.at(l, f"t{k}_{b}"))
                            V_.tensor_copy(eight(tC, b), bank8(b)).then_inc(mv.sem, mv.step(f"tc{k}_{b}"))
                            dve.wait_ge(mp.sem, mp.at(l, f"p{k}_{b}"))
                            V_.tensor_copy(eight(pC, b), bank8(2 + b)).then_inc(mv.sem, mv.step(f"pc{k}_{b}"))
                for i in range(8):
                    s, t, hq = i // 4, (i // 2) % 2, i % 2
                    dve.wait_ge(mp.sem, mp.at(l, f"qkT{i}"))
                    V_.tensor_copy(qkT[s][0:QK, 4 * hq:4 * hq + 4, P * t:P * (t + 1)],
                                                   bank[i][0:QK, :].rearrange("p (h n) -> p h n", h=4)).then_inc(mv.sem, mv.step(f"qkT{i}"))
                for b in range(2):
                    dve.wait_ge(mp.sem, mp.at(l, f"sc{b}"))
                    V_.memset(bank[3 * b][LO, :].rearrange("p (h k) -> p h k", h=4)[:, :, 64:128], NEG)
                    for j in range(2):
                        ins = V_.memset(bank[3 * b + 1 + j][LO, :].rearrange("p (h k) -> p h k", h=2)[:, :, 192:256], NEG)
                    ins.then_inc(mv.sem, mv.step(f"mask{b}"))
                    dve.wait_ge(mv.sem, mv.at(l, f"mask{b}"))
                    m0 = 64 + 8 * b
                    V_.tensor_reduce(stat[:, m0:m0 + 4], bank[3 * b][:].rearrange("p (h k) -> p h k", h=4), AX_X, ALU.max)
                    for j in range(2):
                        ins = V_.tensor_reduce(stat[:, m0 + 4 + 2 * j:m0 + 6 + 2 * j],
                                               bank[3 * b + 1 + j][:].rearrange("p (h k) -> p h k", h=2), AX_X, ALU.max)
                    ins.then_inc(mv.sem, mv.step(f"max{b}"))
                    dve.wait_ge(mv.sem, mv.at(l, f"max{b}"))
                    V_.tensor_scalar(stat[:, 96 + 8 * b:104 + 8 * b], stat[:, m0:m0 + 8], -SCALE, None, ALU.mult).then_inc(mv.sem, mv.step(f"nmax{b}"))
                ahead(len(RW_TILES) + 7), ahead(len(RW_TILES) + 8)
                for b in range(2):
                    dve.wait_ge(mp.sem, mp.at(l, f"pt{b}"))
                    if b:
                        dve.wait_ge(mp.sem, mp.at(l, "pv0"))
                    for m, bk in enumerate((6, 7, 0)):
                        ins = V_.tensor_copy(probT[:, m, :], bank[bk][:])
                    ins.then_inc(mv.sem, mv.step(f"pt{b}"))
                ahead(len(RW_TILES) + 9)
                dve.wait_ge(ma.sem, ma.at(l, "ex1"))
                V_.reciprocal(stat[:, 144:160], stat[:, 128:144]).then_inc(mv.sem, mv.step("rinv"))
                dve.wait_ge(mv.sem, mv.at(l, "rinv"))
                dve.wait_ge(mp.sem, mp.at(l, "pv1"))
                rinv = stat[:, 144:160].rearrange("p (b t j) -> p b t j", b=2, t=2)
                for t in range(2):
                    for b in range(2):
                        y = ymla[:, t, 256 * b:256 * b + 256].rearrange("p (j d) -> p j d", j=4)
                        o = bank[1 + t][:, 256 * b:256 * b + 256].rearrange("p (j d) -> p j d", j=4)
                        ins = V_.tensor_tensor(y, o, rinv[:, b, t, :].unsqueeze(2).to_broadcast((P, 4, DV)), ALU.mult)
                ins.then_inc(mv.sem, mv.step("o"))
                dve.wait_ge(ma.sem, ma.at(l, "ysq"))
                V_.tensor_scalar(root[:, 0, 0:2], stat[:, 160:162], 1.0 / (H * DV), EPS, ALU.mult, ALU.add).then_inc(mv.sem, mv.step("yms"))
                dve.wait_ge(mv.sem, mv.at(l, "yms"))
                rsqrt(mv, l, "ym", 2)
                for t in range(2):
                    ins = V_.tensor_scalar(ymla[:, t, :], ymla[:, t, :], root[:, 1, t:t + 1], None, ALU.mult)
                ins.then_inc(mv.sem, mv.step("yn"))
                dve.wait_ge(mp.sem, mp.at(l, "yT"))
                for f in range(4):
                    ins = V_.tensor_scalar(ymT[:, f, :], bank[3 + f // 2][:, 256 * (f % 2):256 * (f % 2) + 256],
                                           col("out_norm_mla", f), None, ALU.mult)
                ins.then_inc(mv.sem, mv.step("yg"))
                dve.wait_ge(ma.sem, ma.at(l, "yhi0"))
                V_.tensor_tensor(xlo[:, 0:4, :], ymT, xhi[:, 0:4, :].bitcast(F32), ALU.subtract).then_inc(mv.sem, mv.step("ylo0"))
                for c in range(NC):
                    dve.wait_ge(mp.sem, mp.at(l, f"x{c}"))
                    V_.tensor_copy(rec[:, 0], bank[4 + c % 2][:, 0:256].rearrange("p (h i) -> p h i", h=HP)).then_inc(mv.sem, mv.step(f"x{c}"))
                    dve.wait_ge(mp.sem, mp.at(l, f"u{c}"))
                    V_.tensor_copy(rec[:, 1], bank[6 + c % 2][:, 0:256].rearrange("p (h i) -> p h i", h=HP)).then_inc(mv.sem, mv.step(f"u{c}"))
                    if c < NC - 1:
                        dve.wait_ge(mp.sem, mp.at(l, f"s{c}"))
                        grown = bank[2 + c % 2][:, 0:256].rearrange("p (h i) -> p h i", h=HP)
                        new = rec[:, 2 + (c + 1) % 2]
                        if c:
                            V_.tensor_tensor(new, grown, rec[:, 2 + c % 2], ALU.add).then_inc(mv.sem, mv.step(f"sa{c}"))
                            dve.wait_ge(mv.sem, mv.at(l, f"sa{c}"))
                            grown = new
                        V_.tensor_tensor(new, grown, E_c[:, c, :, C:C + 1].to_broadcast((P, HP, HEAD)), ALU.mult).then_inc(mv.sem, mv.step(f"s{c}"))
                for b in range(2):
                    dve.wait_ge(mp.sem, mp.at(l, f"y{2 * b + 1}"))
                    ins = V_.tensor_copy(yT[:, 512 * b:512 * (b + 1)], bank[b][:])
                ins.then_inc(mv.sem, mv.step("y"))
                dve.wait_ge(mv.sem, mv.at(l, "y"))
                dve.wait_ge(mp.sem, mp.at(l, "mean"))
                for b in range(2):
                    s = slice(512 * b, 512 * (b + 1))
                    ins = V_.tensor_tensor(yT[:, s], yT[:, s], bank[4 + b][:], ALU.subtract)
                ins.then_inc(mv.sem, mv.step("yc"))
                dve.wait_ge(mp.sem, mp.at(l, "var"))
                V_.tensor_scalar(root[:, 0, 0:16], bank[6][:, 0:16], GN_EPS, None, ALU.add).then_inc(mv.sem, mv.step("gv"))
                dve.wait_ge(mv.sem, mv.at(l, "gv"))
                rsqrt(mv, l, "gv", 16)
                V_.tensor_copy(sc.rearrange("p (g i) -> p g i", g=16), root[:, 1, 0:16].unsqueeze(2).to_broadcast((P, 16, 64))).then_inc(mv.sem, mv.step("gvw"))
                out0 = MIX_BLOCKS.index("out0")
                ahead(out0 + 3)
                dve.wait_ge(mp.sem, mp.at(l, "gvb"))
                for b in range(2):
                    s = slice(512 * b, 512 * (b + 1))
                    ins = V_.tensor_tensor(yT[:, s], yT[:, s], bank[4 + b][:], ALU.mult)
                ins.then_inc(mv.sem, mv.step("gy"))
                dve.wait_ge(mv.sem, mv.at(l, "gy"))
                y_h = yT.rearrange("p (c h i) -> p h c i", c=NC, h=HP)
                for j in range(HP):
                    ins = V_.tensor_scalar(tiles(yN, j).rearrange("p (c i) -> p c i", c=NC), y_h[:, j],
                                           col("gn_gain", j), col("gn_bias", j), ALU.mult, ALU.add)
                ins.then_inc(mv.sem, mv.step("gg"))
                dve.wait_ge(mv.sem, mv.at(l, "gg"))
                V_.tensor_tensor(yN, yN, bonus, ALU.add).then_inc(mv.sem, mv.step("gb"))
                dve.wait_ge(mv.sem, mv.at(l, "gb"))
                V_.tensor_tensor(yN, yN, gT, ALU.mult).then_inc(mv.sem, mv.step("gm"))
                ahead(out0 + 4)
                for j in range(HP):
                    dve.wait_ge(ma.sem, ma.at(l, f"yhi{4 + j}"))
                    V_.scalar_tensor_tensor(xlo[:, 4 + j, :], tiles(yN, j), col("out_norm_rwkv", j),
                                                                xhi[:, 4 + j, :].bitcast(F32), ALU.mult, ALU.subtract).then_inc(mv.sem, mv.step(f"ylo{4 + j}"))
                dve.wait_ge(w_used, mixed(l, "out3"))
                for i in range(4):
                    V_.tensor_tensor(x_quarter(i), x_quarter(i), bank[i][:], ALU.add).then_inc(mv.sem, mv.step(f"resm{i}"))
                ahead(out0 + 5)
                dve.wait_ge(mp.sem, mp.at(l, "rms"))
                V_.tensor_scalar(root[:, 0, 0:2], bank[0][:, 0:2], 1.0 / RW, EPS, ALU.mult, ALU.add).then_inc(mv.sem, mv.step("rms"))
                dve.wait_ge(mv.sem, mv.at(l, "rms"))
                rsqrt(mv, l, "rms", 2)
                ahead(out0 + 6)
                dve.wait_ge(mp.sem, mp.at(l, "rmsb"))
                V_.tensor_copy(R[:], bank[1][:, 0:SEQ]).then_inc(mv.sem, mv.step("rmsrow"))
                ahead(out0 + 7)
                dve.wait_ge(mv.sem, mv.at(l, "rmsrow"))
                split(ffn_block(l, 1, "gate", 0))
                split(ffn_block(l, 1, "up", 0))

            dve.wait_ge(const_in, 16)
            for i in range(4):
                dve.wait_ge(x_turned, i + 1)
                V_.tensor_copy(xT[:, 2 * i:2 * i + 2, :].rearrange("p t n -> p (t n)"), bank[i][:]).then_inc(x_ready, 1)

            with dve.Fori(0, DEPTH) as l:
                dve.wait_ge(mp.sem, mp.at(l, "prm"))
                V_.tensor_copy(prm[:], bank[5][:, 0:NROWS]).then_inc(mv.sem, mv.step("prm"))
                dve.wait_ge(mv.sem, mv.at(l, "prm"))
                m = ROW["mu_r"]
                V_.tensor_scalar(omm[:], prm[:, m:m + MU_N], -1.0, 1.0, ALU.mult, ALU.add).then_inc(mv.sem, mv.step("omm"))
                V_.tensor_scalar(half[:, 0:8], prm[:, ROW["w0"]:ROW["w0"] + 8], 0.5, None, ALU.mult).then_inc(mv.sem, mv.step("half_wa"))
                V_.tensor_scalar(half[:, 8:12], prm[:, ROW["k_a"]:ROW["k_a"] + 4], 0.5, None, ALU.mult).then_inc(mv.sem, mv.step("half_k"))
                V_.tensor_scalar(half[:, 12:16], prm[:, ROW["k_a"]:ROW["k_a"] + 4], -0.5, 1.0, ALU.mult, ALU.add).then_inc(mv.sem, mv.step("one_k"))
                ffn(l, 0)
                mixing(l)
                ffn(l, 1)
            for i in range(4):
                dve.wait_ge(out_turned, i + 1)
                V_.tensor_copy(unit(0, 2)[:, 512 * i:512 * (i + 1)], bank[i][:]).then_inc(out_copied, 1)

        @block.tensor
        def _(pe):
            mm = nc.tensor.matmul

            def three(out, hi, lo, mhi, mlo, start, stop, **kw):
                mm(out, hi, mhi, start=start, stop=False, **kw)
                mm(out, hi, mlo, start=False, stop=False, **kw)
                return mm(out, lo, mhi, start=False, stop=stop, **kw)

            def turn(out, in_):
                n = in_.shape[0]
                return nc.tensor.transpose(out, in_, ident[0:n, 0:n])

            def squares(st, sta, rnd):
                for i in range(4):
                    pe.wait_ge(sta.sem, sta.at(rnd, f"sq{i}"))
                for n in range(2):
                    for t in range(DT):
                        ins = mm(bank[7][:, n:n + 1], xsq[:, t, P * n:P * (n + 1)], con("ones")[:, 0:1], start=t == 0, stop=t == DT - 1)
                ins.then_inc(st.sem, st.step("ss"))

            def spread_rows(out, i):
                return mm(out, root[:, 1, i:i + 1].to_broadcast((P, P)), ident, start=True, stop=True)

            def spread_heads(b0):
                for j in range(8):
                    ins = mm(bank[b0 + j // 4][:, P * (j % 4):P * (j % 4 + 1)], sc[:, P * j:P * (j + 1)], ident, start=True, stop=True)
                return ins

            def norm_rows(st, stv, rnd):
                pe.wait_ge(stv.sem, stv.at(rnd, "norm_y2"))
                for n in range(2):
                    ins = spread_rows(bank[7][:, P * n:P * (n + 1)], n)
                ins.then_inc(st.sem, st.step("rb"))

            def keep_clock(b, n):
                for _ in range(n):
                    mm(bank[b][:], zeros[:, 0:P], zeros[:], start=True, stop=True)

            def split_ready(b):
                pe.wait_ge(lo_ready, b.number + (RING + 1))

            def column_tile(b, out, wait=None):
                for t in range(DT):
                    if wait is not None and t % 2 == 0:
                        wait(t // 2)
                    s = slice(P * t, P * (t + 1))
                    ins = three(out, whi[:, b.slot, s], wlo[:, b.slot, s], xhi[:, t, :], xlo[:, t, :], t == 0, t == DT - 1)
                return ins

            def ffn(l, which):
                rnd = l * 2 + which
                if which == 0:
                    for i in range(4):
                        pe.wait_ge(x_ready, quarter(l * 3, i))
                else:
                    pe.wait_ge(mv.sem, mv.at(l, "resm3"))
                    keep_clock(0, 16)
                for i in range(4):
                    mm(bank[i][:], zeros[0:1, 0:P], zeros[0:1, :], start=True, stop=False, skip_group_check=True)

                def gate(f, parity):
                    first = isinstance(f, int) and f == 0
                    b = ffn_block(l, which, "gate", f)
                    split_ready(b)
                    pe.wait_ge(h_steps, (rnd * FT + f) * 4 + 2)
                    column_tile(b, bank[4 + parity][:, 0:SEQ],
                                (lambda i: pe.wait_ge(fv.sem, fv.at(rnd, f"lo{i}"))) if first else None).then_inc(w_used, 1)
                    if isinstance(f, int) and f == 1:
                        norm_rows(fp, fv, rnd)
                        pe.wait_ge(fv.sem, fv.at(rnd, "row"))

                def up(f, parity):
                    b = ffn_block(l, which, "up", f)
                    split_ready(b)
                    column_tile(b, bank[6 + parity][:, 0:SEQ]).then_inc(w_used, 1)
                    if isinstance(f, int) and f == 0:
                        squares(fp, fa, rnd)

                def down(f, parity):
                    last = isinstance(f, int) and f == FT - 1
                    b = ffn_block(l, which, "down", f)
                    split_ready(b)
                    pe.wait_ge(hlo_done, (rnd * FT + f) + 1)
                    for t in range(DT):
                        s = slice(P * t, P * (t + 1))
                        ins = three(bank[t // 2][:, SEQ * (t % 2):SEQ * (t % 2 + 1)], whi[:, b.slot, s], wlo[:, b.slot, s],
                                    hhi[:, parity, :], hlo[:, parity, :], False, last, skip_group_check=True)
                    ins.then_inc(w_used, 1)

                ffn_order(pe, gate, up, down)

            def mixing(l):
                def blk(name):
                    b = mix_block(l, name)
                    split_ready(b)
                    return b

                pe.wait_ge(once, ONCE)
                keep_clock(4, 18)
                tiles = RW_TILES + LAT_TILES
                for i, t in enumerate(tiles):
                    b = blk(t)
                    if i >= 4 and i - 4 < len(RW_TILES):
                        pe.wait_ge(mv.sem, mv.at(l, f"pr_{tiles[i - 4]}"))
                    out = bank[i % 4][:, 0:SEQ]
                    for kt in range(DT):
                        if i == 0 and kt % 2 == 0:
                            pe.wait_ge(mv.sem, mv.at(l, f"lo{kt // 2}"))
                        s = slice(P * kt, P * (kt + 1))
                        ins = three(out, whi[:, b.slot, s], wlo[:, b.slot, s], xhi[:, kt, :], xlo[:, kt, :], kt == 0, kt == DT - 1)
                    ins.then_inc(w_used, 1)
                    if t == "r0":
                        squares(mp, ma, l)
                    if t == "r1":
                        norm_rows(mp, mv, l)
                    if t == "k3":
                        pe.wait_ge(small_in, l * SMALL_IN + SMALL_IN)
                        pe.wait_ge(ma.sem, ma.at(l, "tanh_w"))
                        for nm, part, b0 in (("z", LO, 4), ("a", UP, 6)):
                            for j in range(4):
                                ins = mm(bank[b0 + j // 2][:, SEQ * (j % 2):SEQ * (j % 2 + 1)], w2a2[part, P * j:P * (j + 1)],
                                         lora[part, 0, :], start=True, stop=True)
                            ins.then_inc(mp.sem, mp.step(nm))
                    if t == "g1":
                        pe.wait_ge(ma.sem, ma.at(l, "kksq"))
                        heads = con("onesbd")[:, 0:P:64]
                        for j in range(8):
                            ins = mm(bank[4][:, 2 * j:2 * j + 2], sc[:, P * j:P * (j + 1)], heads, start=True, stop=True)
                        ins.then_inc(mp.sem, mp.step("kkss"))

                pe.wait_ge(mv.sem, mv.at(l, "kkw"))
                spread_heads(6).then_inc(mp.sem, mp.step("kkb"))
                b = blk("pe")
                pe.wait_ge(mv.sem, mv.at(l, "pr_g1"))
                for t in range(2):
                    for kt in range(DT):
                        s, n = slice(ROPE * kt, ROPE * (kt + 1)), slice(P * t, P * (t + 1))
                        o = bank[2][:, ROPE * t:ROPE * (t + 1)]
                        mm(o, xhi[:, kt, n], whi[:, b.slot, s], start=kt == 0, stop=False)
                        mm(o, xlo[:, kt, n], whi[:, b.slot, s], start=False, stop=False)
                        ins = mm(o, xhi[:, kt, n], wlo[:, b.slot, s], start=False, stop=kt == DT - 1)
                ins.then_inc(w_used, 1)
                pe.wait_ge(ma.sem, ma.at(l, "lat_sq"))
                one = con("ones")[:, 0:1]
                for t in range(2):
                    n = slice(P * t, P * (t + 1))
                    mm(bank[3][:, t:t + 1], lat_sq[:, 0, n], one, start=True, stop=False)
                    mm(bank[3][:, t:t + 1], lat_sq[:, 1, n], one, start=False, stop=True)
                    ins = mm(bank[3][:, 2 + t:3 + t], lat_sq[:, 2, n], one, start=True, stop=True)
                ins.then_inc(mp.sem, mp.step("latss"))
                pe.wait_ge(mv.sem, mv.at(l, "gs"))
                for j in range(4):
                    o = bank[4 + j // 2][:, SEQ * (j % 2):SEQ * (j % 2 + 1)]
                    mm(o, g2a[:, P * j:P * (j + 1)], lora[:, 1, :], start=True, stop=False)
                    ins = mm(o, g2b[96:128, P * j:P * (j + 1)], lora[96:128, 2, :], start=False, stop=True)
                ins.then_inc(mp.sem, mp.step("gup"))
                pe.wait_ge(mv.sem, mv.at(l, "lat_y2"))
                for j in range(4):
                    ins = spread_rows(bank[3][:, P * j:P * (j + 1)], j)
                ins.then_inc(mp.sem, mp.step("latb"))
                b = blk("kvup")
                pe.wait_ge(mv.sem, mv.at(l, "lat_lo"))
                pe.wait_ge(ma.sem, ma.at(l, "pe"))
                for t in range(2):
                    n = slice(P * t, P * (t + 1))
                    for hf in range(2):
                        o, s = bank[2 * t + hf][:], slice(512 * hf, 512 * (hf + 1))
                        mm(o, xhi[:, 2, n], whi[:, b.slot, s], start=True, stop=False)
                        mm(o, xlo[:, 2, n], whi[:, b.slot, s], start=False, stop=False)
                        ins = mm(o, xhi[:, 2, n], wlo[:, b.slot, s], start=False, stop=True)
                ins.then_inc(w_used, 1)
                pe.wait_ge(ma.sem, ma.at(l, "gT"))
                for hf in range(2):
                    b = blk(f"qup{hf}")
                    for t in range(2):
                        o, n = bank[4 + 2 * t + hf][:, 0:384], slice(P * t, P * (t + 1))
                        for kt in range(2):
                            s = slice(384 * kt, 384 * (kt + 1))
                            mm(o, xhi[:, kt, n], whi[:, b.slot, s], start=kt == 0, stop=False)
                            mm(o, xlo[:, kt, n], whi[:, b.slot, s], start=False, stop=False)
                            ins = mm(o, xhi[:, kt, n], wlo[:, b.slot, s], start=False, stop=kt == 1)
                    ins.then_inc(w_used, 1)
                pe.wait_ge(ma.sem, ma.at(l, "v1"))
                pe.wait_ge(mv.sem, mv.at(l, "rk"))
                for j in range(2):
                    ins = mm(bank[j][:], con("onesbd"), sc[:, 512 * j:512 * (j + 1)], start=True, stop=True)
                ins.then_inc(mp.sem, mp.step("bsum"))
                pe.wait_ge(mv.sem, mv.at(l, "bonus"))
                pe.wait_ge(ma.sem, ma.at(l, "v3"))
                pe.wait_ge(mv.sem, mv.at(l, "qe3"))
                pe.wait_ge(ma.sem, ma.at(l, "vP"))
                for s, lhs, b0 in (("g1", bP, 0), ("g2", kP, 4)):
                    for c in range(NC):
                        for h in range(HP):
                            g = 4 * c + h
                            ins = mm(bank[b0 + c][:, P * h:P * (h + 1)], lhs[:, g, :], AR[:, g].rearrange("p s i -> p (s i)"), start=True, stop=True)
                        ins.then_inc(mp.sem, mp.step(f"{s}_{c}"))
                for s, src, b0, wait in (("tb", bP, 0, "g1_"), ("tk", kP, 4, "g2_"), ("tv", vP, 0, "tb")):
                    for c in range(NC):
                        pe.wait_ge(mv.sem, mv.at(l, f"{wait}{c}"))
                        for h in range(HP):
                            ins = turn(bank[b0 + c][:, P * h:P * (h + 1)], src[:, 4 * c + h, :])
                        ins.then_inc(mp.sem, mp.step(f"{s}{c}"))
                pe.wait_ge(ma.sem, ma.at(l, "pP"))
                pe.wait_ge(ma.sem, ma.at(l, "lP"))
                pe.wait_ge(mv.sem, mv.at(l, f"vc{NC - 1}"))
                for b in range(2):
                    for j in range(8):
                        mm(bank[b][:, 64 * j:64 * (j + 1)], pP[:, 8 * b + j, :], con("eyes"), start=j == 0, stop=False, skip_group_check=True)
                    ins = mm(bank[2 + b][:], ident, pC[:, 8 * b:8 * b + 8, :].rearrange("p g i -> p (g i)"), start=True, stop=False, skip_group_check=True)
                    ins.then_inc(mp.sem, mp.step(f"ti{b}"))
                for k in LV:
                    for b in range(2):
                        pe.wait_ge(mv.sem, mv.at(l, f"t0_{b}" if k == 1 else f"tc{k - 1}_{b}"))
                        for j in range(8):
                            g = 8 * b + j
                            ins = mm(bank[4 + b][:, 64 * j:64 * (j + 1)], lP[:, g, :], tC[:, g, :], start=True, stop=True)
                        ins.then_inc(mp.sem, mp.step(f"u{k}_{b}"))
                    for b in range(2):
                        last = k == LEVELS
                        if not last:
                            pe.wait_ge(mv.sem, mv.at(l, f"um{k}_{b}"))
                            if k > 1:
                                pe.wait_ge(ma.sem, ma.at(l, f"ps{k - 1}_{b}"))
                            for j in range(8):
                                g = 8 * b + j
                                ins = mm(bank[b][:, 64 * j:64 * (j + 1)], pP[:, g, :], uC[:, g, :], start=False, stop=k == LEVELS - 1, skip_group_check=True)
                            ins.then_inc(mp.sem, mp.step(f"t{k}_{b}"))
                        pe.wait_ge(ma.sem, ma.at(l, f"us{k}_{b}"))
                        if k > 1:
                            pe.wait_ge(mv.sem, mv.at(l, f"pc{k - 1}_{b}"))
                        for j in range(8):
                            g = 8 * b + j
                            ins = mm(bank[2 + b][:, 64 * j:64 * (j + 1)], uP[:, g, :], pC[:, g, :], start=False, stop=last, skip_group_check=True)
                        ins.then_inc(mp.sem, mp.step(f"p{k}_{b}"))
                pe.wait_ge(mv.sem, mv.at(l, "rope1"))
                pe.wait_ge(ma.sem, ma.at(l, "ps5_1"))
                for i in range(8):
                    s, t, hq = i // 4, (i // 2) % 2, i % 2
                    for j in range(4):
                        ins = turn(bank[i][0:QK, P * j:P * (j + 1)], qk[:, t, s, 4 * hq + j, :])
                    ins.then_inc(mp.sem, mp.step(f"qkT{i}"))
                pe.wait_ge(mv.sem, mv.at(l, "qkT7"))
                for b in range(2):
                    for j in range(4):
                        h = 4 * b + j
                        mm(bank[3 * b][:, P * j:P * (j + 1)], qkT[0][0:QK, h, 0:P], qkT[1][0:QK, h, 0:P], start=True, stop=True)
                        ins = mm(bank[3 * b + 1 + j // 2][:, 256 * (j % 2):256 * (j % 2) + 256], qkT[0][0:QK, h, P:SEQ], qkT[1][0:QK, h, :],
                                 start=True, stop=True)
                    ins.then_inc(mp.sem, mp.step(f"sc{b}"))
                for b in range(2):
                    pe.wait_ge(ma.sem, ma.at(l, f"ex{b}"))
                    if b:
                        pe.wait_ge(mv.sem, mv.at(l, "pt0"))
                    for m, bk in enumerate((6, 7, 0)):
                        for j in range(4):
                            ins = turn(bank[bk][:, P * j:P * (j + 1)], prob[:, j, P * m:P * (m + 1)])
                    ins.then_inc(mp.sem, mp.step(f"pt{b}"))
                    pe.wait_ge(mv.sem, mv.at(l, f"pt{b}"))
                    for j in range(4):
                        h = 4 * b + j
                        s = slice(DV * h, DV * (h + 1))
                        mm(bank[1][:, s], probT[:, 0, P * j:P * (j + 1)], V[:, 0, h, :], start=True, stop=True)
                        mm(bank[2][:, s], probT[:, 1, P * j:P * (j + 1)], V[:, 0, h, :], start=True, stop=False)
                        ins = mm(bank[2][:, s], probT[:, 2, P * j:P * (j + 1)], V[:, 1, h, :], start=False, stop=True)
                    ins.then_inc(mp.sem, mp.step(f"pv{b}"))
                pe.wait_ge(mv.sem, mv.at(l, "yn"))
                for f in range(4):
                    for t in range(2):
                        ins = turn(bank[3 + f // 2][:, 256 * (f % 2) + P * t:256 * (f % 2) + P * (t + 1)], ymla[:, t, P * f:P * (f + 1)])
                ins.then_inc(mp.sem, mp.step("yT"))
                pe.wait_ge(ma.sem, ma.at(l, "ak"))
                pe.wait_ge(mv.sem, mv.at(l, "yg"))
                for c in range(NC):
                    x_b, u_b, s_b, y_b = bank[4 + c % 2], bank[6 + c % 2], bank[2 + c % 2], bank[c // 2]
                    for h in range(HP):
                        s = slice(64 * h, 64 * (h + 1))
                        ins = mm(x_b[:, s], lP[:, 4 * c + h, :], vC[:, 4 * c + h, :], start=h == 0, stop=c == 0, skip_group_check=True)
                    if c:
                        pe.wait_ge(mv.sem, mv.at(l, f"s{c - 1}"))
                        for h in range(HP):
                            ins = mm(x_b[:, 64 * h:64 * (h + 1)], aP[:, 4 * c + h, :], rec[:, 2 + c % 2, h, :], start=False, stop=True, skip_group_check=True)
                    ins.then_inc(mp.sem, mp.step(f"x{c}"))
                    keep_clock(4 + (c + 1) % 2, 3)
                    pe.wait_ge(mv.sem, mv.at(l, f"x{c}"))
                    for h in range(HP):
                        ins = mm(u_b[:, 64 * h:64 * (h + 1)], pP[:, 4 * c + h, :], rec[:, 0, h, :], start=True, stop=True)
                    ins.then_inc(mp.sem, mp.step(f"u{c}"))
                    keep_clock(4 + (c + 1) % 2, 3)
                    pe.wait_ge(mv.sem, mv.at(l, f"u{c}"))
                    if c < NC - 1:
                        for h in range(HP):
                            g, o = 4 * c + h, s_b[:, 64 * h:64 * (h + 1)]
                            mm(o, kP[:, g, :], vC[:, g, :], start=True, stop=False)
                            ins = mm(o, bP[:, g, :], rec[:, 1, h, :], start=False, stop=True)
                        ins.then_inc(mp.sem, mp.step(f"s{c}"))
                    pe.wait_ge(ma.sem, ma.at(l, f"ub{c}"))
                    if c:
                        pe.wait_ge(ma.sem, ma.at(l, f"sb{c - 1}"))
                    for h in range(HP):
                        g, o = 4 * c + h, y_b[:, 256 * (c % 2) + 64 * h:256 * (c % 2) + 64 * (h + 1)]
                        mm(o, vP[:, g, :], M2[:, g, 1, :], start=True, stop=False)
                        ins = mm(o, uP[:, 4 * (c % 2) + h, :], M1[:, g, 1, :], start=False, stop=c == 0)
                        if c:
                            ins = mm(o, uP[:, 8 + 4 * (c % 2) + h, :], AR[:, g, 1, :], start=False, stop=True)
                    ins.then_inc(mp.sem, mp.step(f"y{c}"))
                pe.wait_ge(mv.sem, mv.at(l, "y"))
                for b in range(2):
                    ins = mm(bank[4 + b][:], con("meanbd"), yT[:, 512 * b:512 * (b + 1)], start=True, stop=True)
                ins.then_inc(mp.sem, mp.step("mean"))

                def clear(b0):
                    for i in range(4):
                        mm(bank[b0 + i][:], zeros[0:1, 0:P], zeros[0:1, :], start=True, stop=False, skip_group_check=True)

                def output(k):
                    b = blk(f"out{k}")
                    if k >= 4:
                        pe.wait_ge(mv.sem, mv.at(l, f"ylo{k}"))
                    for t in range(DT):
                        s = slice(P * t, P * (t + 1))
                        ins = three(bank[4 * (k // 4) + t // 2][:, SEQ * (t % 2):SEQ * (t % 2 + 1)], whi[:, b.slot, s], wlo[:, b.slot, s],
                                    xhi[:, k, :], xlo[:, k, :], False, k % 4 == 3, skip_group_check=True)
                    ins.then_inc(w_used, 1)

                pe.wait_ge(mv.sem, mv.at(l, "s2"))
                clear(0)
                output(0)
                pe.wait_ge(ma.sem, ma.at(l, "gsq"))
                for j in range(8):
                    ins = mm(bank[6][:, 2 * j:2 * j + 2], ysc[:, P * j:P * (j + 1)], con("meanbd")[:, 0:P:64], start=True, stop=True)
                ins.then_inc(mp.sem, mp.step("var"))
                output(1)
                pe.wait_ge(mv.sem, mv.at(l, "gvw"))
                spread_heads(4).then_inc(mp.sem, mp.step("gvb"))
                output(2)
                output(3)
                pe.wait_ge(mv.sem, mv.at(l, "gy"))
                clear(4)
                output(4)
                pe.wait_ge(ma.sem, ma.at(l, "rsq"))
                pe.wait_ge(mv.sem, mv.at(l, "resm0"))
                for t in range(2):
                    for j in range(4):
                        ins = mm(bank[0][:, t:t + 1], ysc[:, SEQ * j + P * t:SEQ * j + P * (t + 1)], one, start=j == 0, stop=j == 3)
                ins.then_inc(mp.sem, mp.step("rms"))
                output(5)
                pe.wait_ge(mv.sem, mv.at(l, "rms_y2"))
                pe.wait_ge(mv.sem, mv.at(l, "resm1"))
                for t in range(2):
                    ins = spread_rows(bank[1][:, P * t:P * (t + 1)], t)
                ins.then_inc(mp.sem, mp.step("rmsb"))
                output(6)
                output(7)

            pe.sem_inc(w_used, RING)
            pe.wait_ge(once, 1)
            keep_clock(7, 12)
            pe.wait_ge(const_in, 16)
            pe.wait_ge(x_in, 16)
            for i in range(4):
                for d in range(2):
                    for t in range(2):
                        ins = turn(bank[i][:, SEQ * d + P * t:SEQ * d + P * (t + 1)], xtok[:, t, P * (2 * i + d):P * (2 * i + d + 1)])
                ins.then_inc(x_turned, 1)

            with pe.Fori(0, DEPTH) as l:
                pe.wait_ge(rows_in, l * ROWS_IN + ROWS_IN)
                pe.wait_ge(x_ready, quarter(l * 3, 3))
                turn(bank[5][:, 0:NROWS], rows[:]).then_inc(mp.sem, mp.step("prm"))
                ffn(l, 0)
                mixing(l)
                ffn(l, 1)
            pe.wait_ge(x_ready, quarter(DEPTH * 3, 3))
            for t in range(2):
                for q in range(2):
                    for d in range(4):
                        ins = turn(bank[2 * t + q][:, P * d:P * (d + 1)], xT[:, 4 * q + d, P * t:P * (t + 1)])
                    ins.then_inc(out_turned, 1)


_VECTORS = ['ffn1_norm', 'mix_norm', 'q_lat_norm', 'kv_lat_norm', 'q_norm', 'k_norm', 'shift_mu', 'w0', 'a0', 'k_k', 'k_a',
            'r_k', 'gn_gain', 'gn_bias', 'out_norm_mla', 'out_norm_rwkv', 'ffn2_norm']
_WEIGHTS = ['ffn1_w_gate', 'ffn1_w_up', 'ffn1_w_down', 'w_in', 'w_q_up', 'w_kv_up', 'w2', 'a2', 'g2', 'w_out',
            'ffn2_w_gate', 'ffn2_w_up', 'ffn2_w_down']


def kernel(**inputs):
    import concourse.bacc as _bacc
    from concourse.bass_utils import run_bass_kernel_spmd as _run

    nc = _bacc.Bacc("TRN2", target_bir_lowering=False, num_devices=1)
    arrays, aps = {}, {}
    for name in ['x'] + _VECTORS + _WEIGHTS:
        a = np.ascontiguousarray(inputs[name])
        arrays[f"in_{name}_dram"] = a
        aps[name] = nc.dram_tensor(f"in_{name}_dram", a.shape, mybir.dt.from_np(a.dtype), kind="ExternalInput").ap()
    arrays["in_consts_dram"] = shape_constants()
    consts = nc.dram_tensor("in_consts_dram", (P, NCONST), F32, kind="ExternalInput").ap()
    out = nc.dram_tensor("out_0_dram", (1, SEQ, D), F32, kind="ExternalOutput").ap()
    build(nc, aps['x'], {k: aps[k] for k in _VECTORS}, {k: aps[k] for k in _WEIGHTS}, consts, out)
    r = _run(nc, [arrays], core_ids=[0])
    return r.results[0]["out_0_dram"]
```

```python
from contextlib import ExitStack

import numpy as np

import concourse.bass as bass
from concourse import mybir

F32 = mybir.dt.float32
F32R = mybir.dt.float32r
BF16 = mybir.dt.bfloat16
I32 = mybir.dt.int32
ALU = mybir.AluOpType
ACT = mybir.ActivationFunctionType
AX_X = mybir.AxisListType.X

P = 128
SEQ, D, DEPTH, F = 256, 1024, 2, 2816
DT, FT = D // P, F // P
H, NOPE, ROPE, DV = 8, 64, 32, 64
QK = NOPE + ROPE
QL, KVL = 256, 128
RW, HEAD, C = 512, 64, 64
NC = SEQ // C
HP = RW // P
G = NC * HP
MLA_IN = QL + KVL + ROPE
O_R = MLA_IN
O_WL = O_R + RW
O_K = O_WL + 64
O_V = O_K + RW
O_AL = O_V + RW
O_GL = O_AL + 64
GLORA = 160
EPS, GN_EPS = 1e-6, 64e-5
DECAY = float(np.exp(-0.5))
SCALE = float(QK) ** -0.5
LEVELS = 5
NEG = -1e30

ROWS = [("ffn1_norm", "ffn1_norm", 0, 8), ("mix_norm", "mix_norm", 0, 8), ("ffn2_norm", "ffn2_norm", 0, 8),
        ("q_lat_norm", "q_lat_norm", 0, 2), ("kv_lat_norm", "kv_lat_norm", 0, 1),
        ("mu_r", "shift_mu", 0, 4), ("mu_k", "shift_mu", O_K - MLA_IN, 4), ("mu_v", "shift_mu", O_V - MLA_IN, 4),
        ("mu_g", "shift_mu", O_GL - MLA_IN, 1), ("mu_g2", "shift_mu", O_GL - MLA_IN + 32, 1),
        ("mu_wa", None, 0, 1),
        ("w0", "w0", 0, 4), ("a0", "a0", 0, 4), ("k_k", "k_k", 0, 4), ("k_a", "k_a", 0, 4), ("r_k", "r_k", 0, 4),
        ("gn_gain", "gn_gain", 0, 4), ("gn_bias", "gn_bias", 0, 4),
        ("out_norm_mla", "out_norm_mla", 0, 4), ("out_norm_rwkv", "out_norm_rwkv", 0, 4)]
ROW = {}
_n = 0
for _name, _, _, _k in ROWS:
    ROW[_name] = _n
    _n += _k
NROWS = _n
MU_N = ROW["mu_wa"] + 1 - ROW["mu_r"]

CONST = {}
_n = 0
for _name, _k in [("ident", 128), ("ones", 128), ("onesbd", 128), ("meanbd", 128), ("eyes", 64), ("upper", 128),
                  ("level", LEVELS * 64), ("level1T", 64), ("reset", 256), ("cos", 32), ("sin", 32)]:
    CONST[_name] = (_n, _n + _k)
    _n += _k
NCONST = _n


def shape_constants():
    c = np.zeros((P, NCONST), np.float32)

    def put(name, a):
        lo, hi = CONST[name]
        c[:, lo:hi] = np.asarray(a, np.float32).reshape(P, hi - lo)

    i = np.arange(P)
    row, col = (i % C)[:, None], np.arange(C)[None, :]
    same = (i[:, None] // C) == (i[None, :] // C)
    put("ident", np.eye(P))
    put("ones", np.ones((P, P)))
    put("onesbd", same)
    put("meanbd", same / HEAD)
    put("eyes", row == col)
    put("upper", np.concatenate([row < col, row <= col], 1))
    lev = []
    for k in range(1, LEVELS + 1):
        s = 1 << k
        lev.append((row // (2 * s) == col // (2 * s)) & (row // s > col // s))
    put("level", np.concatenate(lev, 1))
    put("level1T", (row // 2 == col // 2) & (row < col))
    put("reset", np.broadcast_to((np.arange(SEQ) % C != 0)[None], (P, SEQ)))
    inv = np.float32(10000.0) ** (-np.arange(0, ROPE, 2, dtype=np.float32) / np.float32(ROPE))
    ang = np.arange(SEQ, dtype=np.float32)[:, None] * inv[None, :].astype(np.float32)
    put("cos", np.cos(ang).reshape(2, P, 16).transpose(1, 0, 2))
    put("sin", np.sin(ang).reshape(2, P, 16).transpose(1, 0, 2))
    return c


class Steps:

    def __init__(self, sem, names):
        self.sem, self.names, self.n = sem, names, 0
        assert len(set(names)) == len(names)

    def at(self, rnd, name):
        return rnd * len(self.names) + (self.names.index(name) + 1)

    def step(self, name):
        assert self.names[self.n % len(self.names)] == name, (name, self.names[self.n % len(self.names)])
        self.n += 1
        return 1


RW_TILES = ["wa"] + [f"r{i}" for i in range(4)] + [f"k{i}" for i in range(4)] + [f"v{i}" for i in range(4)] + ["g0", "g1"]
LAT_TILES = ["q0", "q1", "kv"]
MIX_BLOCKS = RW_TILES + LAT_TILES + ["pe", "kvup", "qup0", "qup1"] + [f"out{i}" for i in range(8)]
FFN_BLOCKS = 3 * FT
LAYER_BLOCKS = 2 * FFN_BLOCKS + len(MIX_BLOCKS)
RING = 3
assert FFN_BLOCKS % RING == 0 and len(MIX_BLOCKS) % RING == 0


class Block:

    def __init__(self, number, fills, slot):
        self.number, self.fills, self.slot = number, fills, slot


def ffn_block(l, which, kind, f):
    first = (FFN_BLOCKS + len(MIX_BLOCKS)) * which
    base, rounds = l * LAYER_BLOCKS + first, l * (LAYER_BLOCKS // RING) + first // RING
    if kind == "gate":
        if isinstance(f, int) and f == 0:
            return Block(base, rounds + 1, 0)
        return Block(base + (f * 3 - 1), rounds + f, 2)
    if kind == "up":
        if isinstance(f, int) and f == 0:
            return Block(base + 1, rounds + 1, 1)
        return Block(base + f * 3, rounds + (f + 1), 0)
    if isinstance(f, int) and f == FT - 1:
        return Block(base + (FFN_BLOCKS - 1), rounds + FT, 2)
    return Block(base + (f * 3 + 4), rounds + (f + 2), 1)


def mix_block(l, name):
    j = MIX_BLOCKS.index(name)
    return Block(l * LAYER_BLOCKS + (FFN_BLOCKS + j),
                 l * (LAYER_BLOCKS // RING) + (FFN_BLOCKS // RING + j // RING + 1), j % RING)


def block_width(name):
    return 768 if name[:3] == "qup" else 1024


def ffn_order(eng, gate, up, down):
    gate(0, 0), up(0, 0), gate(1, 1), up(1, 1), down(0, 0)
    with eng.Fori(0, FT // 2 - 1) as i:
        f = i * 2
        gate(f + 2, 0), up(f + 2, 0), down(f + 1, 1)
        gate(f + 3, 1), up(f + 3, 1), down(f + 2, 0)
    down(FT - 1, (FT - 1) % 2)


LO, UP = slice(0, 64), slice(64, 128)


def newton(prefix):
    return [f"{prefix}_{s}" for s in ("shift", "seed") + tuple(f"{x}{i}" for i in range(3) for x in ("sq", "err", "y"))]


NORM_V = [f"lo{i}" for i in range(4)] + ["ms"] + newton("norm") + ["rcol", "row"]
NORM_A = [f"hi{i}" for i in range(4)] + [f"sq{i}" for i in range(4)]
LV = range(1, LEVELS + 1)


def shift_steps():
    steps = []
    for i, t in enumerate(RW_TILES):
        steps += ([f"pr_{t}"] if i == 0 else []) + ([f"pr_{RW_TILES[i + 1]}"] if i + 1 < len(RW_TILES) else []) + [f"sh_{t}"]
        steps += {"k3": ["kk0"], "v0": ["lw"], "v2": ["lc"]}.get(t, [])
    return steps


QK_STEPS = [["qkms"] + newton("qk"), ["qkn"], ["qkg"], ["rope_m0", "rope0"], ["rope_m1", "rope1"]]

Y_STEPS = [["yms"] + newton("ym") + ["yn"], ["ye0", "yg0"], ["yg1"], ["ylo0"]]

MIX_V = (["prm1", "prm", "omm", "half_wa", "one_k"] + NORM_V + shift_steps() + ["gs", "kkms"] + newton("kk") + ["kkw", "lat_copy", "a", "kk"]
         + ["kf", "kmod", "a_c", "lat_ms"] + newton("lat") + ["k_c", "lat_n", "lat_lo", "b_c"]
         + [f"kn{j}" for j in range(4)] + ["bonus", "kpe"] + [f"qe{j}" for j in range(4)]
         + [f"g1_{c}" for c in range(NC)] + [f"g2_{c}" for c in range(NC)]
         + [f"tb{c}" for c in range(NC)] + ["p1a", "p1", "qkss"]
         + ["t0_0", "t0_1"]
         + [s for k in LV for s in [f"um{k}_0", f"um{k}_1"] + QK_STEPS[k - 1]
            + ([f"tc{k}_0", f"pc{k}_0", f"tc{k}_1", f"pc{k}_1"] if k < LEVELS else [])]
         + [f"qkT{i}" for i in range(8)]
         + ["mask0", "max0", "nmax0", "mask1", "max1", "nmax1", "pt0", "pt1"]
         + ["rinv", "o"]
         + [s for c in range(NC) for s in ([f"x{c}", f"u{c}"] + ([f"sa{c}"] if 0 < c < NC - 1 else [])
                                           + ([f"s{c}"] if c < NC - 1 else []) + Y_STEPS[c])]
         + ["ye1", "yc", "gv"] + newton("gv") + ["gvw"] + ["gy", "gg", "gb", "gm"] + [f"ylo{4 + j}" for j in range(HP)]
         + [f"resm{i}" for i in range(4)] + ["rms"] + newton("rms") + ["rmsrow"] + [f"resr{i}" for i in range(4)])
MIX_A = (NORM_A + [f"mu_{t}" for t in RW_TILES[:5]] + ["tanh_w"] + [f"mu_{t}" for t in RW_TILES[5:9]]
         + ["tz", "ta", "kksq"] + [f"mu_{t}" for t in RW_TILES[9:]] + ["gs0", "E", "einv", "lat_sq"]
         + ["pe_T", "gT", "pe", "aP", "lat_hi", "kP", "bP", "vP"] + [f"v{j}" for j in range(4)] + ["qksq"]
         + ["lP"] + [f"tk{c}" for c in range(NC)] + [f"tv{c}" for c in range(NC)] + ["pP"]
         + [f"{s}{k}_{b}" for k in LV for s in ("us", "ps") for b in range(2)]
         + ["ak", "ex0", "ex1", "ysq"] + [s for c in range(NC) for s in ([f"ub{c}"] + ([f"sb{c}"] if c < NC - 1 else []))] + ["yhi0"]
         + ["gsq"] + [f"yhi{4 + j}" for j in range(HP)] + ["rsq"])
MIX_P = (["prm1", "prm", "ss", "rb", "z", "a", "kkss", "kkb", "latss", "gup", "peT", "latb", "bsum"]
         + [f"g1_{c}" for c in range(NC)] + [f"g2_{c}" for c in range(NC)]
         + [f"tb{c}" for c in range(NC)] + [f"tk{c}" for c in range(NC)] + [f"tv{c}" for c in range(NC)] + ["ti0", "ti1"]
         + [s for k in LV for s in [f"u{k}_0", f"u{k}_1"] + [x for b in range(2) for x in
                                                           ([f"t{k}_{b}"] if k < LEVELS else []) + [f"p{k}_{b}"]]]
         + [f"qkT{i}" for i in range(8)] + ["sc0", "sc1", "pt0", "pv0", "pt1", "pv1"]
         + [s for c in range(NC) for s in [f"x{c}", f"u{c}"] + ([f"s{c}"] if c < NC - 1 else []) + [f"y{c}"]
            + {1: ["yT0"], 2: ["yT1"]}.get(c, [])]
         + ["mean", "var", "gvb", "rms", "rmsb", "sum0", "sum1", "sum2"])


def mu_col(tile):
    return {"wa": ("mu_wa", 0), "g0": ("mu_g", 0), "g1": ("mu_g2", 0)}.get(tile) or (f"mu_{tile[0]}", int(tile[1]))


def build(nc, x, par, w, consts, out):
    with ExitStack() as ctx:
        def sb(name, shape, dt=F32):
            return ctx.enter_context(nc.sbuf_tensor(name, shape, dt))

        def sem(name):
            return ctx.enter_context(nc.semaphore(name))

        bank = [ctx.enter_context(nc.psum_tensor(f"bank{i}", [P, 512], F32)) for i in range(8)]

        cst = sb("cst", [P, NCONST])
        rows1 = sb("rows1", [8, P])
        rows = sb("rows", [NROWS - 8, P])
        prm = sb("prm", [P, NROWS])
        omm = sb("omm", [P, MU_N])
        half = sb("half", [P, 12])
        qkgain = sb("qkgain", [P, 2, QK])
        xT = sb("xT", [P, DT, SEQ])
        xhi = sb("xhi", [P, DT, SEQ], F32R)
        xlo = sb("xlo", [P, DT, SEQ], F32R)
        raw = sb("raw", [P, RING, 1024])
        whi = sb("whi", [P, RING, 1024], F32R)
        wlo = sb("wlo", [P, RING, 1024], F32R)
        hhi = sb("hhi", [P, 2, SEQ], F32R)
        hlo = sb("hlo", [P, 2, SEQ], F32R)
        root = sb("root", [P, 3, 32])
        R = sb("R", [P, SEQ])
        rcol = sb("rcol", [P, 2])
        scaled = sb("scaled", [P, 2, SEQ])
        zeros = sb("zeros", [P, 512], BF16)
        E = sb("E", [P, G, C + 1])
        stat = sb("stat", [P, 256])
        shift = sb("shift", [P, 2, SEQ + 1])
        lora = sb("lora", [P, 3, SEQ])
        kpe = sb("kpe", [P, 2, ROPE])
        work = sb("work", [P, 16, 1024])
        pairs = sb("pairs", [P, 7, G, P])

        def unit(i, n=1):
            return work[:, i:i + n, :].rearrange("p u n -> p (u n)")

        def stacks(i):
            return unit(i).rearrange("p (g i) -> p g i", g=G)

        def double(i):
            return unit(i, 2).rearrange("p (g s i) -> p g s i", g=G, s=2)

        rT, kT, vT, zl, ta, lc, kk, sc, einv, kmod, gT, bonus = (unit(i) for i in range(12))
        w2a2 = unit(10)[:, 0:RW]
        g2a, g2b = unit(11)[:, 0:RW], unit(11)[:, RW:2 * RW]
        AR = double(12)
        bC, kC = stacks(14), stacks(15)
        def two(i, j):
            return work[:, i:j + 1:j - i, :].rearrange("p s (g i) -> p g s i", g=G)

        M1, M2 = two(8, 14), two(9, 15)
        vC, tC, pC, uC = stacks(2), stacks(0), stacks(7), stacks(1)
        rec = unit(3).rearrange("p (s h i) -> p s h i", s=4, h=HP)
        yT, yN, ysc, scrap = unit(4), unit(5), unit(8), unit(7)
        parts = unit(7, 2)
        aP, bP, kP, vP, lP, pP, uP = (pairs[:, i] for i in range(7))
        lat = unit(3)[:, 0:768].rearrange("p (t n) -> p t n", t=3)
        lat_sq = unit(5)[:, 0:768].rearrange("p (t n) -> p t n", t=3)
        qk = unit(3, 3).rearrange("p (t s h d) -> p t s h d", t=2, s=2, h=H)
        qk_sq = unit(0, 3)
        rope = [lora[:, 0, :], lora[:, 1, :], lora[:, 2, :], scaled[:, 0, :]]
        qkT = [unit(u, 2).rearrange("p (h n) -> p h n", h=H) for u in (7, 0)]
        V = unit(6).rearrange("p (t h d) -> p t h d", t=2, h=H)
        prob = unit(3, 3)[:, 0:1536].rearrange("p (h k) -> p h k", h=4)
        probT = unit(3, 3)[:, 1536:3072].rearrange("p (m n) -> p m n", m=3)
        ymla = unit(9).rearrange("p (t n) -> p t n", t=2)
        ymT = unit(6).rearrange("p (f n) -> p f n", f=4)
        xsq = unit(3, 2).rearrange("p (t n) -> p t n", t=DT)
        ft = unit(5).rearrange("p (s n) -> p s n", n=SEQ)
        gs = unit(6)[:, 0:512].rearrange("p (s n) -> p s n", n=SEQ)
        xtok = unit(0, 2).rearrange("p (b n) -> p b n", b=2)

        def con(name):
            lo, hi = CONST[name]
            return cst[:, lo:hi]

        ident = con("ident")

        def col(name, i=0):
            return prm[:, ROW[name] + i:ROW[name] + i + 1]

        const_in, x_in, rows1_in, rows_in, small_in, half_in = (sem(s) for s in ("const_in", "x_in", "rows1_in",
                                                                                 "rows_in", "small_in",
                                                                                 "half_in"))
        raw_in = [sem(f"raw_in{i}") for i in range(RING)]
        hi_ready = sem("hi_ready")
        lo_ready = sem("lo_ready")
        w_used = sem("w_used")
        x_ready = sem("x_ready")
        tanh_done, hhi_done, hlo_done = sem("tanh_done"), sem("hhi_done"), sem("hlo_done")
        h_steps = sem("h_steps")
        once = sem("once")
        x_turned, out_turned, out_copied, out_done = (sem(s) for s in ("x_turned", "out_turned", "out_copied",
                                                                       "out_done"))
        ffn_dve, ffn_act, ffn_pe = Steps(sem("ffn_dve"), NORM_V), Steps(sem("ffn_act"),
                                                                        NORM_A), Steps(sem("ffn_pe"),
                                                                                       ["ss", "rb", "sum0",
                                                                                        "sum1", "sum2"])
        mix_dve, mix_act, mix_pe = Steps(sem("mix_dve"), MIX_V), Steps(sem("mix_act"),
                                                                       MIX_A), Steps(sem("mix_pe"), MIX_P)
        mix_pool = Steps(sem("mix_pool"), ["kk2", "r_c", "rrk", "rk", "vC"])
        ONCE = 5

        def quarter(phase, i):
            return phase * 4 + (i + 1)

        def mixed(l, name):
            return mix_block(l, name).number + (RING + 1)

        def x_quarter(i):
            return xT[:, 2 * i:2 * i + 2, :].rearrange("p t n -> p (t n)")

        def tile_done(l, which, kind, f):
            return ffn_block(l, which, kind, f).number + (RING + 1)

        block = ctx.enter_context(nc.Block())

        @block.gpsimd
        def _(pool):
            pool.memset(zeros[:], 0.0).then_inc(once, 1)
            pool.memset(shift[:], 0.0).then_inc(once, 1)
            pool.memset(E[:, :, 0:1], 1.0).then_inc(once, 1)
            pool.memset(stat[:], 0.0).then_inc(once, 1)
            pool.memset(pairs[:].rearrange("p s g n -> p (s g n)"), 0.0).then_inc(once, 1)

            with pool.Fori(0, DEPTH) as l:
                pool.wait_ge(mix_dve.sem, mix_dve.at(l, "kmod"))
                nc.gpsimd.tensor_tensor(sc, ta, kk, ALU.mult).then_inc(mix_pool.sem, mix_pool.step("kk2"))
                pool.wait_ge(mix_act.sem, mix_act.at(l, "E"))
                E_c = E[:].rearrange("p (h c) i -> p c h i", h=HP)
                for c in range(NC):
                    ins = nc.gpsimd.tensor_tensor(AR[:, :, 1, :].rearrange("p (c h) i -> p c h i", h=HP)[:, c],
                                                  rT.rearrange("p (h c i) -> p c h i", h=HP, c=NC)[:, c],
                                                  E_c[:, c, :, 1:C + 1], ALU.mult)
                ins.then_inc(mix_pool.sem, mix_pool.step("r_c"))
                pool.wait_ge(mix_pool.sem, mix_pool.at(l, "r_c"))
                r_h = rT.rearrange("p (h n) -> p h n", h=HP)
                nc.gpsimd.tensor_tensor(r_h, r_h,
                                        prm[:,
                                            ROW["r_k"]:ROW["r_k"] + HP].unsqueeze(2).to_broadcast((P, HP, SEQ)),
                                        ALU.mult).then_inc(mix_pool.sem, mix_pool.step("rrk"))
                pool.wait_ge(mix_pool.sem, mix_pool.at(l, "rrk"))
                nc.gpsimd.tensor_tensor(rT, rT, kmod, ALU.mult).then_inc(mix_pool.sem, mix_pool.step("rk"))
                pool.wait_ge(mix_act.sem, mix_act.at(l, "tv3"))
                pool.wait_ge(mix_dve.sem, mix_dve.at(l, "qkss"))
                nc.gpsimd.tensor_tensor(vC[LO], vP[LO, :, 0:64], vP[LO, :, 64:128], ALU.add)
                nc.gpsimd.tensor_tensor(vC[UP], vP[UP, :, 64:128], vP[UP, :, 0:64],
                                        ALU.add).then_inc(mix_pool.sem, mix_pool.step("vC"))
                for i in (1, 3):
                    pool.wait_ge(mix_dve.sem, mix_dve.at(l, f"resr{i}"))
                    pool.wait_ge(x_ready, quarter(l * 3 + 2, i - 1))
                    part = parts[:, 512 * i:512 * (i + 1)]
                    nc.gpsimd.tensor_tensor(x_quarter(i), x_quarter(i), part, ALU.add).then_inc(x_ready, 1)

        @block.sync
        def _(sp):
            sp.dma_start(cst[:], consts).then_inc(const_in, 16)
            sp.dma_start(xtok, x.rearrange("o (b p) n -> p (o b) n", p=P)).then_inc(x_in, 16)

            def load(b, dst, src):
                sp.wait_ge(lo_ready, b.number + 1)
                sp.dma_start(dst, src).then_inc(raw_in[b.slot], 16)

            def columns(src, l, first, n=P):
                return src[bass.ds(l, 1), :, bass.ds(first, n)].rearrange("a (t p) n -> p (a t) n", p=P)

            def in_slot(b, n=P):
                return raw[:, b.slot, 0:DT * n].rearrange("p (t n) -> p t n", t=DT)

            def parameter_rows(l):
                for name, src, first, k in ROWS[1:]:
                    r0 = ROW[name] - 8
                    if src is None:
                        for j, o in enumerate((O_WL - MLA_IN, O_AL - MLA_IN)):
                            sp.dma_start(rows[r0:r0 + 1, 64 * j:64 * j + 64],
                                         par["shift_mu"][bass.ds(l, 1), o:o + 64]).then_inc(rows_in, 16)
                    else:
                        v = par[src]
                        if len(v.shape) == 3:
                            v = v.rearrange("a h n -> a (h n)")
                        sp.dma_start(rows[r0:r0 + k, :],
                                     v[bass.ds(l, 1), first:first + P * k].rearrange("a (k n) -> (a k) n",
                                                                                     n=P)).then_inc(rows_in, 16)

            def ffn_loads(l, which):
                wg, wu, wd = (w[f"ffn{which + 1}_w_{s}"] for s in ("gate", "up", "down"))

                def gate(f, parity):
                    b = ffn_block(l, which, "gate", f)
                    load(b, in_slot(b), columns(wg, l, f * P))
                    if isinstance(f, int) and f == 1 and which == 0:
                        parameter_rows(l)

                def up(f, parity):
                    b = ffn_block(l, which, "up", f)
                    load(b, in_slot(b), columns(wu, l, f * P))

                def down(f, parity):
                    b = ffn_block(l, which, "down", f)
                    load(b, raw[:, b.slot, :],
                         wd[bass.ds(l, 1), bass.ds(f * P, P), :].rearrange("a p n -> p (a n)"))

                ffn_order(sp, gate, up, down)

            def flat(name, l, lo=None, hi=None):
                v = w[name][bass.ds(l, 1)] if lo is None else w[name][bass.ds(l, 1), lo:hi]
                return v.rearrange("a p n -> p (a n)")

            with sp.Fori(0, DEPTH) as l:
                sp.dma_start(rows1[:],
                             par["ffn1_norm"][bass.ds(l, 1), :].rearrange("a (k n) -> (a k) n",
                                                                          n=P)).then_inc(rows1_in, 16)
                ffn_loads(l, 0)
                first_col = {"g0": O_GL, "g1": O_GL + GLORA - P, "q0": 0, "q1": P, "kv": QL}
                for i in range(4):
                    first_col.update({f"r{i}": O_R + P * i, f"k{i}": O_K + P * i, f"v{i}": O_V + P * i})
                for name in MIX_BLOCKS:
                    b = mix_block(l, name)
                    if name == "wa":
                        load(b, in_slot(b)[:, :, 0:64], columns(w["w_in"], l, O_WL, 64))
                        sp.dma_start(in_slot(b)[:, :, 64:128],
                                     columns(w["w_in"], l, O_AL, 64)).then_inc(half_in, 16)
                        sp.dma_start(w2a2[LO, :], flat("w2", l)).then_inc(small_in, 16)
                        sp.dma_start(w2a2[UP, :], flat("a2", l)).then_inc(small_in, 16)
                        sp.dma_start(g2a, flat("g2", l, 0, P)).then_inc(small_in, 16)
                        sp.dma_start(g2b[96:128, :], flat("g2", l, P, GLORA)).then_inc(small_in, 16)
                        for i, nm in enumerate(("q_norm", "k_norm")):
                            sp.dma_start(qkgain[:, i, :],
                                         par[nm][bass.ds(l, 1), :].to_broadcast((P, QK))).then_inc(small_in, 16)
                    elif name == "q0":
                        load(b, in_slot(b)[:, 4:, :], columns(w["w_in"], l, 0)[:, 4:, :])
                        sp.dma_start(in_slot(b)[:, 0:4, :],
                                     columns(w["w_in"], l, 0)[:, 0:4, :]).then_inc(half_in, 16)
                    elif name in first_col:
                        load(b, in_slot(b), columns(w["w_in"], l, first_col[name]))
                    elif name == "pe":
                        load(b, in_slot(b), columns(w["w_in"], l, MLA_IN - P))
                    elif name == "kvup":
                        load(b, raw[:, b.slot, :], flat("w_kv_up", l))
                    elif name[:3] == "qup":
                        c0 = 384 * int(name[3])
                        load(b, raw[:, b.slot, 0:768].rearrange("p (t n) -> p t n", t=2),
                             w["w_q_up"][bass.ds(l, 1), :, c0:c0 + 384].rearrange("a (t p) n -> p (a t) n",
                                                                                  p=P))
                    else:
                        load(b, raw[:, b.slot, :], flat("w_out", l, P * int(name[3]), P * (int(name[3]) + 1)))
                ffn_loads(l, 1)
            for t in range(2):
                sp.wait_ge(out_copied, 2 * (t + 1))
                sp.dma_start(out[0, P * t:P * (t + 1), :], xtok[:, t, :]).then_inc(out_done, 16)
            sp.wait_ge(out_done, 32)

        ROWS_IN, SMALL_IN = 16 * len(ROWS), 16 * 6

        @block.scalar
        def _(act):
            def split(b, width=1024, halves=None):
                act.wait_ge(raw_in[b.slot], b.fills * 16)
                if halves is not None:
                    act.wait_ge(half_in, halves * 16)
                act.wait_ge(w_used, b.number + 1)
                nc.scalar.activation(whi[:, b.slot, 0:width], raw[:, b.slot, 0:width],
                                     ACT.Copy).then_inc(hi_ready, 1)

            def norm(st, phase, gain):
                for i in range(4):
                    act.wait_ge(x_ready, quarter(phase, i))
                    for t in (2 * i, 2 * i + 1):
                        ins = nc.scalar.activation(xhi[:, t, :], xT[:, t, :], ACT.Copy, scale=col(gain, t))
                    ins.then_inc(st.sem, st.step(f"hi{i}"))
                for i in range(4):
                    nc.scalar.activation(xsq[:, 2 * i:2 * i + 2, :], xT[:, 2 * i:2 * i + 2, :],
                                         ACT.Square).then_inc(st.sem, st.step(f"sq{i}"))

            def ffn(l, which):
                rnd = l * 2 + which
                split(ffn_block(l, which, "gate", 0))
                split(ffn_block(l, which, "up", 0))
                if which == 0:
                    act.wait_ge(mix_dve.sem, mix_dve.at(l, "prm1"))
                norm(ffn_act, l * 3 + 2 * which, f"ffn{which + 1}_norm")

                def gate(f, parity):
                    if not (isinstance(f, int) and f == 0):
                        split(ffn_block(l, which, "gate", f))

                def up(f, parity):
                    if not (isinstance(f, int) and f == 0):
                        split(ffn_block(l, which, "up", f))

                def down(f, parity):
                    tile = rnd * FT + f
                    act.wait_ge(h_steps, tile * 4 + 9)
                    nc.scalar.activation(ft[:, parity, :], gs[:, parity, :], ACT.Tanh,
                                         scale=0.5).then_inc(tanh_done, 1)
                    split(ffn_block(l, which, "down", f))
                    act.wait_ge(h_steps, tile * 4 + 12)
                    act.wait_ge(w_used, ffn_block(l, which, "up", 0).number + (f * 3 + 1))
                    nc.scalar.activation(hhi[:, parity, :], ft[:, 2 + parity, :], ACT.Copy).then_inc(hhi_done, 1)

                ffn_order(act, gate, up, down)

            def spread(dst, src, g0=0, n=G):
                nc.scalar.activation(dst[LO, g0:g0 + n, 0:64], src[LO], ACT.Copy)
                return nc.scalar.activation(dst[UP, g0:g0 + n, 64:128], src[UP], ACT.Copy)

            def mixing(l):
                def ahead(i):
                    if i < len(MIX_BLOCKS):
                        split(mix_block(l, MIX_BLOCKS[i]), block_width(MIX_BLOCKS[i]),
                              {0: l * 2 + 1, Q0: l * 2 + 2}.get(i))

                Q0 = MIX_BLOCKS.index("q0")
                ahead(0), ahead(1)
                act.wait_ge(once, ONCE)
                norm(mix_act, l * 3 + 1, "mix_norm")
                ahead(2), ahead(3)
                for i, t in enumerate(RW_TILES):
                    if i:
                        ahead(i + 3)
                    act.wait_ge(mix_dve.sem, mix_dve.at(l, f"pr_{t}"))
                    nc.scalar.activation(shift[:, i % 2, 1:SEQ + 1], scaled[:, i % 2, :], ACT.Copy,
                                         scale=col(*mu_col(t))).then_inc(mix_act.sem, mix_act.step(f"mu_{t}"))
                    if t == "r3":
                        act.wait_ge(mix_dve.sem, mix_dve.at(l, "sh_wa"))
                        nc.scalar.activation(lora[LO, 0, :], lora[LO, 0, :], ACT.Tanh).then_inc(mix_act.sem, mix_act.step("tanh_w"))
                    if t == "k3":
                        act.wait_ge(mix_pe.sem, mix_pe.at(l, "z"))
                        for j in range(4):
                            ins = nc.scalar.activation(zl[:, SEQ * j:SEQ * (j + 1)],
                                                       bank[4 + j // 2][:, SEQ * (j % 2):SEQ * (j % 2 + 1)],
                                                       ACT.Tanh, bias=half[:, j:j + 1], scale=0.5)
                        ins.then_inc(mix_act.sem, mix_act.step("tz"))
                        act.wait_ge(mix_pe.sem, mix_pe.at(l, "a"))
                        for j in range(4):
                            ins = nc.scalar.activation(ta[:, SEQ * j:SEQ * (j + 1)],
                                                       bank[6 + j // 2][:, SEQ * (j % 2):SEQ * (j % 2 + 1)],
                                                       ACT.Tanh, bias=half[:, 4 + j:5 + j], scale=0.5)
                        ins.then_inc(mix_act.sem, mix_act.step("ta"))
                        act.wait_ge(mix_dve.sem, mix_dve.at(l, "kk0"))
                        nc.scalar.activation(sc, kk, ACT.Square).then_inc(mix_act.sem, mix_act.step("kksq"))
                act.wait_ge(mix_dve.sem, mix_dve.at(l, "sh_g1"))
                nc.scalar.activation(lora[:, 1:3, :], lora[:, 1:3, :], ACT.Tanh,
                                     scale=0.5).then_inc(mix_act.sem, mix_act.step("gs0"))
                act.wait_ge(mix_dve.sem, mix_dve.at(l, "lc"))
                lc_g = lc.rearrange("p (g i) -> p g i", g=G)
                nc.scalar.activation(E[:, :, 1:C + 1], lc_g, ACT.Exp).then_inc(mix_act.sem, mix_act.step("E"))
                nc.scalar.activation(einv, lc, ACT.Exp, scale=-1.0).then_inc(mix_act.sem, mix_act.step("einv"))
                ahead(len(RW_TILES) + 3)
                act.wait_ge(mix_dve.sem, mix_dve.at(l, "lat_copy"))
                act.wait_ge(mix_act.sem, mix_act.at(l, "einv"))
                nc.scalar.activation(lat_sq, lat, ACT.Square).then_inc(mix_act.sem, mix_act.step("lat_sq"))
                ahead(len(RW_TILES) + 4), ahead(len(RW_TILES) + 5), ahead(len(RW_TILES) + 6)
                act.wait_ge(w_used, mixed(l, "pe"))
                act.wait_ge(mix_dve.sem, mix_dve.at(l, "sh_g1"))
                nc.scalar.activation(scaled[96:128, 1, :], bank[2][96:128, 0:SEQ],
                                     ACT.Copy).then_inc(mix_act.sem, mix_act.step("pe_T"))
                act.wait_ge(mix_pe.sem, mix_pe.at(l, "gup"))
                for j in range(2):
                    ins = nc.scalar.activation(gT[:, 512 * j:512 * (j + 1)], bank[4 + j][:], ACT.Copy)
                ins.then_inc(mix_act.sem, mix_act.step("gT"))
                act.wait_ge(mix_pe.sem, mix_pe.at(l, "peT"))
                for t in range(2):
                    ins = nc.scalar.activation(kpe[:, t, :], bank[2][:, ROPE * t:ROPE * (t + 1)], ACT.Copy,
                                               scale=rcol[:, t:t + 1])
                ins.then_inc(mix_act.sem, mix_act.step("pe"))
                act.wait_ge(mix_dve.sem, mix_dve.at(l, "a_c"))
                spread(aP, AR[:, :, 0, :]).then_inc(mix_act.sem, mix_act.step("aP"))
                act.wait_ge(mix_dve.sem, mix_dve.at(l, "lat_n"))
                nc.scalar.activation(xhi[:, 0:3, :], lat, ACT.Copy).then_inc(mix_act.sem, mix_act.step("lat_hi"))
                act.wait_ge(mix_dve.sem, mix_dve.at(l, "k_c"))
                spread(kP, kC).then_inc(mix_act.sem, mix_act.step("kP"))
                act.wait_ge(mix_dve.sem, mix_dve.at(l, "b_c"))
                spread(bP, bC).then_inc(mix_act.sem, mix_act.step("bP"))
                vT_g = vT.rearrange("p (h c i) -> p c h i", h=HP, c=NC)
                for c in range(NC):
                    ins = spread(vP, vT_g[:, c], 4 * c, 4)
                ins.then_inc(mix_act.sem, mix_act.step("vP"))
                for j in range(4):
                    act.wait_ge(mix_dve.sem, mix_dve.at(l, f"kn{j}"))
                    t, hf = j // 2, j % 2
                    nc.scalar.activation(V[:, t, 4 * hf:4 * hf + 4, :],
                                         bank[j][:].rearrange("p (h d) -> p h d", h=4)[:, :, NOPE:],
                                         ACT.Copy).then_inc(mix_act.sem, mix_act.step(f"v{j}"))
                act.wait_ge(mix_dve.sem, mix_dve.at(l, "qe3"))
                act.wait_ge(mix_act.sem, mix_act.at(l, "vP"))
                nc.scalar.activation(qk_sq, unit(3, 3), ACT.Square).then_inc(mix_act.sem, mix_act.step("qksq"))
                act.wait_ge(mix_dve.sem, mix_dve.at(l, "g1_3"))
                spread(lP, M1[:, :, 0, :]).then_inc(mix_act.sem, mix_act.step("lP"))
                for s, dst in (("tk", kP), ("tv", vP)):
                    for c in range(NC):
                        act.wait_ge(mix_pe.sem, mix_pe.at(l, f"{s}{c}"))
                        b = bank[4 + c] if s == "tk" else bank[c]
                        nc.scalar.activation(dst[:, 4 * c:4 * c + 4, :],
                                             b[:].rearrange("p (g n) -> p g n", g=4),
                                             ACT.Copy).then_inc(mix_act.sem, mix_act.step(f"{s}{c}"))
                act.wait_ge(mix_dve.sem, mix_dve.at(l, "p1"))
                spread(pP, pC).then_inc(mix_act.sem, mix_act.step("pP"))
                ahead(len(RW_TILES) + 7), ahead(len(RW_TILES) + 8), ahead(len(RW_TILES) + 9)
                for k in LV:
                    for b in range(2):
                        act.wait_ge(mix_dve.sem, mix_dve.at(l, f"um{k}_{b}"))
                        spread(uP, uC[:, 8 * b:8 * b + 8], 8 * b, 8).then_inc(mix_act.sem, mix_act.step(f"us{k}_{b}"))
                    for b in range(2):
                        if k < LEVELS:
                            act.wait_ge(mix_dve.sem, mix_dve.at(l, f"pc{k}_{b}"))
                            spread(pP, pC[:, 8 * b:8 * b + 8], 8 * b, 8).then_inc(mix_act.sem, mix_act.step(f"ps{k}_{b}"))
                        else:
                            act.wait_ge(mix_pe.sem, mix_pe.at(l, f"p{k}_{b}"))
                            spread(pP, bank[2 + b][:].rearrange("p (g i) -> p g i", g=8), 8 * b,
                                   8).then_inc(mix_act.sem, mix_act.step(f"ps{k}_{b}"))
                spread(lP, M2[:, :, 0, :]).then_inc(mix_act.sem, mix_act.step("ak"))
                for b in range(2):
                    act.wait_ge(mix_dve.sem, mix_dve.at(l, f"nmax{b}"))
                    if b:
                        act.wait_ge(mix_pe.sem, mix_pe.at(l, "pt0"))
                    for t in range(2):
                        for j in range(4):
                            i = 8 * b + 4 * t + j
                            src = bank[3 * b][:, P * j:P * (j + 1)] if t == 0 else bank[3 * b + 1 + j // 2][:,
                                                                                                            256 * (j % 2):256 * (j % 2) + 256]
                            dst = prob[:, j, 0:P] if t == 0 else prob[:, j, P:3 * P]
                            ins = nc.scalar.activation(dst, src, ACT.Exp, bias=stat[:, 96 + i:97 + i],
                                                       scale=SCALE, accum_out=stat[:, 128 + i:129 + i])
                    ins.then_inc(mix_act.sem, mix_act.step(f"ex{b}"))
                act.wait_ge(mix_dve.sem, mix_dve.at(l, "o"))
                for t in range(2):
                    ins = nc.scalar.activation(scrap[:, 512 * t:512 * (t + 1)], ymla[:, t, :], ACT.Square,
                                               accum_out=stat[:, 160 + t:161 + t])
                ins.then_inc(mix_act.sem, mix_act.step("ysq"))
                for c in range(NC):
                    act.wait_ge(mix_dve.sem, mix_dve.at(l, f"u{c}"))
                    spread(uP, rec[:, 1], 4 * (c % 2), 4).then_inc(mix_act.sem, mix_act.step(f"ub{c}"))
                    if c < NC - 1:
                        act.wait_ge(mix_dve.sem, mix_dve.at(l, f"s{c}"))
                        spread(uP, rec[:, 2 + (c + 1) % 2], 8 + 4 * ((c + 1) % 2), 4).then_inc(mix_act.sem, mix_act.step(f"sb{c}"))
                act.wait_ge(mix_dve.sem, mix_dve.at(l, "yg1"))
                nc.scalar.activation(xhi[:, 0:4, :], ymT, ACT.Copy).then_inc(mix_act.sem, mix_act.step("yhi0"))
                out0 = MIX_BLOCKS.index("out0")
                assert out0 == len(RW_TILES) + 7
                act.wait_ge(mix_dve.sem, mix_dve.at(l, "yc"))
                nc.scalar.activation(ysc, yT, ACT.Square).then_inc(mix_act.sem, mix_act.step("gsq"))
                ahead(out0 + 3), ahead(out0 + 4)
                act.wait_ge(mix_dve.sem, mix_dve.at(l, "gm"))
                for j in range(HP):
                    nc.scalar.activation(xhi[:, 4 + j, :], yN[:, SEQ * j:SEQ * (j + 1)], ACT.Copy,
                                         scale=col("out_norm_rwkv", j)).then_inc(mix_act.sem, mix_act.step(f"yhi{4 + j}"))
                nc.scalar.activation(ysc, yN, ACT.Square).then_inc(mix_act.sem, mix_act.step("rsq"))
                for i in range(out0 + 5, len(MIX_BLOCKS)):
                    ahead(i)

            with act.Fori(0, DEPTH) as l:
                ffn(l, 0)
                mixing(l)
                ffn(l, 1)

        @block.vector
        def _(dve):
            V_ = nc.vector
            dve.sem_inc(lo_ready, RING)
            dve.sem_inc(h_steps, 8)

            def split(b, width=1024):
                dve.wait_ge(hi_ready, b.number + 1)
                V_.tensor_tensor(wlo[:, b.slot, 0:width], raw[:, b.slot, 0:width],
                                 whi[:, b.slot, 0:width].bitcast(F32), ALU.subtract).then_inc(lo_ready, 1)

            def rsqrt(st, rnd, prefix, n):
                v, y, t = (root[:, i, 0:n] for i in range(3))

                def did(name, ins):
                    ins.then_inc(st.sem, st.step(f"{prefix}_{name}"))
                    dve.wait_ge(st.sem, st.at(rnd, f"{prefix}_{name}"))

                did("shift", V_.tensor_scalar(t.bitcast(I32), v.bitcast(I32), 1, None, ALU.logical_shift_right))
                did("seed",
                    V_.tensor_scalar(y.bitcast(I32), t.bitcast(I32), -1.0, float(0x5F3759DF), ALU.mult,
                                     ALU.add))
                for i in range(3):
                    did(f"sq{i}", V_.tensor_tensor(t, y, y, ALU.mult))
                    did(f"err{i}", V_.scalar_tensor_tensor(t, t, -0.5, v, ALU.mult, ALU.mult))
                    did(f"y{i}", V_.scalar_tensor_tensor(y, t, 1.5, y, ALU.add, ALU.mult))

            def norm(st, sta, stp, rnd, phase, gain, b0, between, before_row, residual=None):
                if residual is not None:
                    residual(0)
                for i in range(4):
                    if residual is not None and i < 3:
                        residual(i + 1)
                    dve.wait_ge(x_ready, quarter(phase, i))
                    dve.wait_ge(sta.sem, sta.at(rnd, f"hi{i}"))
                    for t in (2 * i, 2 * i + 1):
                        ins = V_.scalar_tensor_tensor(xlo[:, t, :], xT[:, t, :], col(gain, t),
                                                      xhi[:, t, :].bitcast(F32), ALU.mult, ALU.subtract)
                    ins.then_inc(st.sem, st.step(f"lo{i}"))
                between()
                dve.wait_ge(stp.sem, stp.at(rnd, "ss"))
                V_.tensor_scalar(root[:, 0, 0:2], bank[b0][:, 0:2], 1.0 / D, EPS, ALU.mult,
                                 ALU.add).then_inc(st.sem, st.step("ms"))
                dve.wait_ge(st.sem, st.at(rnd, "ms"))
                rsqrt(st, rnd, "norm", 2)
                before_row()
                V_.tensor_copy(rcol[:], root[:, 1, 0:2]).then_inc(st.sem, st.step("rcol"))
                dve.wait_ge(stp.sem, stp.at(rnd, "rb"))
                V_.tensor_copy(R[:], bank[b0][:, 0:SEQ]).then_inc(st.sem, st.step("row"))
                dve.wait_ge(st.sem, st.at(rnd, "row"))

            def parameters(l):
                dve.wait_ge(mix_pe.sem, mix_pe.at(l, "prm"))
                V_.tensor_copy(prm[:, 8:NROWS], bank[2][:, 0:NROWS - 8]).then_inc(mix_dve.sem, mix_dve.step("prm"))
                dve.wait_ge(mix_dve.sem, mix_dve.at(l, "prm"))
                m = ROW["mu_r"]
                V_.tensor_scalar(omm[:], prm[:, m:m + MU_N], -1.0, 1.0, ALU.mult, ALU.add).then_inc(mix_dve.sem, mix_dve.step("omm"))
                V_.tensor_scalar(half[:, 0:8], prm[:, ROW["w0"]:ROW["w0"] + 8], 0.5, None,
                                 ALU.mult).then_inc(mix_dve.sem, mix_dve.step("half_wa"))
                V_.tensor_scalar(half[:, 8:12], prm[:, ROW["k_a"]:ROW["k_a"] + 4], -1.0, 1.0, ALU.mult,
                                 ALU.add).then_inc(mix_dve.sem, mix_dve.step("one_k"))

            def ffn_residual(l, which):
                def quarter_of(i):
                    if i < 3:
                        dve.wait_ge(ffn_pe.sem, ffn_pe.at(l * 2 + which, f"sum{i}"))
                    else:
                        dve.wait_ge(w_used, tile_done(l, which, "down", FT - 1))
                    V_.scalar_tensor_tensor(x_quarter(i), bank[i][:], 0.25, x_quarter(i), ALU.mult,
                                            ALU.add).then_inc(x_ready, 1)
                return quarter_of

            def mix_residual(l):
                def quarter_of(i):
                    if i < 3:
                        dve.wait_ge(mix_pe.sem, mix_pe.at(l, f"sum{i}"))
                    else:
                        dve.wait_ge(w_used, mixed(l, "out7"))
                    part = parts[:, 512 * i:512 * (i + 1)]
                    V_.tensor_tensor(part.rearrange("p (t n) -> p t n", t=2),
                                     bank[4 + i][:].rearrange("p (t n) -> p t n", t=2),
                                     R[:].unsqueeze(1).to_broadcast((P, 2, SEQ)),
                                     ALU.mult).then_inc(mix_dve.sem, mix_dve.step(f"resr{i}"))
                    if i % 2 == 0:
                        dve.wait_ge(mix_dve.sem, mix_dve.at(l, f"resr{i}"))
                        if i:
                            dve.wait_ge(x_ready, quarter(l * 3 + 2, i - 1))
                        V_.tensor_tensor(x_quarter(i), x_quarter(i), part, ALU.add).then_inc(x_ready, 1)
                return quarter_of

            def ffn(l, which):
                rnd = l * 2 + which
                if which == 0:
                    split(ffn_block(l, which, "gate", 0))
                    split(ffn_block(l, which, "up", 0))
                norm(ffn_dve, ffn_act, ffn_pe, rnd, l * 3 + 2 * which, f"ffn{which + 1}_norm", 0,
                     lambda: split(ffn_block(l, which, "gate", 1)), lambda: split(ffn_block(l, which, "up", 1)),
                     mix_residual(l) if which else None)
                if which == 0:
                    parameters(l)

                def gate(f, parity):
                    if not (isinstance(f, int) and f < 2):
                        split(ffn_block(l, which, "gate", f))

                def up(f, parity):
                    if not (isinstance(f, int) and f < 2):
                        split(ffn_block(l, which, "up", f))

                def down(f, parity):
                    tile = rnd * FT + f
                    g, u, t, h = bank[4 + parity], bank[6 + parity], ft[:, parity, :], ft[:, 2 + parity, :]
                    dve.wait_ge(w_used, tile_done(l, which, "gate", f))
                    V_.tensor_tensor(gs[:, parity, :], g[:, 0:SEQ], R[:], ALU.mult).then_inc(h_steps, 1)
                    dve.wait_ge(w_used, tile_done(l, which, "up", f))
                    V_.tensor_tensor(h, u[:, 0:SEQ], R[:], ALU.mult).then_inc(h_steps, 1)
                    dve.wait_ge(h_steps, tile * 4 + 10)
                    V_.tensor_tensor(h, h, gs[:, parity, :], ALU.mult).then_inc(h_steps, 1)
                    dve.wait_ge(tanh_done, tile + 1)
                    dve.wait_ge(h_steps, tile * 4 + 11)
                    V_.scalar_tensor_tensor(h, t, 1.0, h, ALU.add, ALU.mult).then_inc(h_steps, 1)
                    split(ffn_block(l, which, "down", f))
                    dve.wait_ge(hhi_done, tile + 1)
                    V_.tensor_tensor(hlo[:, parity, :], h, hhi[:, parity, :].bitcast(F32),
                                     ALU.subtract).then_inc(hlo_done, 1)

                ffn_order(dve, gate, up, down)
                if which == 0:
                    split(mix_block(l, MIX_BLOCKS[0]))
                    split(mix_block(l, MIX_BLOCKS[1]))
                else:
                    for i in range(4):
                        ffn_residual(l, which)(i)

            def mixing(l):
                def ahead(i):
                    if i < len(MIX_BLOCKS):
                        split(mix_block(l, MIX_BLOCKS[i]), block_width(MIX_BLOCKS[i]))

                def tiles(v, j):
                    return v[:, SEQ * j:SEQ * (j + 1)]

                def chunked(v):
                    return v.rearrange("p (h c i) -> p c h i", h=HP, c=NC)

                def grouped(v):
                    return v.rearrange("p (c h) i -> p c h i", h=HP)

                dve.wait_ge(once, ONCE)
                norm(mix_dve, mix_act, mix_pe, l, l * 3 + 1, "mix_norm", 7, lambda: ahead(2), lambda: ahead(3),
                     ffn_residual(l, 0))
                dest = {"wa": lora[:, 0, :], "g0": lora[:, 1, :], "g1": lora[:, 2, :]}
                for j in range(4):
                    dest.update({f"r{j}": tiles(rT, j), f"k{j}": tiles(kT, j), f"v{j}": tiles(vT, j)})

                def scale(i):
                    if i >= 2:
                        dve.wait_ge(mix_dve.sem, mix_dve.at(l, f"sh_{RW_TILES[i - 2]}"))
                    dve.wait_ge(w_used, mixed(l, RW_TILES[i]))
                    V_.tensor_tensor(scaled[:, i % 2, :], bank[i % 4][:, 0:SEQ], R[:],
                                     ALU.mult).then_inc(mix_dve.sem, mix_dve.step(f"pr_{RW_TILES[i]}"))

                scale(0)
                for i, t in enumerate(RW_TILES):
                    if i + 1 < len(RW_TILES):
                        scale(i + 1)
                    if i:
                        ahead(i + 3)
                    dve.wait_ge(mix_dve.sem, mix_dve.at(l, f"pr_{t}"))
                    dve.wait_ge(mix_act.sem, mix_act.at(l, f"mu_{t}"))
                    m = ROW[mu_col(t)[0]] + mu_col(t)[1] - ROW["mu_r"]
                    V_.scalar_tensor_tensor(dest[t], scaled[:, i % 2, :], omm[:, m:m + 1],
                                            shift[:, i % 2, 0:SEQ], ALU.mult, ALU.add).then_inc(mix_dve.sem, mix_dve.step(f"sh_{t}"))
                    if t == "k3":
                        dve.wait_ge(mix_dve.sem, mix_dve.at(l, "sh_k3"))
                        for j in range(4):
                            ins = V_.tensor_scalar(tiles(kk, j), tiles(kT, j), col("k_k", j), None, ALU.mult)
                        ins.then_inc(mix_dve.sem, mix_dve.step("kk0"))
                    if t == "v0":
                        dve.wait_ge(mix_act.sem, mix_act.at(l, "tz"))
                        V_.tensor_scalar(zl, zl, -DECAY / 2, -DECAY / 2, ALU.mult,
                                         ALU.add).then_inc(mix_dve.sem, mix_dve.step("lw"))
                    if t == "v2":
                        dve.wait_ge(mix_dve.sem, mix_dve.at(l, "lw"))
                        for j in range(4):
                            ins = V_.tensor_tensor_scan(tiles(lc, j), con("reset"), tiles(zl, j), 0.0, ALU.mult,
                                                        ALU.add)
                        ins.then_inc(mix_dve.sem, mix_dve.step("lc"))
                dve.wait_ge(mix_act.sem, mix_act.at(l, "gs0"))
                V_.tensor_scalar(lora[:, 1:3, :], lora[:, 1:3, :], 0.5, 0.5, ALU.mult,
                                 ALU.add).then_inc(mix_dve.sem, mix_dve.step("gs"))
                ahead(len(RW_TILES) + 3)
                dve.wait_ge(mix_pe.sem, mix_pe.at(l, "kkss"))
                V_.tensor_scalar(root[:, 0, 0:16], bank[4][:, 0:16], 1e-24, None, ALU.max).then_inc(mix_dve.sem, mix_dve.step("kkms"))
                dve.wait_ge(mix_dve.sem, mix_dve.at(l, "kkms"))
                rsqrt(mix_dve, l, "kk", 16)
                V_.tensor_copy(sc.rearrange("p (g i) -> p g i", g=16),
                               root[:, 1, 0:16].unsqueeze(2).to_broadcast((P, 16, 64))).then_inc(mix_dve.sem, mix_dve.step("kkw"))
                dve.wait_ge(mix_dve.sem, mix_dve.at(l, "lc"))
                dve.wait_ge(w_used, mixed(l, "kv"))
                for j in range(3):
                    ins = V_.tensor_tensor(lat[:, j, :], bank[(len(RW_TILES) + j) % 4][:, 0:SEQ], R[:],
                                           ALU.mult)
                ins.then_inc(mix_dve.sem, mix_dve.step("lat_copy"))
                dve.wait_ge(mix_act.sem, mix_act.at(l, "ta"))
                V_.tensor_scalar(ta, ta, 0.5, 0.5, ALU.mult, ALU.add).then_inc(mix_dve.sem, mix_dve.step("a"))
                dve.wait_ge(mix_pe.sem, mix_pe.at(l, "kkb"))
                for b in range(2):
                    s = slice(512 * b, 512 * (b + 1))
                    ins = V_.tensor_tensor(kk[:, s], kk[:, s], bank[6 + b][:], ALU.mult)
                ins.then_inc(mix_dve.sem, mix_dve.step("kk"))
                dve.wait_ge(mix_dve.sem, mix_dve.at(l, "a"))
                dve.wait_ge(mix_dve.sem, mix_dve.at(l, "kk"))
                for j in range(4):
                    ins = V_.tensor_scalar(tiles(sc, j), tiles(ta, j), col("k_a", j), half[:, 8 + j:9 + j],
                                           ALU.mult, ALU.add)
                ins.then_inc(mix_dve.sem, mix_dve.step("kf"))
                dve.wait_ge(mix_dve.sem, mix_dve.at(l, "kf"))
                V_.tensor_tensor(kmod, kT, sc, ALU.mult).then_inc(mix_dve.sem, mix_dve.step("kmod"))
                dve.wait_ge(mix_act.sem, mix_act.at(l, "einv"))
                E_c = E[:].rearrange("p (h c) i -> p c h i", h=HP)

                def per_chunk(fn):
                    for c in range(NC):
                        ins = fn(c)
                    return ins

                per_chunk(lambda c: V_.scalar_tensor_tensor(grouped(AR[:, :, 0, :])[:, c], chunked(kk)[:, c],
                                                            -1.0, E_c[:, c, :, 0:C], ALU.mult,
                                                            ALU.mult)).then_inc(mix_dve.sem, mix_dve.step("a_c"))
                dve.wait_ge(mix_dve.sem, mix_dve.at(l, "kkw"))
                dve.wait_ge(mix_pe.sem, mix_pe.at(l, "latss"))
                V_.tensor_scalar(root[:, 0, 0:2], bank[3][:, 0:2], 1.0 / QL, EPS, ALU.mult, ALU.add)
                V_.tensor_scalar(root[:, 0, 2:4], bank[3][:, 2:4], 1.0 / KVL, EPS, ALU.mult,
                                 ALU.add).then_inc(mix_dve.sem, mix_dve.step("lat_ms"))
                dve.wait_ge(mix_dve.sem, mix_dve.at(l, "lat_ms"))
                rsqrt(mix_dve, l, "lat", 4)
                ahead(len(RW_TILES) + 4)
                dve.wait_ge(mix_dve.sem, mix_dve.at(l, "kmod"))
                per_chunk(lambda c: V_.tensor_tensor(grouped(kC)[:, c], chunked(kmod)[:, c],
                                                     chunked(einv)[:, c], ALU.mult)).then_inc(mix_dve.sem, mix_dve.step("k_c"))
                dve.wait_ge(mix_pe.sem, mix_pe.at(l, "latb"))
                for j in range(3):
                    g = col("q_lat_norm", j) if j < 2 else col("kv_lat_norm")
                    r = bank[3][:, 0:SEQ] if j < 2 else bank[3][:, SEQ:512]
                    ins = V_.scalar_tensor_tensor(lat[:, j, :], lat[:, j, :], g, r, ALU.mult, ALU.mult)
                ins.then_inc(mix_dve.sem, mix_dve.step("lat_n"))
                dve.wait_ge(mix_act.sem, mix_act.at(l, "lat_hi"))
                V_.tensor_tensor(xlo[:, 0:3, :], lat, xhi[:, 0:3, :].bitcast(F32),
                                 ALU.subtract).then_inc(mix_dve.sem, mix_dve.step("lat_lo"))
                ahead(len(RW_TILES) + 5)
                dve.wait_ge(mix_pool.sem, mix_pool.at(l, "kk2"))
                per_chunk(lambda c: V_.tensor_tensor(grouped(bC)[:, c], chunked(sc)[:, c], chunked(einv)[:, c],
                                                     ALU.mult)).then_inc(mix_dve.sem, mix_dve.step("b_c"))
                ahead(len(RW_TILES) + 6)
                dve.wait_ge(w_used, mixed(l, "kvup"))
                for j in range(4):
                    t, hf = j // 2, j % 2
                    V_.tensor_copy(qk[:, t, 1, 4 * hf:4 * hf + 4, 0:NOPE],
                                   bank[j][:].rearrange("p (h d) -> p h d", h=4)[:, :,
                                                                                 0:NOPE]).then_inc(mix_dve.sem, mix_dve.step(f"kn{j}"))
                dve.wait_ge(mix_pe.sem, mix_pe.at(l, "bsum"))
                for b in range(2):
                    s = slice(512 * b, 512 * (b + 1))
                    ins = V_.tensor_tensor(bonus[:, s], bank[5 + 2 * b][:], vT[:, s], ALU.mult)
                ins.then_inc(mix_dve.sem, mix_dve.step("bonus"))
                dve.wait_ge(mix_act.sem, mix_act.at(l, "pe"))
                for t in range(2):
                    ins = V_.tensor_copy(qk[:, t, 1, :, NOPE:QK], kpe[:, t:t + 1, :].to_broadcast((P, H, ROPE)))
                ins.then_inc(mix_dve.sem, mix_dve.step("kpe"))
                for hf in range(2):
                    dve.wait_ge(w_used, mixed(l, f"qup{hf}"))
                    for t in range(2):
                        V_.tensor_copy(qk[:, t, 0, 4 * hf:4 * hf + 4, :],
                                       bank[4 + 2 * t + hf][:, 0:384].rearrange("p (h d) -> p h d",
                                                                                h=4)).then_inc(mix_dve.sem, mix_dve.step(f"qe{2 * hf + t}"))
                upper = con("upper").rearrange("p (s i) -> p s i", s=2).unsqueeze(1).to_broadcast((P, 4, 2, C))
                for s, M, b0 in (("g1", M1, 0), ("g2", M2, 4)):
                    for c in range(NC):
                        dve.wait_ge(mix_pe.sem, mix_pe.at(l, f"{s}_{c}"))
                        V_.tensor_tensor(M[:, 4 * c:4 * c + 4],
                                         bank[b0 + c][:].rearrange("p (g s i) -> p g s i", g=4, s=2), upper,
                                         ALU.mult).then_inc(mix_dve.sem, mix_dve.step(f"{s}_{c}"))
                for c in range(NC):
                    dve.wait_ge(mix_pe.sem, mix_pe.at(l, f"tb{c}"))
                    V_.tensor_copy(bP[:, 4 * c:4 * c + 4, :],
                                   bank[c][:].rearrange("p (g n) -> p g n", g=4)).then_inc(mix_dve.sem, mix_dve.step(f"tb{c}"))
                dve.wait_ge(mix_dve.sem, mix_dve.at(l, "g1_3"))
                V_.tensor_tensor(pC, M1[:, :, 0, :], con("level1T").unsqueeze(1).to_broadcast((P, G, C)),
                                 ALU.mult).then_inc(mix_dve.sem, mix_dve.step("p1a"))
                dve.wait_ge(mix_dve.sem, mix_dve.at(l, "p1a"))
                V_.tensor_tensor(pC, pC, con("eyes").unsqueeze(1).to_broadcast((P, G, C)),
                                 ALU.add).then_inc(mix_dve.sem, mix_dve.step("p1"))
                dve.wait_ge(mix_act.sem, mix_act.at(l, "qksq"))
                V_.tensor_reduce(stat[:, 0:32], qk_sq.rearrange("p (g d) -> p g d", d=QK), AX_X,
                                 ALU.add).then_inc(mix_dve.sem, mix_dve.step("qkss"))
                dve.wait_ge(mix_dve.sem, mix_dve.at(l, "qkss"))
                def eight(v, b):
                    return v[:, 8 * b:8 * b + 8, :]

                def bank8(i):
                    return bank[i][:].rearrange("p (g i) -> p g i", g=8)

                for b in range(2):
                    dve.wait_ge(mix_pe.sem, mix_pe.at(l, f"ti{b}"))
                    V_.tensor_copy(eight(tC, b), bank8(b)).then_inc(mix_dve.sem, mix_dve.step(f"t0_{b}"))
                q3 = unit(3, 3).rearrange("p (g d) -> p g d", d=QK)

                def qk_piece(k):
                    if k == 1:
                        V_.tensor_scalar(root[:, 0, :], stat[:, 0:32], 1.0 / QK, EPS, ALU.mult,
                                         ALU.add).then_inc(mix_dve.sem, mix_dve.step("qkms"))
                        dve.wait_ge(mix_dve.sem, mix_dve.at(l, "qkms"))
                        rsqrt(mix_dve, l, "qk", 32)
                    elif k == 2:
                        V_.tensor_tensor(q3, q3, root[:, 1, :].unsqueeze(2).to_broadcast((P, 32, QK)),
                                         ALU.mult).then_inc(mix_dve.sem, mix_dve.step("qkn"))
                    elif k == 3:
                        dve.wait_ge(mix_dve.sem, mix_dve.at(l, "qkn"))
                        for t in range(2):
                            for s in range(2):
                                ins = V_.tensor_tensor(qk[:, t, s], qk[:, t, s],
                                                       qkgain[:, s:s + 1, :].to_broadcast((P, H, QK)), ALU.mult)
                        ins.then_inc(mix_dve.sem, mix_dve.step("qkg"))
                    else:
                        t = k - 4
                        dve.wait_ge(mix_dve.sem, mix_dve.at(l, f"rope{t - 1}" if t else "qkg"))
                        qt = qk[:, t].rearrange("p s h d -> p (s h) d")
                        x1, x2 = qt[:, :, NOPE:NOPE + 16], qt[:, :, NOPE + 16:QK]
                        cos, sin = (con(n)[:,
                                           16 * t:16 * t + 16].unsqueeze(1).to_broadcast((P, 2 * H,
                                                                                          16)) for n in ("cos",
                                                                                                         "sin"))
                        r = [v.rearrange("p (g n) -> p g n", g=2 * H) for v in rope]
                        for v, (a, b) in zip(r, ((x1, cos), (x2, sin), (x2, cos), (x1, sin))):
                            ins = V_.tensor_tensor(v, a, b, ALU.mult)
                        ins.then_inc(mix_dve.sem, mix_dve.step(f"rope_m{t}"))
                        dve.wait_ge(mix_dve.sem, mix_dve.at(l, f"rope_m{t}"))
                        V_.tensor_tensor(x1, r[0], r[1], ALU.subtract)
                        V_.tensor_tensor(x2, r[2], r[3], ALU.add).then_inc(mix_dve.sem, mix_dve.step(f"rope{t}"))

                for k in LV:
                    lev = con("level")[:, 64 * (k - 1):64 * k].unsqueeze(1).to_broadcast((P, 8, C))
                    for b in range(2):
                        dve.wait_ge(mix_pe.sem, mix_pe.at(l, f"u{k}_{b}"))
                        V_.tensor_tensor(eight(uC, b), bank8(4 + b), lev, ALU.mult).then_inc(mix_dve.sem, mix_dve.step(f"um{k}_{b}"))
                    qk_piece(k)
                    if k < LEVELS:
                        for b in range(2):
                            dve.wait_ge(mix_pe.sem, mix_pe.at(l, f"t{k}_{b}"))
                            V_.tensor_copy(eight(tC, b), bank8(b)).then_inc(mix_dve.sem, mix_dve.step(f"tc{k}_{b}"))
                            dve.wait_ge(mix_pe.sem, mix_pe.at(l, f"p{k}_{b}"))
                            V_.tensor_copy(eight(pC, b), bank8(2 + b)).then_inc(mix_dve.sem, mix_dve.step(f"pc{k}_{b}"))
                for i in range(8):
                    s, t, hq = i // 4, (i // 2) % 2, i % 2
                    dve.wait_ge(mix_pe.sem, mix_pe.at(l, f"qkT{i}"))
                    V_.tensor_copy(qkT[s][0:QK, 4 * hq:4 * hq + 4, P * t:P * (t + 1)],
                                   bank[i][0:QK, :].rearrange("p (h n) -> p h n", h=4)).then_inc(mix_dve.sem, mix_dve.step(f"qkT{i}"))
                for b in range(2):
                    dve.wait_ge(mix_pe.sem, mix_pe.at(l, f"sc{b}"))
                    V_.memset(bank[3 * b][LO, :].rearrange("p (h k) -> p h k", h=4)[:, :, 64:128], NEG)
                    for j in range(2):
                        ins = V_.memset(bank[3 * b + 1 + j][LO, :].rearrange("p (h k) -> p h k", h=2)[:, :,
                                                                                                      192:256],
                                        NEG)
                    ins.then_inc(mix_dve.sem, mix_dve.step(f"mask{b}"))
                    dve.wait_ge(mix_dve.sem, mix_dve.at(l, f"mask{b}"))
                    m0 = 64 + 8 * b
                    V_.tensor_reduce(stat[:, m0:m0 + 4], bank[3 * b][:].rearrange("p (h k) -> p h k", h=4),
                                     AX_X, ALU.max)
                    for j in range(2):
                        ins = V_.tensor_reduce(stat[:, m0 + 4 + 2 * j:m0 + 6 + 2 * j],
                                               bank[3 * b + 1 + j][:].rearrange("p (h k) -> p h k", h=2), AX_X,
                                               ALU.max)
                    ins.then_inc(mix_dve.sem, mix_dve.step(f"max{b}"))
                    dve.wait_ge(mix_dve.sem, mix_dve.at(l, f"max{b}"))
                    V_.tensor_scalar(stat[:, 96 + 8 * b:104 + 8 * b], stat[:, m0:m0 + 8], -SCALE, None,
                                     ALU.mult).then_inc(mix_dve.sem, mix_dve.step(f"nmax{b}"))
                ahead(len(RW_TILES) + 7), ahead(len(RW_TILES) + 8)
                for b in range(2):
                    dve.wait_ge(mix_pe.sem, mix_pe.at(l, f"pt{b}"))
                    if b:
                        dve.wait_ge(mix_pe.sem, mix_pe.at(l, "pv0"))
                    for m, bk in enumerate(((6, 7, 0), (3, 4, 5))[b]):
                        ins = V_.tensor_copy(probT[:, m, :], bank[bk][:])
                    ins.then_inc(mix_dve.sem, mix_dve.step(f"pt{b}"))
                ahead(len(RW_TILES) + 9)
                dve.wait_ge(mix_act.sem, mix_act.at(l, "ex1"))
                V_.reciprocal(stat[:, 144:160], stat[:, 128:144]).then_inc(mix_dve.sem, mix_dve.step("rinv"))
                dve.wait_ge(mix_dve.sem, mix_dve.at(l, "rinv"))
                dve.wait_ge(mix_pe.sem, mix_pe.at(l, "pv1"))
                rinv = stat[:, 144:160].rearrange("p (b t j) -> p b t j", b=2, t=2)
                for t in range(2):
                    for b in range(2):
                        y = ymla[:, t, 256 * b:256 * b + 256].rearrange("p (j d) -> p j d", j=4)
                        o = bank[1 + t][:, 256 * b:256 * b + 256].rearrange("p (j d) -> p j d", j=4)
                        ins = V_.tensor_tensor(y, o, rinv[:, b, t, :].unsqueeze(2).to_broadcast((P, 4, DV)),
                                               ALU.mult)
                ins.then_inc(mix_dve.sem, mix_dve.step("o"))

                def y_piece(c):
                    if c == 0:
                        dve.wait_ge(mix_act.sem, mix_act.at(l, "ysq"))
                        V_.tensor_scalar(root[:, 0, 0:2], stat[:, 160:162], 1.0 / (H * DV), EPS, ALU.mult,
                                         ALU.add).then_inc(mix_dve.sem, mix_dve.step("yms"))
                        dve.wait_ge(mix_dve.sem, mix_dve.at(l, "yms"))
                        rsqrt(mix_dve, l, "ym", 2)
                        for t in range(2):
                            ins = V_.tensor_scalar(ymla[:, t, :], ymla[:, t, :], root[:, 1, t:t + 1], None,
                                                   ALU.mult)
                        ins.then_inc(mix_dve.sem, mix_dve.step("yn"))
                    if c == 1:
                        dve.wait_ge(mix_pe.sem, mix_pe.at(l, "y1"))
                        V_.tensor_copy(yT[:, 0:512], bank[0][:]).then_inc(mix_dve.sem, mix_dve.step("ye0"))
                    if c in (1, 2):
                        dve.wait_ge(mix_pe.sem, mix_pe.at(l, f"yT{c - 1}"))
                        for f in (2 * c - 2, 2 * c - 1):
                            ins = V_.tensor_scalar(ymT[:, f, :],
                                                   bank[2 - c][:, 256 * (f % 2):256 * (f % 2) + 256],
                                                   col("out_norm_mla", f), None, ALU.mult)
                        ins.then_inc(mix_dve.sem, mix_dve.step(f"yg{c - 1}"))
                    if c == 3:
                        dve.wait_ge(mix_act.sem, mix_act.at(l, "yhi0"))
                        V_.tensor_tensor(xlo[:, 0:4, :], ymT, xhi[:, 0:4, :].bitcast(F32),
                                         ALU.subtract).then_inc(mix_dve.sem, mix_dve.step("ylo0"))

                for c in range(NC):
                    dve.wait_ge(mix_pe.sem, mix_pe.at(l, f"x{c}"))
                    V_.tensor_copy(rec[:, 0],
                                   bank[4 + c % 2][:, 0:256].rearrange("p (h i) -> p h i",
                                                                       h=HP)).then_inc(mix_dve.sem, mix_dve.step(f"x{c}"))
                    dve.wait_ge(mix_pe.sem, mix_pe.at(l, f"u{c}"))
                    V_.tensor_copy(rec[:, 1],
                                   bank[6 + c % 2][:, 0:256].rearrange("p (h i) -> p h i",
                                                                       h=HP)).then_inc(mix_dve.sem, mix_dve.step(f"u{c}"))
                    if c < NC - 1:
                        dve.wait_ge(mix_pe.sem, mix_pe.at(l, f"s{c}"))
                        grown = bank[2 + c % 2][:, 0:256].rearrange("p (h i) -> p h i", h=HP)
                        new = rec[:, 2 + (c + 1) % 2]
                        if c:
                            V_.tensor_tensor(new, grown, rec[:, 2 + c % 2], ALU.add).then_inc(mix_dve.sem, mix_dve.step(f"sa{c}"))
                            dve.wait_ge(mix_dve.sem, mix_dve.at(l, f"sa{c}"))
                            grown = new
                        V_.tensor_tensor(new, grown, E_c[:, c, :, C:C + 1].to_broadcast((P, HP, HEAD)),
                                         ALU.mult).then_inc(mix_dve.sem, mix_dve.step(f"s{c}"))
                    y_piece(c)
                dve.wait_ge(mix_pe.sem, mix_pe.at(l, "y3"))
                V_.tensor_copy(yT[:, 512:1024], bank[1][:]).then_inc(mix_dve.sem, mix_dve.step("ye1"))
                dve.wait_ge(mix_dve.sem, mix_dve.at(l, "ye1"))
                dve.wait_ge(mix_pe.sem, mix_pe.at(l, "mean"))
                for b in range(2):
                    s = slice(512 * b, 512 * (b + 1))
                    ins = V_.tensor_tensor(yT[:, s], yT[:, s], bank[4 + b][:], ALU.subtract)
                ins.then_inc(mix_dve.sem, mix_dve.step("yc"))
                dve.wait_ge(mix_pe.sem, mix_pe.at(l, "var"))
                V_.tensor_scalar(root[:, 0, 0:16], bank[6][:, 0:16], GN_EPS, None,
                                 ALU.add).then_inc(mix_dve.sem, mix_dve.step("gv"))
                dve.wait_ge(mix_dve.sem, mix_dve.at(l, "gv"))
                rsqrt(mix_dve, l, "gv", 16)
                V_.tensor_copy(sc.rearrange("p (g i) -> p g i", g=16),
                               root[:, 1, 0:16].unsqueeze(2).to_broadcast((P, 16, 64))).then_inc(mix_dve.sem, mix_dve.step("gvw"))
                out0 = MIX_BLOCKS.index("out0")
                ahead(out0 + 3)
                dve.wait_ge(mix_pe.sem, mix_pe.at(l, "gvb"))
                for b in range(2):
                    s = slice(512 * b, 512 * (b + 1))
                    ins = V_.tensor_tensor(yT[:, s], yT[:, s], bank[4 + b][:], ALU.mult)
                ins.then_inc(mix_dve.sem, mix_dve.step("gy"))
                dve.wait_ge(mix_dve.sem, mix_dve.at(l, "gy"))
                y_h = yT.rearrange("p (c h i) -> p h c i", c=NC, h=HP)
                for j in range(HP):
                    ins = V_.tensor_scalar(tiles(yN, j).rearrange("p (c i) -> p c i", c=NC), y_h[:, j],
                                           col("gn_gain", j), col("gn_bias", j), ALU.mult, ALU.add)
                ins.then_inc(mix_dve.sem, mix_dve.step("gg"))
                dve.wait_ge(mix_dve.sem, mix_dve.at(l, "gg"))
                V_.tensor_tensor(yN, yN, bonus, ALU.add).then_inc(mix_dve.sem, mix_dve.step("gb"))
                dve.wait_ge(mix_dve.sem, mix_dve.at(l, "gb"))
                V_.tensor_tensor(yN, yN, gT, ALU.mult).then_inc(mix_dve.sem, mix_dve.step("gm"))
                ahead(out0 + 4)
                for j in range(HP):
                    dve.wait_ge(mix_act.sem, mix_act.at(l, f"yhi{4 + j}"))
                    V_.scalar_tensor_tensor(xlo[:, 4 + j, :], tiles(yN, j), col("out_norm_rwkv", j),
                                            xhi[:, 4 + j, :].bitcast(F32), ALU.mult,
                                            ALU.subtract).then_inc(mix_dve.sem, mix_dve.step(f"ylo{4 + j}"))
                dve.wait_ge(w_used, mixed(l, "out3"))
                for i in range(4):
                    V_.tensor_tensor(x_quarter(i), x_quarter(i), bank[i][:], ALU.add).then_inc(mix_dve.sem, mix_dve.step(f"resm{i}"))
                ahead(out0 + 5)
                dve.wait_ge(mix_pe.sem, mix_pe.at(l, "rms"))
                V_.tensor_scalar(root[:, 0, 0:2], bank[0][:, 0:2], 1.0 / RW, EPS, ALU.mult,
                                 ALU.add).then_inc(mix_dve.sem, mix_dve.step("rms"))
                dve.wait_ge(mix_dve.sem, mix_dve.at(l, "rms"))
                rsqrt(mix_dve, l, "rms", 2)
                ahead(out0 + 6)
                dve.wait_ge(mix_pe.sem, mix_pe.at(l, "rmsb"))
                V_.tensor_copy(R[:], bank[1][:, 0:SEQ]).then_inc(mix_dve.sem, mix_dve.step("rmsrow"))
                ahead(out0 + 7)
                dve.wait_ge(mix_dve.sem, mix_dve.at(l, "rmsrow"))
                split(ffn_block(l, 1, "gate", 0))
                split(ffn_block(l, 1, "up", 0))

            dve.wait_ge(const_in, 16)
            for i in range(4):
                dve.wait_ge(x_turned, i + 1)
                V_.tensor_copy(xT[:, 2 * i:2 * i + 2, :].rearrange("p t n -> p (t n)"),
                               bank[i][:]).then_inc(x_ready, 1)

            with dve.Fori(0, DEPTH) as l:
                dve.wait_ge(mix_pe.sem, mix_pe.at(l, "prm1"))
                V_.tensor_copy(prm[:, 0:8], bank[5][:, 0:8]).then_inc(mix_dve.sem, mix_dve.step("prm1"))
                dve.wait_ge(mix_dve.sem, mix_dve.at(l, "prm1"))
                ffn(l, 0)
                mixing(l)
                ffn(l, 1)
            for i in range(4):
                dve.wait_ge(out_turned, i + 1)
                V_.tensor_copy(unit(0, 2)[:, 512 * i:512 * (i + 1)], bank[i][:]).then_inc(out_copied, 1)

        @block.tensor
        def _(pe):
            mm = nc.tensor.matmul

            def three(out, hi, lo, mhi, mlo, start, stop, **kw):
                mm(out, hi, mhi, start=start, stop=False, **kw)
                mm(out, hi, mlo, start=False, stop=False, **kw)
                return mm(out, lo, mhi, start=False, stop=stop, **kw)

            def turn(out, in_):
                n = in_.shape[0]
                return nc.tensor.transpose(out, in_, ident[0:n, 0:n])

            def squares(st, sta, rnd, b0, part):
                n = part // 2
                if part == 0:
                    for i in range(4):
                        pe.wait_ge(sta.sem, sta.at(rnd, f"sq{i}"))
                for t in range(4 * (part % 2), 4 * (part % 2) + 4):
                    ins = mm(bank[b0][:, n:n + 1], xsq[:, t, P * n:P * (n + 1)], con("ones")[:, 0:1],
                             start=t == 0, stop=t == DT - 1)
                if part == 3:
                    ins.then_inc(st.sem, st.step("ss"))

            def spread_rows(out, i):
                return mm(out, root[:, 1, i:i + 1].to_broadcast((P, P)), ident, start=True, stop=True)

            def spread_heads(b0):
                for j in range(8):
                    ins = mm(bank[b0 + j // 4][:, P * (j % 4):P * (j % 4 + 1)], sc[:, P * j:P * (j + 1)], ident,
                             start=True, stop=True)
                return ins

            def norm_rows(st, stv, rnd, b0):
                pe.wait_ge(stv.sem, stv.at(rnd, "norm_y2"))
                for n in range(2):
                    ins = spread_rows(bank[b0][:, P * n:P * (n + 1)], n)
                ins.then_inc(st.sem, st.step("rb"))

            def keep_clock(b, n):
                for _ in range(n):
                    mm(bank[b][:], zeros[:, 0:P], zeros[:], start=True, stop=True)

            def clear(b0):
                for i in range(4):
                    mm(bank[b0 + i][:], zeros[0:1, 0:P], zeros[0:1, :], start=True, stop=False,
                       skip_group_check=True)

            def split_ready(b):
                pe.wait_ge(lo_ready, b.number + (RING + 1))

            def column_tile(b, out, wait=None, among=None):
                for t in range(DT):
                    if wait is not None and t % 2 == 0:
                        wait(t // 2)
                    s = slice(P * t, P * (t + 1))
                    if among is not None and t >= 4:
                        among(t - 4)
                    ins = three(out, whi[:, b.slot, s], wlo[:, b.slot, s], xhi[:, t, :], xlo[:, t, :], t == 0,
                                t == DT - 1)
                return ins

            def ffn(l, which):
                rnd = l * 2 + which
                if which == 0:
                    for i in range(4):
                        pe.wait_ge(x_ready, quarter(l * 3, i))
                else:
                    pe.wait_ge(mix_dve.sem, mix_dve.at(l, "resm3"))
                    keep_clock(0, 16)

                def gate(f, parity):
                    first = isinstance(f, int) and f == 0
                    b = ffn_block(l, which, "gate", f)
                    split_ready(b)
                    pe.wait_ge(h_steps, (rnd * FT + f) * 4 + 2)

                    def low_ready(i):
                        pe.wait_ge(ffn_dve.sem, ffn_dve.at(rnd, f"lo{i}"))

                    column_tile(b, bank[4 + parity][:, 0:SEQ], low_ready if first else None).then_inc(w_used, 1)
                    if isinstance(f, int) and f == 1:
                        norm_rows(ffn_pe, ffn_dve, rnd, 0)
                        if which == 0:
                            pe.wait_ge(rows_in, l * ROWS_IN + ROWS_IN)
                            turn(bank[2][:, 0:NROWS - 8], rows[:]).then_inc(mix_pe.sem, mix_pe.step("prm"))

                def up(f, parity):
                    b = ffn_block(l, which, "up", f)
                    split_ready(b)
                    column_tile(b, bank[6 + parity][:, 0:SEQ],
                                among=(lambda i: squares(ffn_pe, ffn_act, rnd, 0, i)) if isinstance(f, int) and f == 0 else None).then_inc(w_used, 1)

                def down(f, parity):
                    last = isinstance(f, int) and f == FT - 1
                    b = ffn_block(l, which, "down", f)
                    split_ready(b)
                    if isinstance(f, int) and f == 0:
                        pe.wait_ge(ffn_dve.sem, ffn_dve.at(rnd, "row"))
                        if which == 0:
                            pe.wait_ge(mix_dve.sem, mix_dve.at(l, "prm"))
                        clear(0)
                    pe.wait_ge(hlo_done, (rnd * FT + f) + 1)
                    for t in range(DT):
                        s = slice(P * t, P * (t + 1))
                        ins = three(bank[t // 2][:, SEQ * (t % 2):SEQ * (t % 2 + 1)], whi[:, b.slot, s],
                                    wlo[:, b.slot, s], hhi[:, parity, :], hlo[:, parity, :], False, last,
                                    skip_group_check=True)
                        if last and t in (1, 3, 5):
                            ins.then_inc(ffn_pe.sem, ffn_pe.step(f"sum{t // 2}"))
                    ins.then_inc(w_used, 1)

                ffn_order(pe, gate, up, down)

            def mixing(l):
                def blk(name):
                    b = mix_block(l, name)
                    split_ready(b)
                    return b

                pe.wait_ge(once, ONCE)
                keep_clock(4, 18)
                tiles = RW_TILES + LAT_TILES
                for i, t in enumerate(tiles):
                    b = blk(t)
                    if i >= 4 and i - 4 < len(RW_TILES):
                        pe.wait_ge(mix_dve.sem, mix_dve.at(l, f"pr_{tiles[i - 4]}"))
                    out = bank[i % 4][:, 0:SEQ]
                    for kt in range(DT):
                        if t == "r0" and kt >= 4:
                            squares(mix_pe, mix_act, l, 7, kt - 4)
                        if i == 0 and kt % 2 == 0:
                            pe.wait_ge(mix_dve.sem, mix_dve.at(l, f"lo{kt // 2}"))
                        s = slice(P * kt, P * (kt + 1))
                        ins = three(out, whi[:, b.slot, s], wlo[:, b.slot, s], xhi[:, kt, :], xlo[:, kt, :],
                                    kt == 0, kt == DT - 1)
                    ins.then_inc(w_used, 1)
                    if t == "r1":
                        norm_rows(mix_pe, mix_dve, l, 7)
                    if t == "k3":
                        pe.wait_ge(small_in, l * SMALL_IN + SMALL_IN)
                        pe.wait_ge(mix_act.sem, mix_act.at(l, "tanh_w"))
                        for nm, part, b0 in (("z", LO, 4), ("a", UP, 6)):
                            for j in range(4):
                                ins = mm(bank[b0 + j // 2][:, SEQ * (j % 2):SEQ * (j % 2 + 1)],
                                         w2a2[part, P * j:P * (j + 1)], lora[part, 0, :], start=True, stop=True)
                            ins.then_inc(mix_pe.sem, mix_pe.step(nm))
                    if t == "g1":
                        pe.wait_ge(mix_act.sem, mix_act.at(l, "kksq"))
                        heads = con("onesbd")[:, 0:P:64]
                        for j in range(8):
                            ins = mm(bank[4][:, 2 * j:2 * j + 2], sc[:, P * j:P * (j + 1)], heads, start=True,
                                     stop=True)
                        ins.then_inc(mix_pe.sem, mix_pe.step("kkss"))

                pe.wait_ge(mix_dve.sem, mix_dve.at(l, "kkw"))
                spread_heads(6).then_inc(mix_pe.sem, mix_pe.step("kkb"))
                b = blk("pe")
                pe.wait_ge(mix_dve.sem, mix_dve.at(l, "pr_g1"))
                ins = column_tile(b, bank[2][:, 0:SEQ])
                ins.then_inc(w_used, 1)
                pe.wait_ge(mix_act.sem, mix_act.at(l, "lat_sq"))
                one = con("ones")[:, 0:1]
                for t in range(2):
                    n = slice(P * t, P * (t + 1))
                    mm(bank[3][:, t:t + 1], lat_sq[:, 0, n], one, start=True, stop=False)
                    mm(bank[3][:, t:t + 1], lat_sq[:, 1, n], one, start=False, stop=True)
                    ins = mm(bank[3][:, 2 + t:3 + t], lat_sq[:, 2, n], one, start=True, stop=True)
                ins.then_inc(mix_pe.sem, mix_pe.step("latss"))
                pe.wait_ge(mix_dve.sem, mix_dve.at(l, "gs"))
                for j in range(4):
                    o = bank[4 + j // 2][:, SEQ * (j % 2):SEQ * (j % 2 + 1)]
                    mm(o, g2a[:, P * j:P * (j + 1)], lora[:, 1, :], start=True, stop=False)
                    ins = mm(o, g2b[96:128, P * j:P * (j + 1)], lora[96:128, 2, :], start=False, stop=True)
                ins.then_inc(mix_pe.sem, mix_pe.step("gup"))
                pe.wait_ge(mix_act.sem, mix_act.at(l, "pe_T"))
                keep_clock(2, 2)
                for t in range(2):
                    ins = nc.tensor.transpose(bank[2][:, ROPE * t:ROPE * (t + 1)],
                                              scaled[96:128, 1, P * t:P * (t + 1)], ident[96:128, 96:128])
                ins.then_inc(mix_pe.sem, mix_pe.step("peT"))
                pe.wait_ge(mix_dve.sem, mix_dve.at(l, "lat_y2"))
                for j in range(4):
                    ins = spread_rows(bank[3][:, P * j:P * (j + 1)], j)
                ins.then_inc(mix_pe.sem, mix_pe.step("latb"))
                keep_clock(0, 5)
                b = blk("kvup")
                pe.wait_ge(mix_dve.sem, mix_dve.at(l, "lat_lo"))
                pe.wait_ge(mix_act.sem, mix_act.at(l, "pe"))
                for t in range(2):
                    n = slice(P * t, P * (t + 1))
                    for hf in range(2):
                        o, s = bank[2 * t + hf][:], slice(512 * hf, 512 * (hf + 1))
                        mm(o, xhi[:, 2, n], whi[:, b.slot, s], start=True, stop=False)
                        mm(o, xlo[:, 2, n], whi[:, b.slot, s], start=False, stop=False)
                        ins = mm(o, xhi[:, 2, n], wlo[:, b.slot, s], start=False, stop=True)
                ins.then_inc(w_used, 1)
                pe.wait_ge(mix_act.sem, mix_act.at(l, "gT"))
                pe.wait_ge(mix_pool.sem, mix_pool.at(l, "rk"))
                for j in range(2):
                    ins = mm(bank[5 + 2 * j][:], con("onesbd"), rT[:, 512 * j:512 * (j + 1)], start=True,
                             stop=True)
                ins.then_inc(mix_pe.sem, mix_pe.step("bsum"))
                for hf in range(2):
                    if hf:
                        pe.wait_ge(mix_dve.sem, mix_dve.at(l, "bonus"))
                    b = blk(f"qup{hf}")
                    for t in range(2):
                        o, n = bank[4 + 2 * t + hf][:, 0:384], slice(P * t, P * (t + 1))
                        for kt in range(2):
                            s = slice(384 * kt, 384 * (kt + 1))
                            mm(o, xhi[:, kt, n], whi[:, b.slot, s], start=kt == 0, stop=False)
                            mm(o, xlo[:, kt, n], whi[:, b.slot, s], start=False, stop=False)
                            ins = mm(o, xhi[:, kt, n], wlo[:, b.slot, s], start=False, stop=kt == 1)
                    ins.then_inc(w_used, 1)
                pe.wait_ge(mix_act.sem, mix_act.at(l, "v3"))
                pe.wait_ge(mix_dve.sem, mix_dve.at(l, "qe3"))
                pe.wait_ge(mix_act.sem, mix_act.at(l, "vP"))
                for s, lhs, b0 in (("g1", bP, 0), ("g2", kP, 4)):
                    for c in range(NC):
                        for h in range(HP):
                            g = 4 * c + h
                            ins = mm(bank[b0 + c][:, P * h:P * (h + 1)], lhs[:, g, :],
                                     AR[:, g].rearrange("p s i -> p (s i)"), start=True, stop=True)
                        ins.then_inc(mix_pe.sem, mix_pe.step(f"{s}_{c}"))
                for s, src, b0, wait in (("tb", bP, 0, "g1_"), ("tk", kP, 4, "g2_"), ("tv", vP, 0, "tb")):
                    for c in range(NC):
                        pe.wait_ge(mix_dve.sem, mix_dve.at(l, f"{wait}{c}"))
                        for h in range(HP):
                            ins = turn(bank[b0 + c][:, P * h:P * (h + 1)], src[:, 4 * c + h, :])
                        ins.then_inc(mix_pe.sem, mix_pe.step(f"{s}{c}"))
                pe.wait_ge(mix_act.sem, mix_act.at(l, "tk3"))
                keep_clock(4, 8)
                pe.wait_ge(mix_act.sem, mix_act.at(l, "pP"))
                pe.wait_ge(mix_act.sem, mix_act.at(l, "lP"))
                for b in range(2):
                    for j in range(8):
                        mm(bank[b][:, 64 * j:64 * (j + 1)], pP[:, 8 * b + j, :], con("eyes"), start=j == 0,
                           stop=False, skip_group_check=True)
                    ins = mm(bank[2 + b][:], ident, pC[:, 8 * b:8 * b + 8, :].rearrange("p g i -> p (g i)"),
                             start=True, stop=False, skip_group_check=True)
                    ins.then_inc(mix_pe.sem, mix_pe.step(f"ti{b}"))
                for k in LV:
                    for b in range(2):
                        pe.wait_ge(mix_dve.sem, mix_dve.at(l, f"t0_{b}" if k == 1 else f"tc{k - 1}_{b}"))
                        for j in range(8):
                            g = 8 * b + j
                            ins = mm(bank[4 + b][:, 64 * j:64 * (j + 1)], lP[:, g, :], tC[:, g, :], start=True,
                                     stop=True)
                        ins.then_inc(mix_pe.sem, mix_pe.step(f"u{k}_{b}"))
                    for b in range(2):
                        last = k == LEVELS
                        if not last:
                            pe.wait_ge(mix_dve.sem, mix_dve.at(l, f"um{k}_{b}"))
                            if k > 1:
                                pe.wait_ge(mix_act.sem, mix_act.at(l, f"ps{k - 1}_{b}"))
                            for j in range(8):
                                g = 8 * b + j
                                ins = mm(bank[b][:, 64 * j:64 * (j + 1)], pP[:, g, :], uC[:, g, :], start=False,
                                         stop=k == LEVELS - 1, skip_group_check=True)
                            ins.then_inc(mix_pe.sem, mix_pe.step(f"t{k}_{b}"))
                        pe.wait_ge(mix_act.sem, mix_act.at(l, f"us{k}_{b}"))
                        if k > 1:
                            pe.wait_ge(mix_dve.sem, mix_dve.at(l, f"pc{k - 1}_{b}"))
                        for j in range(8):
                            g = 8 * b + j
                            ins = mm(bank[2 + b][:, 64 * j:64 * (j + 1)], uP[:, g, :], pC[:, g, :], start=False,
                                     stop=last, skip_group_check=True)
                        ins.then_inc(mix_pe.sem, mix_pe.step(f"p{k}_{b}"))
                pe.wait_ge(mix_dve.sem, mix_dve.at(l, "rope1"))
                pe.wait_ge(mix_act.sem, mix_act.at(l, "ps5_1"))
                for i in range(8):
                    s, t, hq = i // 4, (i // 2) % 2, i % 2
                    for j in range(4):
                        ins = turn(bank[i][0:QK, P * j:P * (j + 1)], qk[:, t, s, 4 * hq + j, :])
                    ins.then_inc(mix_pe.sem, mix_pe.step(f"qkT{i}"))
                pe.wait_ge(mix_dve.sem, mix_dve.at(l, "qkT0"))
                keep_clock(0, 8)
                pe.wait_ge(mix_dve.sem, mix_dve.at(l, "qkT7"))
                for b in range(2):
                    for j in range(4):
                        h = 4 * b + j
                        mm(bank[3 * b][:, P * j:P * (j + 1)], qkT[0][0:QK, h, 0:P], qkT[1][0:QK, h, 0:P],
                           start=True, stop=True)
                        ins = mm(bank[3 * b + 1 + j // 2][:, 256 * (j % 2):256 * (j % 2) + 256],
                                 qkT[0][0:QK, h, P:SEQ], qkT[1][0:QK, h, :], start=True, stop=True)
                    ins.then_inc(mix_pe.sem, mix_pe.step(f"sc{b}"))
                for b in range(2):
                    keep_clock(6, (14, 0)[b])
                    pe.wait_ge(mix_act.sem, mix_act.at(l, f"ex{b}"))
                    if b:
                        pe.wait_ge(mix_dve.sem, mix_dve.at(l, "pt0"))
                    for m, bk in enumerate(((6, 7, 0), (3, 4, 5))[b]):
                        for j in range(4):
                            ins = turn(bank[bk][:, P * j:P * (j + 1)], prob[:, j, P * m:P * (m + 1)])
                    ins.then_inc(mix_pe.sem, mix_pe.step(f"pt{b}"))
                    if b == 0:
                        keep_clock(1, 8)
                    pe.wait_ge(mix_dve.sem, mix_dve.at(l, f"pt{b}"))
                    for j in range(4):
                        h = 4 * b + j
                        s = slice(DV * h, DV * (h + 1))
                        mm(bank[1][:, s], probT[:, 0, P * j:P * (j + 1)], V[:, 0, h, :], start=True, stop=True)
                        mm(bank[2][:, s], probT[:, 1, P * j:P * (j + 1)], V[:, 0, h, :], start=True, stop=False)
                        ins = mm(bank[2][:, s], probT[:, 2, P * j:P * (j + 1)], V[:, 1, h, :], start=False,
                                 stop=True)
                    ins.then_inc(mix_pe.sem, mix_pe.step(f"pv{b}"))
                pe.wait_ge(mix_act.sem, mix_act.at(l, "ak"))
                pe.wait_ge(mix_pool.sem, mix_pool.at(l, "vC"))
                for c in range(NC):
                    x_b, u_b, s_b, y_b = bank[4 + c % 2], bank[6 + c % 2], bank[2 + c % 2], bank[c // 2]
                    for h in range(HP):
                        s = slice(64 * h, 64 * (h + 1))
                        ins = mm(x_b[:, s], lP[:, 4 * c + h, :], vC[:, 4 * c + h, :], start=h == 0, stop=c == 0,
                                 skip_group_check=True)
                    if c:
                        pe.wait_ge(mix_dve.sem, mix_dve.at(l, f"s{c - 1}"))
                        for h in range(HP):
                            ins = mm(x_b[:, 64 * h:64 * (h + 1)], aP[:, 4 * c + h, :], rec[:, 2 + c % 2, h, :],
                                     start=False, stop=True, skip_group_check=True)
                    ins.then_inc(mix_pe.sem, mix_pe.step(f"x{c}"))
                    keep_clock(4 + (c + 1) % 2, 3)
                    pe.wait_ge(mix_dve.sem, mix_dve.at(l, f"x{c}"))
                    for h in range(HP):
                        ins = mm(u_b[:, 64 * h:64 * (h + 1)], pP[:, 4 * c + h, :], rec[:, 0, h, :], start=True,
                                 stop=True)
                    ins.then_inc(mix_pe.sem, mix_pe.step(f"u{c}"))
                    keep_clock(4 + (c + 1) % 2, 3)
                    pe.wait_ge(mix_dve.sem, mix_dve.at(l, f"u{c}"))
                    if c < NC - 1:
                        if c == 0:
                            pe.wait_ge(mix_dve.sem, mix_dve.at(l, "o"))
                        for h in range(HP):
                            g, o = 4 * c + h, s_b[:, 64 * h:64 * (h + 1)]
                            mm(o, kP[:, g, :], vC[:, g, :], start=True, stop=False)
                            ins = mm(o, bP[:, g, :], rec[:, 1, h, :], start=False, stop=True)
                        ins.then_inc(mix_pe.sem, mix_pe.step(f"s{c}"))
                    pe.wait_ge(mix_act.sem, mix_act.at(l, f"ub{c}"))
                    if c:
                        pe.wait_ge(mix_act.sem, mix_act.at(l, f"sb{c - 1}"))
                    if c == 2:
                        pe.wait_ge(mix_dve.sem, mix_dve.at(l, "yg0"))
                    for h in range(HP):
                        g, o = 4 * c + h, y_b[:, 256 * (c % 2) + 64 * h:256 * (c % 2) + 64 * (h + 1)]
                        mm(o, vP[:, g, :], M2[:, g, 1, :], start=True, stop=False)
                        ins = mm(o, uP[:, 4 * (c % 2) + h, :], M1[:, g, 1, :], start=False, stop=c == 0)
                        if c:
                            ins = mm(o, uP[:, 8 + 4 * (c % 2) + h, :], AR[:, g, 1, :], start=False, stop=True)
                    ins.then_inc(mix_pe.sem, mix_pe.step(f"y{c}"))
                    if c in (1, 2):
                        pe.wait_ge(mix_dve.sem, mix_dve.at(l, "yn" if c == 1 else "ye0"))
                        for f in (2 * c - 2, 2 * c - 1):
                            for t in range(2):
                                ins = turn(bank[2 - c][:, 256 * (f % 2) + P * t:256 * (f % 2) + P * (t + 1)],
                                           ymla[:, t, P * f:P * (f + 1)])
                        ins.then_inc(mix_pe.sem, mix_pe.step(f"yT{c - 1}"))
                pe.wait_ge(mix_dve.sem, mix_dve.at(l, "ye1"))
                for b in range(2):
                    ins = mm(bank[4 + b][:], con("meanbd"), yT[:, 512 * b:512 * (b + 1)], start=True, stop=True)
                ins.then_inc(mix_pe.sem, mix_pe.step("mean"))

                def output(k):
                    b = blk(f"out{k}")
                    pe.wait_ge(mix_dve.sem, mix_dve.at(l, "ylo0" if k < 4 else f"ylo{k}"))
                    for t in range(DT):
                        s = slice(P * t, P * (t + 1))
                        ins = three(bank[4 * (k // 4) + t // 2][:, SEQ * (t % 2):SEQ * (t % 2 + 1)],
                                    whi[:, b.slot, s], wlo[:, b.slot, s], xhi[:, k, :], xlo[:, k, :], False,
                                    k % 4 == 3, skip_group_check=True)
                        if k == 7 and t in (1, 3, 5):
                            ins.then_inc(mix_pe.sem, mix_pe.step(f"sum{t // 2}"))
                    ins.then_inc(w_used, 1)

                pe.wait_ge(mix_dve.sem, mix_dve.at(l, "s2"))
                clear(0)
                output(0)
                pe.wait_ge(mix_act.sem, mix_act.at(l, "gsq"))
                for j in range(8):
                    ins = mm(bank[6][:, 2 * j:2 * j + 2], ysc[:, P * j:P * (j + 1)], con("meanbd")[:, 0:P:64],
                             start=True, stop=True)
                ins.then_inc(mix_pe.sem, mix_pe.step("var"))
                output(1)
                pe.wait_ge(mix_dve.sem, mix_dve.at(l, "gvw"))
                spread_heads(4).then_inc(mix_pe.sem, mix_pe.step("gvb"))
                output(2)
                output(3)
                pe.wait_ge(mix_dve.sem, mix_dve.at(l, "gy"))
                clear(4)
                output(4)
                pe.wait_ge(mix_act.sem, mix_act.at(l, "rsq"))
                pe.wait_ge(mix_dve.sem, mix_dve.at(l, "resm0"))
                for t in range(2):
                    for j in range(4):
                        ins = mm(bank[0][:, t:t + 1], ysc[:, SEQ * j + P * t:SEQ * j + P * (t + 1)], one,
                                 start=j == 0, stop=j == 3)
                ins.then_inc(mix_pe.sem, mix_pe.step("rms"))
                output(5)
                pe.wait_ge(mix_dve.sem, mix_dve.at(l, "rms_y2"))
                pe.wait_ge(mix_dve.sem, mix_dve.at(l, "resm1"))
                for t in range(2):
                    ins = spread_rows(bank[1][:, P * t:P * (t + 1)], t)
                ins.then_inc(mix_pe.sem, mix_pe.step("rmsb"))
                output(6)
                output(7)

            pe.sem_inc(w_used, RING)
            pe.wait_ge(once, 1)
            keep_clock(7, 12)
            pe.wait_ge(const_in, 16)
            pe.wait_ge(x_in, 16)
            for i in range(4):
                for d in range(2):
                    for t in range(2):
                        ins = turn(bank[i][:, SEQ * d + P * t:SEQ * d + P * (t + 1)],
                                   xtok[:, t, P * (2 * i + d):P * (2 * i + d + 1)])
                ins.then_inc(x_turned, 1)

            with pe.Fori(0, DEPTH) as l:
                pe.wait_ge(rows1_in, l * 16 + 16)
                pe.wait_ge(h_steps, l * (2 * FT * 4) + 8)
                keep_clock(5, 4)
                turn(bank[5][:, 0:8], rows1[:]).then_inc(mix_pe.sem, mix_pe.step("prm1"))
                ffn(l, 0)
                mixing(l)
                ffn(l, 1)
            pe.wait_ge(x_ready, quarter(DEPTH * 3, 3))
            for t in range(2):
                for q in range(2):
                    for d in range(4):
                        ins = turn(bank[2 * t + q][:, P * d:P * (d + 1)], xT[:, 4 * q + d, P * t:P * (t + 1)])
                    ins.then_inc(out_turned, 1)


_VECTORS = ['ffn1_norm', 'mix_norm', 'q_lat_norm', 'kv_lat_norm', 'q_norm', 'k_norm', 'shift_mu', 'w0', 'a0',
            'k_k', 'k_a', 'r_k', 'gn_gain', 'gn_bias', 'out_norm_mla', 'out_norm_rwkv', 'ffn2_norm']
_WEIGHTS = ['ffn1_w_gate', 'ffn1_w_up', 'ffn1_w_down', 'w_in', 'w_q_up', 'w_kv_up', 'w2', 'a2', 'g2', 'w_out',
            'ffn2_w_gate', 'ffn2_w_up', 'ffn2_w_down']


def kernel(**inputs):
    import concourse.bacc as _bacc
    from concourse.bass_utils import run_bass_kernel_spmd as _run

    nc = _bacc.Bacc("TRN2", target_bir_lowering=False, num_devices=1)
    arrays, aps = {}, {}
    for name in ['x'] + _VECTORS + _WEIGHTS:
        a = np.ascontiguousarray(inputs[name])
        arrays[f"in_{name}_dram"] = a
        aps[name] = nc.dram_tensor(f"in_{name}_dram", a.shape, mybir.dt.from_np(a.dtype),
                                   kind="ExternalInput").ap()
    arrays["in_consts_dram"] = shape_constants()
    consts = nc.dram_tensor("in_consts_dram", (P, NCONST), F32, kind="ExternalInput").ap()
    out = nc.dram_tensor("out_0_dram", (1, SEQ, D), F32, kind="ExternalOutput").ap()
    build(nc, aps['x'], {k: aps[k] for k in _VECTORS}, {k: aps[k] for k in _WEIGHTS}, consts, out)
    r = _run(nc, [arrays], core_ids=[0])
    return r.results[0]["out_0_dram"]
```
